# Optimizing a Trainium2 kernel written in Bass

```python
import math
import jax, jax.numpy as jnp
from jax import lax
import numpy as np

D_MODEL = 1024
BATCH = 1
SEQ = 512
DEPTH = 1

CHUNK = 64
N_META = 16
DN_HEADS = 8
DN_DK = 128
DN_DV = 256
DN_CONV = 4
DN_QK = DN_HEADS * DN_DK
DN_V = DN_HEADS * DN_DV
SB_HEADS = 8
SB_DH = 128
SB_W = SB_HEADS * SB_DH
SB_BLOCK = 128
D_FF = -(-8 * D_MODEL // (3 * 256)) * 256
PROJ_WIDTH = 2 * DN_QK + 2 * DN_V + 2 * DN_HEADS + 3 * SB_W + 2 * D_MODEL
RMS_EPS = 1e-6
L2_EPS = 1e-6


def _split_points():
    widths = (DN_QK, DN_QK, DN_V, DN_V, DN_HEADS, DN_HEADS, SB_W, SB_W, SB_W, D_MODEL, D_MODEL)
    return [int(s) for s in np.cumsum(widths)[:-1]]

def rmsnorm(x, gain):
    xf = x.astype(jnp.float32)
    y = xf * lax.rsqrt(jnp.mean(xf * xf, axis=-1, keepdims=True) + RMS_EPS)
    return (y * gain.astype(jnp.float32)).astype(x.dtype)

def l2norm(x):
    xf = x.astype(jnp.float32)
    return xf * lax.rsqrt(jnp.sum(xf * xf, axis=-1, keepdims=True) + L2_EPS)

def causal_depthwise_conv(x, w):
    K, C = w.shape
    return lax.conv_general_dilated(
        x, w[:, None, :].astype(x.dtype), window_strides=(1,), padding=[(K - 1, 0)],
        dimension_numbers=('NWC', 'WIO', 'NWC'), feature_group_count=C)

def gated_delta_rule(q, k, v, g, beta):
    B, T, H, DK = q.shape
    DV = v.shape[-1]
    N = T // CHUNK
    f32 = jnp.float32

    def to_chunks(a):
        a = a.astype(f32).reshape((B, N, CHUNK, H) + a.shape[3:])
        return jnp.moveaxis(a, (1, 3), (0, 2))

    q = to_chunks(q) * (DK ** -0.5)
    k = to_chunks(k)
    v = to_chunks(v)
    beta = to_chunks(beta)
    g = jnp.cumsum(to_chunks(g), axis=-1)
    idx = jnp.arange(CHUNK)
    incl = idx[:, None] >= idx[None, :]
    strict = idx[:, None] > idx[None, :]
    decay = jnp.exp(jnp.where(incl, g[..., :, None] - g[..., None, :], -jnp.inf))
    kb = k * beta[..., None]
    lower = jnp.where(strict, jnp.einsum('nbhid,nbhjd->nbhij', kb, k) * decay, 0.0)
    eye = jnp.eye(CHUNK, dtype=f32)
    rhs = jnp.concatenate([v * beta[..., None], kb * jnp.exp(g)[..., None]], axis=-1)
    sol = lax.linalg.triangular_solve(eye + lower, rhs, left_side=True, lower=True)
    u, w = sol[..., :DV], sol[..., DV:]
    attn = jnp.einsum('nbhid,nbhjd->nbhij', q, k) * decay
    q_dec = q * jnp.exp(g)[..., None]
    k_dec = k * jnp.exp(g[..., -1:] - g)[..., None]
    g_last = jnp.exp(g[..., -1])

    def step(S, xs):
        u_c, w_c, attn_c, qd_c, kd_c, gl_c = xs
        v_new = u_c - jnp.einsum('bhcd,bhde->bhce', w_c, S)
        o = jnp.einsum('bhcd,bhde->bhce', qd_c, S) + jnp.einsum('bhij,bhje->bhie', attn_c, v_new)
        S = S * gl_c[..., None, None] + jnp.einsum('bhcd,bhce->bhde', kd_c, v_new)
        return S, o

    S0 = jnp.zeros((B, H, DK, DV), f32)
    _, o = lax.scan(step, S0, (u, w, attn, q_dec, k_dec, g_last))
    return jnp.moveaxis(o, (0, 2), (1, 3)).reshape(B, T, H, DV)

def stick_breaking_attention(q, k, v):
    B, T, H, D = q.shape
    nq = -(-T // SB_BLOCK)
    Tp = nq * SB_BLOCK
    pad = ((0, 0), (0, Tp - T), (0, 0), (0, 0))
    f32 = jnp.float32
    qh = jnp.pad(q.astype(f32), pad).reshape(B, nq, SB_BLOCK, H, D).transpose(1, 0, 3, 2, 4)
    kh = jnp.pad(k.astype(f32), pad).transpose(0, 2, 1, 3)
    vh = jnp.pad(v.astype(f32), pad).transpose(0, 2, 1, 3)
    key_pos = jnp.arange(Tp)
    scale = D ** -0.5

    def block(args):
        q_blk, start = args
        z = jnp.einsum('bhqd,bhkd->bhqk', q_blk, kh) * scale
        q_pos = start + jnp.arange(SB_BLOCK)
        visible = key_pos[None, :] < q_pos[:, None]
        log_keep = jnp.where(visible, jax.nn.log_sigmoid(-z), 0.0)
        log_w = jax.nn.log_sigmoid(z) + lax.cumsum(log_keep, axis=3, reverse=True) - log_keep
        w = jnp.where(visible, jnp.exp(log_w), 0.0)
        return jnp.einsum('bhqk,bhkd->bhqd', w, vh)

    o = lax.map(block, (qh, jnp.arange(nq) * SB_BLOCK))
    return o.transpose(1, 0, 3, 2, 4).reshape(B, Tp, H, D)[:, :T]

def hybrid_mixer(hn, w_in, conv_q, conv_k, conv_v, a_log, dt_bias, dn_gain, sbq_gain, sbk_gain,
                 w_branch_dn, w_branch_sb, w_out):
    B, T, _ = hn.shape
    proj = hn @ w_in
    (dq, dk, dv, dz, da, db, sq, sk, sv, gate_dn, gate_sb) = jnp.split(proj, _split_points(), axis=-1)

    def heads(a, d):
        return a.reshape(B, T, -1, d)

    q = l2norm(heads(jax.nn.silu(causal_depthwise_conv(dq, conv_q)), DN_DK))
    k = l2norm(heads(jax.nn.silu(causal_depthwise_conv(dk, conv_k)), DN_DK))
    v = heads(jax.nn.silu(causal_depthwise_conv(dv, conv_v)), DN_DV)
    g = -jnp.exp(a_log.astype(jnp.float32)) * jax.nn.softplus(da.astype(jnp.float32) + dt_bias.astype(jnp.float32))
    beta = jax.nn.sigmoid(db.astype(jnp.float32))
    pad_l = (-N_META) % CHUNK
    pad_r = (-(T + pad_l)) % CHUNK

    def chunk_pad(a):
        return jnp.pad(a, ((0, 0), (pad_l, pad_r)) + ((0, 0),) * (a.ndim - 2))

    o_dn = gated_delta_rule(chunk_pad(q), chunk_pad(k), chunk_pad(v), chunk_pad(g), chunk_pad(beta))
    o_dn = o_dn[:, pad_l:pad_l + T]
    o_dn = rmsnorm(o_dn, dn_gain) * jax.nn.silu(heads(dz, DN_DV).astype(jnp.float32))
    o_dn = o_dn.astype(hn.dtype).reshape(B, T, DN_V)

    qs = rmsnorm(heads(sq, SB_DH), sbq_gain)
    ks = rmsnorm(heads(sk, SB_DH), sbk_gain)
    o_sb = stick_breaking_attention(qs, ks, heads(sv, SB_DH)).astype(hn.dtype).reshape(B, T, SB_W)

    merged = jax.nn.sigmoid(gate_dn) * (o_dn @ w_branch_dn) + jax.nn.sigmoid(gate_sb) * (o_sb @ w_branch_sb)
    return merged @ w_out

def swiglu(hn, w_ffn_in, w_ffn_out):
    gate, up = jnp.split(hn @ w_ffn_in, 2, axis=-1)
    return (jax.nn.silu(gate) * up) @ w_ffn_out

def first_inputs(seed: int = 0) -> dict:
    key = jax.random.key(seed)
    ks = jax.random.split(key, 20)
    f32 = jnp.float32

    def nrm(k, shape, fan_in):
        return jax.random.normal(k, shape, f32) * (fan_in ** -0.5)

    def gain(k, n):
        return 1.0 + 0.02 * jax.random.normal(k, (DEPTH, n), f32)

    dt = jnp.exp(jax.random.uniform(ks[7], (DEPTH, DN_HEADS), f32) * (math.log(0.1) - math.log(1e-3)) + math.log(1e-3))
    return {
        'x': jax.random.normal(ks[0], (BATCH, SEQ, D_MODEL), f32),
        'meta_tokens': jax.random.normal(ks[1], (N_META, D_MODEL), f32),
        'norm_mix_gain': gain(ks[2], D_MODEL),
        'w_in': nrm(ks[3], (DEPTH, D_MODEL, PROJ_WIDTH), D_MODEL),
        'conv_q': nrm(ks[4], (DEPTH, DN_CONV, DN_QK), DN_CONV),
        'conv_k': nrm(ks[5], (DEPTH, DN_CONV, DN_QK), DN_CONV),
        'conv_v': nrm(ks[6], (DEPTH, DN_CONV, DN_V), DN_CONV),
        'dn_a_log': jnp.log(jax.random.uniform(ks[8], (DEPTH, DN_HEADS), f32, 1.0, 16.0)),
        'dn_dt_bias': dt + jnp.log(-jnp.expm1(-dt)),
        'dn_out_norm_gain': gain(ks[9], DN_DV),
        'sb_q_norm_gain': gain(ks[10], SB_DH),
        'sb_k_norm_gain': gain(ks[11], SB_DH),
        'w_branch_dn': nrm(ks[12], (DEPTH, DN_V, D_MODEL), DN_V),
        'w_branch_sb': nrm(ks[13], (DEPTH, SB_W, D_MODEL), SB_W),
        'w_out': nrm(ks[14], (DEPTH, D_MODEL, D_MODEL), D_MODEL),
        'norm_ffn_gain': gain(ks[15], D_MODEL),
        'w_ffn_in': nrm(ks[16], (DEPTH, D_MODEL, 2 * D_FF), D_MODEL),
        'w_ffn_out': nrm(ks[17], (DEPTH, D_FF, D_MODEL), D_FF),
    }

def first_block(x, meta_tokens, norm_mix_gain, w_in, conv_q, conv_k, conv_v, dn_a_log, dn_dt_bias,
              dn_out_norm_gain, sb_q_norm_gain, sb_k_norm_gain, w_branch_dn, w_branch_sb, w_out,
              norm_ffn_gain, w_ffn_in, w_ffn_out):
    B = x.shape[0]
    meta = jnp.broadcast_to(meta_tokens[None].astype(x.dtype), (B, N_META, D_MODEL))
    h = jnp.concatenate([meta, x], axis=1)
    for l in range(DEPTH):
        h = h + hybrid_mixer(rmsnorm(h, norm_mix_gain[l]), w_in[l], conv_q[l], conv_k[l], conv_v[l],
                             dn_a_log[l], dn_dt_bias[l], dn_out_norm_gain[l], sb_q_norm_gain[l],
                             sb_k_norm_gain[l], w_branch_dn[l], w_branch_sb[l], w_out[l])
        h = h + swiglu(rmsnorm(h, norm_ffn_gain[l]), w_ffn_in[l], w_ffn_out[l])
    return h[:, N_META:]


DEPTH_2 = 2

N_MIXERS = 3
GRID_W = 64
EPS = 1e-6
N_HEADS = 16
HEAD_DIM = D_MODEL // N_HEADS
N_KV_HEADS = 4
Q_BLOCK = 128
ROPE_THETA = 10000.0
HY_ORDER = 2
HY_EMB_DIM = 33
HY_FILTER_WIDTH = 64
HY_FAST_DECAY = 0.3
HY_SLOW_DECAY = 1.5
HY_TARGET = 1e-2
S5_GROUP = 16
S5_GROUPS = D_MODEL // S5_GROUP
S5_STATE = 64
S5_DT_MIN = 1e-3
S5_DT_MAX = 1e-1
D_FF_2 = 2816


def rmsnorm_2(x, g):
    xf = x.astype(jnp.float32)
    y = xf * lax.rsqrt(jnp.mean(xf * xf, axis=-1, keepdims=True) + EPS)
    return (y * g.astype(jnp.float32)).astype(x.dtype)

def dwconv3(x, w, b):
    L = x.shape[1]
    xp = jnp.pad(x, ((0, 0), (1, 1), (0, 0)))
    return xp[:, :L] * w[0] + xp[:, 1:L + 1] * w[1] + xp[:, 2:] * w[2] + b

def axial_rope_tables(L):
    rows = L // GRID_W
    n_freq = HEAD_DIM // 4
    inv = 1.0 / (ROPE_THETA ** (jnp.arange(n_freq, dtype=jnp.float32) / n_freq))
    r = jnp.arange(rows, dtype=jnp.float32)
    col = jnp.arange(GRID_W, dtype=jnp.float32)
    ang_r = jnp.broadcast_to(r[:, None, None] * inv, (rows, GRID_W, n_freq))
    ang_c = jnp.broadcast_to(col[None, :, None] * inv, (rows, GRID_W, n_freq))
    ang = jnp.concatenate([ang_r, ang_c], axis=-1).reshape(L, 2 * n_freq)
    return jnp.cos(ang), jnp.sin(ang)

def apply_rope(x, cos, sin):
    xf = x.astype(jnp.float32).reshape(x.shape[:-1] + (HEAD_DIM // 2, 2))
    x0, x1 = xf[..., 0], xf[..., 1]
    c = cos[None, :, None, :]
    s = sin[None, :, None, :]
    out = jnp.stack([x0 * c - x1 * s, x0 * s + x1 * c], axis=-1).reshape(x.shape)
    return out.astype(x.dtype)

def attention_mixer(h, w_qkv, w_o, q_gain, k_gain, cos, sin):
    Bsz, L, _ = h.shape
    G = N_HEADS // N_KV_HEADS
    qkv = h @ w_qkv
    q, k, v = jnp.split(qkv, [N_HEADS * HEAD_DIM, (N_HEADS + N_KV_HEADS) * HEAD_DIM], axis=-1)
    q = q.reshape(Bsz, L, N_HEADS, HEAD_DIM)
    k = k.reshape(Bsz, L, N_KV_HEADS, HEAD_DIM)
    v = v.reshape(Bsz, L, N_KV_HEADS, HEAD_DIM)
    q = apply_rope(rmsnorm_2(q, q_gain), cos, sin)
    k = apply_rope(rmsnorm_2(k, k_gain), cos, sin)
    nb = L // Q_BLOCK
    qb = q.reshape(Bsz, nb, Q_BLOCK, N_KV_HEADS, G, HEAD_DIM).transpose(1, 0, 2, 3, 4, 5)
    scale = HEAD_DIM ** -0.5

    def block(q_blk):
        s = jnp.einsum('bqkgd,bskd->bkgqs', q_blk, k, preferred_element_type=jnp.float32) * scale
        p = jax.nn.softmax(s, axis=-1).astype(v.dtype)
        return jnp.einsum('bkgqs,bskd->bqkgd', p, v)

    o = lax.map(block, qb)
    o = o.transpose(1, 0, 2, 3, 4, 5).reshape(Bsz, L, N_HEADS * HEAD_DIM)
    return o @ w_o

def hyena_pos_features(L):
    t = jnp.linspace(0.0, 1.0, L, dtype=jnp.float32)[:, None]
    bands = (HY_EMB_DIM - 1) // 2
    w = 2.0 * math.pi * jnp.arange(L, dtype=jnp.float32) / L
    f = jnp.linspace(1e-4, bands - 1, bands, dtype=jnp.float32)
    ang = w[:, None] * f[None, :]
    z = jnp.concatenate([t, jnp.cos(ang), -jnp.sin(ang)], axis=-1)
    deltas = jnp.abs(jnp.linspace(math.log(HY_TARGET) / HY_SLOW_DECAY,
                                  math.log(HY_TARGET) / HY_FAST_DECAY, D_MODEL, dtype=jnp.float32))
    decay = jnp.exp(-t * deltas[None, :])
    return z, decay

def hyena_mixer(h, w_in, conv_w, conv_b, f_w1, f_b1, f_w2, f_b2, f_w3, f_freq, skip, w_out, z, decay):
    Bsz, L, D = h.shape
    u = dwconv3(h @ w_in, conv_w, conv_b)
    v, x1, x2 = jnp.split(u, 3, axis=-1)
    a = jnp.sin(f_freq * (z @ f_w1 + f_b1))
    a = jnp.sin(f_freq * (a @ f_w2 + f_b2))
    filt = (a @ f_w3).astype(jnp.float32).reshape(L, HY_ORDER, 2, D) * decay[:, None, None, :]
    fwd = filt[:, :, 0]
    bwd = filt[:, :, 1]
    k2 = jnp.concatenate([fwd, jnp.zeros_like(fwd[:1]), bwd[1:][::-1]], axis=0)
    k2 = k2 / jnp.sum(jnp.abs(k2), axis=0, keepdims=True)
    kf = jnp.fft.rfft(k2, axis=0)
    gates = (x1, x2)
    zc = v
    for o in range(HY_ORDER):
        zf = jnp.fft.rfft(zc.astype(jnp.float32), n=2 * L, axis=1)
        y = jnp.fft.irfft(zf * kf[None, :, o], n=2 * L, axis=1)[:, :L]
        zc = gates[o] * (y.astype(h.dtype) + skip[o] * zc)
    return zc @ w_out

def s5_direction(u, A_re, A_im, log_dt, B_re, B_im, C_re, C_im, reverse):
    L = u.shape[1]
    lam = lax.complex(jnp.minimum(A_re.astype(jnp.float32), -1e-4), A_im.astype(jnp.float32))
    dt = jnp.exp(log_dt.astype(jnp.float32))[:, None]
    lam_bar = jnp.exp(lam * dt)
    b_c = lax.complex(B_re.astype(jnp.float32), B_im.astype(jnp.float32))
    b_bar = ((lam_bar - 1.0) / lam)[..., None] * b_c
    bu = jnp.einsum('blgh,gph->blgp', u.astype(jnp.complex64), b_bar)
    a = jnp.broadcast_to(lam_bar[None, None], (1, L) + lam_bar.shape)

    def combine(e1, e2):
        a1, b1 = e1
        a2, b2 = e2
        return a2 * a1, a2 * b1 + b2

    _, xs = lax.associative_scan(combine, (a, bu), axis=1, reverse=reverse)
    c_c = lax.complex(C_re.astype(jnp.float32), C_im.astype(jnp.float32))
    return jnp.einsum('blgp,ghp->blgh', xs, c_c).real

def s5_mixer(h, A_re, A_im, log_dt, B_re, B_im, C_re, C_im, d_skip, w_glu):
    Bsz, L, D = h.shape
    hf = h.astype(jnp.float32)
    u = hf.reshape(Bsz, L, S5_GROUPS, S5_GROUP)
    y_f = s5_direction(u, A_re[0], A_im[0], log_dt[0], B_re[0], B_im[0], C_re[0], C_im[0], False)
    y_b = s5_direction(u, A_re[1], A_im[1], log_dt[1], B_re[1], B_im[1], C_re[1], C_im[1], True)
    y = (y_f + y_b).reshape(Bsz, L, D) + d_skip.astype(jnp.float32) * hf
    y = jax.nn.gelu(y.astype(h.dtype))
    g_a, g_b = jnp.split(y @ w_glu, 2, axis=-1)
    return g_a * jax.nn.sigmoid(g_b)

def conv_ffn(h, w_up, conv_w, conv_b, w_down):
    gate, val = jnp.split(h @ w_up, 2, axis=-1)
    gate = dwconv3(gate, conv_w, conv_b)
    return (jax.nn.silu(gate) * val) @ w_down

def second_inputs(seed: int = 0) -> dict:
    key = jax.random.key(seed)
    ks = iter(jax.random.split(key, 48))
    f32 = jnp.float32

    def nrm(shape, scale):
        return jax.random.normal(next(ks), shape, f32) * scale

    n_attn = len(range(0, DEPTH_2, N_MIXERS))
    n_hy = len(range(1, DEPTH_2, N_MIXERS))
    n_s5 = len(range(2, DEPTH_2, N_MIXERS))
    D = D_MODEL
    G, P, Hg = S5_GROUPS, S5_STATE, S5_GROUP
    qkv_w = (N_HEADS + 2 * N_KV_HEADS) * HEAD_DIM
    return {
        'x': nrm((BATCH, SEQ, D), 1.0),
        'c': nrm((BATCH, D), 1.0),
        'ada_w': nrm((DEPTH_2, D, 6 * D), 0.5 * D ** -0.5),
        'ada_b': nrm((DEPTH_2, 6 * D), 0.02),
        'norm1_g': 1.0 + nrm((DEPTH_2, D), 0.02),
        'norm2_g': 1.0 + nrm((DEPTH_2, D), 0.02),
        'final_g': 1.0 + nrm((D,), 0.02),
        'attn_w_qkv': nrm((n_attn, D, qkv_w), D ** -0.5),
        'attn_w_o': nrm((n_attn, N_HEADS * HEAD_DIM, D), D ** -0.5),
        'attn_q_gain': 1.0 + nrm((n_attn, HEAD_DIM), 0.02),
        'attn_k_gain': 1.0 + nrm((n_attn, HEAD_DIM), 0.02),
        'hy_w_in': nrm((n_hy, D, 3 * D), D ** -0.5),
        'hy_conv_w': nrm((n_hy, 3, 3 * D), 3 ** -0.5),
        'hy_conv_b': nrm((n_hy, 3 * D), 0.02),
        'hy_f_w1': nrm((n_hy, HY_EMB_DIM, HY_FILTER_WIDTH), HY_EMB_DIM ** -0.5),
        'hy_f_b1': nrm((n_hy, HY_FILTER_WIDTH), 0.1),
        'hy_f_w2': nrm((n_hy, HY_FILTER_WIDTH, HY_FILTER_WIDTH), HY_FILTER_WIDTH ** -0.5),
        'hy_f_b2': nrm((n_hy, HY_FILTER_WIDTH), 0.1),
        'hy_f_w3': nrm((n_hy, HY_FILTER_WIDTH, HY_ORDER * 2 * D), HY_FILTER_WIDTH ** -0.5),
        'hy_f_freq': 1.0 + nrm((n_hy, HY_FILTER_WIDTH), 0.02),
        'hy_skip': nrm((n_hy, HY_ORDER, D), 1.0),
        'hy_w_out': nrm((n_hy, D, D), D ** -0.5),
        's5_A_re': -0.5 + nrm((n_s5, 2, G, P), 0.01),
        's5_A_im': math.pi * jnp.arange(P, dtype=f32) + nrm((n_s5, 2, G, P), 0.01),
        's5_log_dt': jax.random.uniform(next(ks), (n_s5, 2, G), f32, math.log(S5_DT_MIN), math.log(S5_DT_MAX)),
        's5_B_re': nrm((n_s5, 2, G, P, Hg), (2 * Hg) ** -0.5),
        's5_B_im': nrm((n_s5, 2, G, P, Hg), (2 * Hg) ** -0.5),
        's5_C_re': nrm((n_s5, 2, G, Hg, P), (2 * P) ** -0.5),
        's5_C_im': nrm((n_s5, 2, G, Hg, P), (2 * P) ** -0.5),
        's5_D': nrm((n_s5, D), 1.0),
        's5_w_glu': nrm((n_s5, D, 2 * D), D ** -0.5),
        'ffn_w_up': nrm((DEPTH_2, D, 2 * D_FF_2), D ** -0.5),
        'ffn_conv_w': nrm((DEPTH_2, 3, D_FF_2), 3 ** -0.5),
        'ffn_conv_b': nrm((DEPTH_2, D_FF_2), 0.02),
        'ffn_w_down': nrm((DEPTH_2, D_FF_2, D), D_FF_2 ** -0.5),
    }

def second_block(x, c, ada_w, ada_b, norm1_g, norm2_g, final_g,
              attn_w_qkv, attn_w_o, attn_q_gain, attn_k_gain,
              hy_w_in, hy_conv_w, hy_conv_b, hy_f_w1, hy_f_b1, hy_f_w2, hy_f_b2, hy_f_w3, hy_f_freq,
              hy_skip, hy_w_out,
              s5_A_re, s5_A_im, s5_log_dt, s5_B_re, s5_B_im, s5_C_re, s5_C_im, s5_D, s5_w_glu,
              ffn_w_up, ffn_conv_w, ffn_conv_b, ffn_w_down):
    L = x.shape[1]
    cos, sin = axial_rope_tables(L)
    z, decay = hyena_pos_features(L)
    c_act = jax.nn.silu(c)
    for i in range(DEPTH_2):
        m, j = i % N_MIXERS, i // N_MIXERS
        mod = (c_act @ ada_w[i] + ada_b[i])[:, None, :]
        sh1, sc1, g1, sh2, sc2, g2 = jnp.split(mod, 6, axis=-1)
        h = rmsnorm_2(x, norm1_g[i]) * (1.0 + sc1) + sh1
        if m == 0:
            y = attention_mixer(h, attn_w_qkv[j], attn_w_o[j], attn_q_gain[j], attn_k_gain[j], cos, sin)
        elif m == 1:
            y = hyena_mixer(h, hy_w_in[j], hy_conv_w[j], hy_conv_b[j], hy_f_w1[j], hy_f_b1[j],
                            hy_f_w2[j], hy_f_b2[j], hy_f_w3[j], hy_f_freq[j], hy_skip[j], hy_w_out[j],
                            z, decay)
        else:
            y = s5_mixer(h, s5_A_re[j], s5_A_im[j], s5_log_dt[j], s5_B_re[j], s5_B_im[j],
                         s5_C_re[j], s5_C_im[j], s5_D[j], s5_w_glu[j])
        x = x + g1 * y
        h = rmsnorm_2(x, norm2_g[i]) * (1.0 + sc2) + sh2
        x = x + g2 * conv_ffn(h, ffn_w_up[i], ffn_conv_w[i], ffn_conv_b[i], ffn_w_down[i])
    return rmsnorm_2(x, final_g)


def setup_inputs(seed=0):
    out = dict(first_inputs(seed))
    for name, value in second_inputs(seed + 1).items():
        if name != "x":
            out[name + "_2"] = value
    return out


def reference(
    x, meta_tokens, norm_mix_gain, w_in, conv_q, conv_k, conv_v, dn_a_log, dn_dt_bias,
    dn_out_norm_gain, sb_q_norm_gain, sb_k_norm_gain, w_branch_dn, w_branch_sb, w_out,
    norm_ffn_gain, w_ffn_in, w_ffn_out, c_2, ada_w_2, ada_b_2, norm1_g_2, norm2_g_2, final_g_2,
    attn_w_qkv_2, attn_w_o_2, attn_q_gain_2, attn_k_gain_2, hy_w_in_2, hy_conv_w_2, hy_conv_b_2,
    hy_f_w1_2, hy_f_b1_2, hy_f_w2_2, hy_f_b2_2, hy_f_w3_2, hy_f_freq_2, hy_skip_2, hy_w_out_2,
    s5_A_re_2, s5_A_im_2, s5_log_dt_2, s5_B_re_2, s5_B_im_2, s5_C_re_2, s5_C_im_2, s5_D_2,
    s5_w_glu_2, ffn_w_up_2, ffn_conv_w_2, ffn_conv_b_2, ffn_w_down_2,
):
    x = first_block(
        x, meta_tokens, norm_mix_gain, w_in, conv_q, conv_k, conv_v, dn_a_log, dn_dt_bias,
        dn_out_norm_gain, sb_q_norm_gain, sb_k_norm_gain, w_branch_dn, w_branch_sb, w_out,
        norm_ffn_gain, w_ffn_in, w_ffn_out,
    )
    return second_block(
        x, c_2, ada_w_2, ada_b_2, norm1_g_2, norm2_g_2, final_g_2, attn_w_qkv_2, attn_w_o_2,
        attn_q_gain_2, attn_k_gain_2, hy_w_in_2, hy_conv_w_2, hy_conv_b_2, hy_f_w1_2, hy_f_b1_2,
        hy_f_w2_2, hy_f_b2_2, hy_f_w3_2, hy_f_freq_2, hy_skip_2, hy_w_out_2, s5_A_re_2,
        s5_A_im_2, s5_log_dt_2, s5_B_re_2, s5_B_im_2, s5_C_re_2, s5_C_im_2, s5_D_2, s5_w_glu_2,
        ffn_w_up_2, ffn_conv_w_2, ffn_conv_b_2, ffn_w_down_2,
    )


_drawn_inputs = setup_inputs


def setup_inputs(seed=0):
    import zlib

    import numpy as np

    out = dict(_drawn_inputs(seed))
    spreads = {}
    factors = {'norm_mix_gain': 3.544,
     'dn_out_norm_gain': 7.885,
     'sb_q_norm_gain': 8.0,
     'sb_k_norm_gain': 8.0,
     'norm_ffn_gain': 3.778,
     'norm1_g_2': 5.568,
     'norm2_g_2': 8.0,
     'final_g_2': 2.96,
     'attn_q_gain_2': 8.0,
     'attn_k_gain_2': 8.0,
     'hy_conv_b_2': 5.709,
     'hy_f_b1_2': 4.761,
     'hy_f_b2_2': 3.686,
     'hy_f_freq_2': 8.0,
     'ffn_conv_b_2': 8.0}
    for name, (base, spread) in spreads.items():
        noise = np.random.default_rng([zlib.crc32(name.encode()), seed]).standard_normal(out[name].shape)
        drawn = base * np.exp(spread * noise) if base else spread * noise
        out[name] = __import__('jax').numpy.asarray(drawn.astype(out[name].dtype))
    for name, factor in factors.items():
        out[name] = (out[name] * factor).astype(out[name].dtype)
    return out
```

```python
from contextlib import ExitStack

import numpy as np

import concourse.bass as bass
from concourse import mybir

F32 = mybir.dt.float32
ALU = mybir.AluOpType
ACT = mybir.ActivationFunctionType
AX = mybir.AxisListType
ds = bass.ds

P = 128
D = 1024
KD = D // P
SEQ = 512
META = 16
T = META + SEQ
TH = T // 2
NT = SEQ // P
HEADS = 8
DV = 256
DFF = 2816
KF = DFF // P
EPS = 1e-6
R = 4
SLOT = 11 * 256
NEG = -1e30
LEVELS = 7
QH, KVH, HD = 16, 4, 64
ORDERS = 2
EMB, FW = 33, 64

C_DQ, C_DK, C_DV, C_DZ = 0, 1024, 2048, 4096
C_AB, C_SQ, C_SK, C_SV = 6144, 6160, 7184, 8208
C_GD, C_GS = 9232, 10256

ROWS = {}


def _rows():
    tiles = [
        [("conv_q", 32), ("conv_k", 32), ("conv_v", 64)],
        [("norm_mix", 8), ("dn_gain", 2), ("sbq", 1), ("sbk", 1), ("norm_ffn", 8), ("norm1", 16),
         ("norm2", 16), ("final", 8), ("gq", 1), ("gk", 1), ("freq", 1), ("b1", 1), ("b2", 1),
         ("c", 8), ("skip", 16)],
        [("hy_w", 72), ("hy_b", 24)],
        [("ada_b", 96)],
        [("fc_w0", 66), ("fc_b0", 22)],
        [("fc_w1", 66), ("fc_b1", 22)],
    ]
    for n, tile in enumerate(tiles):
        at = n * P
        for name, rows in tile:
            ROWS[name] = (at, rows)
            at += rows
    return len(tiles)


PT = _rows()


def tables():
    i = np.arange(P)
    square = [
        np.eye(P),
        (i[:, None] <= i[None, :]),
        (i[:, None] >= i[None, :]),
        (i[:, None] // HD == i[None, :] // HD),
        (i[:, None] < i[None, :]),
        np.where(i[:, None] < i[None, :], 0.0, NEG),
        (i[:, None] == i[None, :] % HD),
        (i[:, None] == HD + i[None, :] % HD),
    ]
    rot = np.zeros((P, P))
    rot[i[1::2], i[0::2]] = -1.0
    rot[i[0::2], i[1::2]] = 1.0
    square.append(rot)
    delta = [
        np.where(i[None, :] >= i[:, None], 0.0, NEG),
        np.where(i[None, :] < i[:, None], 0.0, NEG),
    ]
    for s in range(LEVELS):
        b = i >> s
        delta.append((b[:, None] % 2 == 1) & (b[None, :] == b[:, None] - 1))
    flat = lambda a: np.ascontiguousarray(np.concatenate([np.asarray(x, np.float32) for x in a], axis=1))
    n_freq = HD // 4
    inv = (1.0 / (np.float32(10000.0) ** (np.arange(n_freq, dtype=np.float32) / np.float32(n_freq)))).astype(np.float32)
    t = np.arange(SEQ)
    ang = np.concatenate([(t // 64)[:, None].astype(np.float32) * inv, (t % 64)[:, None].astype(np.float32) * inv], 1)
    ang = np.repeat(ang.astype(np.float64), 2, axis=1).T
    rope = flat([np.tile(np.cos(ang), (2, 1)), np.tile(np.sin(ang), (2, 1))])
    w = np.pi * ((2 * t[:, None] + 1) * t[None, :] % (4 * SEQ)) / (2 * SEQ)
    rows = lambda a: flat([a[n * P:(n + 1) * P] for n in range(NT)])
    fwd = flat([rows(np.cos(w).T), rows(np.sin(w).T)])
    inv_dft = flat([rows(np.cos(w) / SEQ), rows(np.sin(w) / SEQ)])
    lin = np.linspace(0.0, 1.0, SEQ, dtype=np.float32)[:, None]
    bands = (EMB - 1) // 2
    wl = (np.float32(2.0 * np.pi) * np.arange(SEQ, dtype=np.float32) / np.float32(SEQ))
    f = np.linspace(1e-4, bands - 1, bands, dtype=np.float32)
    a = (wl[:, None] * f[None, :]).astype(np.float32)
    pos = np.concatenate([lin, np.cos(a), -np.sin(a)], axis=1).astype(np.float32).T
    deltas = np.abs(np.linspace(np.log(1e-2) / 1.5, np.log(1e-2) / 0.3, D, dtype=np.float32))
    decay = np.exp(-lin * deltas[None, :]).astype(np.float32)
    return {"t_square": flat(square), "t_delta": flat(delta), "t_rope": rope, "t_fwd": fwd,
            "t_inv": inv_dft, "t_pos": np.ascontiguousarray(pos), "t_decay": decay}


def build(nc, A, out, stop=None):
    ctx = ExitStack()
    with ctx:
        top = [(nc.sbuf_base + 31) // 32 * 32]

        def at(name, shape, offset, parts=P):
            return nc.alloc_sbuf_tensor_at(name, [parts, *shape], F32, offset=top[0] + 4 * offset)

        here = [0]

        def fresh(name, *shape, parts=P):
            n = int(np.prod(shape))
            t = at(name, shape, here[0], parts)
            here[0] += (n + 7) // 8 * 8
            return t

        def sem(name):
            return ctx.enter_context(nc.semaphore(name))

        ring = fresh("ring", R, SLOT)
        H = fresh("H", KD, T)
        H_END = here[0]
        HN = fresh("HN", KD, T)
        pcol = fresh("pcol", PT, P)
        square = fresh("square", 9, P)
        ident, triu, tril, pair_ones, vis, vis_neg, dup0, dup1, rot = (square[:, n, :] for n in range(9))
        ones = fresh("ones", P)
        tiny = fresh("tiny", 8)
        eps, zero = tiny[:, 0:1], tiny[:, 1:2]
        mod = fresh("mod", 2, 6 * KD)
        gsc = fresh("gsc", 2, 2, KD)
        csil = fresh("csil", KD)
        top_words = (nc.sbuf_usable_end - top[0]) // 4

        def col(name, n=0):
            c = ROWS[name][0] + n
            return pcol[:, c // P, c % P:c % P + 1]

        def cols(name, n, count):
            c = ROWS[name][0] + n
            return pcol[:, c // P, c % P:c % P + count]

        def dcol(name, n):
            c = ROWS[name][0]
            return pcol[:, c // P, ds(n + c % P, 1)]

        norm_at = here[0]
        NSQ = fresh("NSQ", 2, T)
        NRS = fresh("NRS", T)
        work = here[0]

        QK = fresh("QK", 2 * HEADS, T)
        QC, KC = QK[:, 0:HEADS, :], QK[:, HEADS:2 * HEADS, :]
        VO = fresh("VO", NT, HEADS, DV)
        g_tok = fresh("g_tok", NT + 1, HEADS)
        b_tok = fresh("b_tok", NT + 1, HEADS)
        ab = fresh("ab", 16)
        wab = fresh("wab", KD, 16)
        abrow = fresh("abrow", 16, parts=1)
        soft = fresh("soft", 2, NT + 1, 16)
        xt = at("xt", [NT, D], work)
        mt = at("mt", [D], work + NT * D, META)
        prow = at("prow", [PT, P], work + NT * D + D)
        scratch = here[0]
        xpad = fresh("xpad", 2, 536)
        cv = fresh("cv", 2, T)
        RSB = fresh("RSB", T)
        vm = fresh("vm", HEADS, DV, parts=META)
        vmb = fresh("vmb", HEADS, DV, parts=META)
        km = fresh("km", HEADS, P, parts=META)
        gmb = fresh("gmb", HEADS, META, parts=META)
        ml = fresh("ml", HEADS, META, parts=META)
        mlm = fresh("mlm", HEADS, META, parts=META)
        mx = fresh("mx", HEADS, META, parts=META)
        my = fresh("my", HEADS, META, parts=META)
        mp = fresh("mp", HEADS, META, parts=META)
        msm = fresh("msm", 5, HEADS, parts=META)
        peak = [here[0]]
        here[0] = scratch
        masks = fresh("masks", 2 + LEVELS, P)
        S = fresh("S", HEADS, DV)
        G4 = HEADS // 2
        group = []
        for g in range(2):
            group.append(dict(
                k=fresh(f"k{g}", G4, P),
                q=fresh(f"q{g}", G4, P),
                gb=fresh(f"gb{g}", G4, P),
                dt=fresh(f"dt{g}", G4, P),
                lp=fresh(f"lp{g}", 2, G4, P),
                x=fresh(f"x{g}", G4, P),
                y=at(f"y{g}", [G4, P], norm_at + g * G4 * P),
                lm=fresh(f"lm{g}", 2, G4, P),
                sm=fresh(f"sm{g}", 8, G4)))
        peak.append(here[0])
        assert max(peak) <= top_words, (peak, top_words)

        QSK = at("QSK", [2 * HEADS, T], work)
        here[0] = scratch
        SV = fresh("SV", NT + 1, D)
        SBW = 14 * P
        SBX = 10 * P
        sbz = fresh("sbz", 2, SBW)
        sbe = fresh("sbe", SBW)
        sbn = fresh("sbn", SBW)
        here[0] = norm_at
        sbk = fresh("sbk", T)
        sbv = fresh("sbv", NT + 1, P)
        assert here[0] <= work
        here[0] = scratch
        ZT = at("ZT", [2, SEQ], scratch)
        GT = fresh("GT", KD, SEQ)
        MG = fresh("MG", KD, SEQ)
        ACTF = at("ACTF", [KF, SEQ], work)
        SG = at("SG", [2, SEQ], work + KF * SEQ)

        GP = at("GP", [2, SEQ + 2], work + (KF + 2) * SEQ)
        here[0] = work
        QG = fresh("QG", 10, SEQ)
        KDUP = fresh("KDUP", KVH, SEQ)
        VG = fresh("VG", NT, KVH * HD)
        ropes = fresh("ropes", 2, SEQ)
        rtmp = fresh("rtmp", SEQ)
        PB = fresh("PB", 2, NT, SEQ)
        PTB = fresh("PTB", 2, NT, SEQ)
        OG = fresh("OG", KD, SEQ)
        qst = fresh("qst", 2, SEQ)
        kst = fresh("kst", SEQ)
        vst = fresh("vst", NT, HD)
        asm = fresh("asm", 2, 4, NT)
        assert here[0] <= top_words
        here[0] = work
        U = fresh("U", 3 * KD, SEQ)
        UP_AT = here[0]
        UP = fresh("UP", 2, SEQ + 2)
        ZK = fresh("ZK", NT, SEQ)
        PM = fresh("PM", 2, NT, SEQ)
        FB = fresh("FB", 2, SEQ)
        AB = fresh("AB", 2, SEQ)
        KS = fresh("KS", 2, 2, SEQ)
        YT = at("YT", [2, SEQ], UP_AT)
        DEC = fresh("DEC", NT, SEQ)
        W3 = fresh("W3", 2, SEQ, parts=FW)
        A1 = fresh("A1", 3, SEQ, parts=FW)
        POS = fresh("POS", SEQ, parts=EMB)
        W1 = fresh("W1", FW, parts=EMB)
        W2 = fresh("W2", FW, parts=FW)
        later_t = fresh("later_t", 1)
        rn = fresh("rn", NT)
        assert here[0] <= top_words, here[0]
        ytmp = at("ytmp", [2, SEQ], norm_at)
        YF = at("YF", [2, NT, SEQ], H_END)
        OUT = at("OUT", [NT, D], work)

        ps = ctx.enter_context(nc.psum_tensor("ps", [P, 8, 512], F32))

        def half(b, m=P):
            return ps[0:m, b:b + 2, 0:TH]

        def split(ap):
            return ap.rearrange("p (h n) -> p h n", h=2)

        slot_full = [sem(f"slot_full{r}") for r in range(R)]
        acc_ready = sem("acc_ready")
        acc_free = [sem(f"acc_free{b}") for b in range(2)]
        x_in, small_in, table_in = sem("x_in"), sem("small_in"), sem("table_in")
        mask_in = sem("mask_in")
        cleared = sem("cleared")
        t_ready, t_done = sem("t_ready"), sem("t_done")
        n_sq, n_sum, n_rs, n_out = sem("n_sq"), sem("n_sum"), sem("n_rs"), sem("n_out")
        ab_ready = sem("ab_ready")
        conv_done, silu_done = sem("conv_done"), sem("silu_done")
        l2_sq, l2_sum, l2_rs, l2_done = sem("l2_sq"), sem("l2_sum"), sem("l2_rs"), sem("l2_done")
        vt_ready, vt_done = sem("vt_ready"), sem("vt_done")
        ab_x, ab_l = sem("ab_x"), sem("ab_l")
        m_pe, m_dve, m_act = sem("m_pe"), sem("m_dve"), sem("m_act")
        steps = ("staged", "gates", "expin", "expd", "lower", "masked", "prod", "inv", "pcopy", "delta", "ktok",
                 "kbg", "wt", "nw", "vb", "vn", "vnc", "o", "oc", "sd", "state")
        chunk = [{name: sem(f"{name}{g}") for name in steps} for g in range(2)]
        o_sq, o_sum, o_rs, z_done = sem("o_sq"), sem("o_sum"), sem("o_rs"), sem("z_done")
        h_sq, h_sum, h_rs, h_done = sem("h_sq"), sem("h_sum"), sem("h_rs"), sem("h_done")
        sv_done = sem("sv_done")
        sb_k, sb_v_in, sb_z, sb_zs, sb_abs, sb_ln = sem("sb_k"), sem("sb_v_in"), sem("sb_z"), sem("sb_zs"), sem("sb_abs"), sem("sb_ln")
        sb_n, sb_c, sb_lw, sb_w, sb_o, sb_oc = sem("sb_n"), sem("sb_c"), sem("sb_lw"), sem("sb_w"), sem("sb_o"), sem("sb_oc")
        merged = sem("merged")
        mod_done, silu_c, fc_conv, fc_silu = sem("mod_done"), sem("silu_c"), sem("fc_conv"), sem("fc_silu")
        a_in, a_nrm, a_rot, a_done, a_dup, a_dupc = sem("a_in"), sem("a_nrm"), sem("a_rot"), sem("a_done"), sem("a_dup"), sem("a_dupc")
        a_qk, a_v, a_s, a_mx, a_e, a_p = sem("a_qk"), sem("a_v"), sem("a_s"), sem("a_mx"), sem("a_e"), sem("a_p")
        a_t, a_tc, a_o, a_oc = sem("a_t"), sem("a_tc"), sem("a_o"), sem("a_oc")
        y_in, y_w, y_mlp, y_arg, y_sin = sem("y_in"), sem("y_w"), sem("y_mlp"), sem("y_arg"), sem("y_sin")
        y_conv, y_f, y_fb, y_ab, y_pm, y_n, y_rn = sem("y_conv"), sem("y_f"), sem("y_fb"), sem("y_ab"), sem("y_pm"), sem("y_n"), sem("y_rn")
        y_t, y_tc, y_dft, y_kc, y_y, y_inv, y_z = sem("y_t"), sem("y_tc"), sem("y_dft"), sem("y_kc"), sem("y_y"), sem("y_inv"), sem("y_z")
        f_t, f_out, stored = sem("f_t"), sem("f_out"), sem("stored")

        class Gemm:
            slabs = tiles = evacs = 0
            landed = [0] * R

            def __init__(self, src, nslab, kt, width, per=2, pair=False, evac=True, parts=1):
                self.src, self.nslab, self.kt, self.width, self.per, self.pair = src, nslab, kt, width, per, pair
                self.s0, self.t0, self.f0 = Gemm.slabs, Gemm.tiles, Gemm.evacs
                Gemm.slabs += nslab
                Gemm.tiles += nslab * per
                Gemm.evacs += nslab * per if evac else 0
                self.parts, self.base = parts, list(Gemm.landed)
                for r in range(nslab):
                    Gemm.landed[self.slot(r)] += 16 * parts
                plan.append(self)

            def slot(self, r):
                return (self.s0 + r) % R

            def view(self, r):
                return ring[:, self.slot(r), 0:self.kt * self.width].rearrange("p (k n) -> p k n", k=self.kt)

            def full(self, r):
                return self.base[self.slot(r)] + 16 * self.parts * (r // R + 1)

            def last(self, r):
                return self.t0 + (2 * (r // 2 + 1) if self.pair else self.per * (r + 1))

            def ready(self, t):
                return self.t0 + t + 1

            def free(self, t):
                return (self.f0 + t) // 2 + 1

            def freed(self, t):
                return self.free(t) + 1

            def buf(self, t):
                return (self.f0 + t) % 2

        plan = []

        def w_cols(w, c0, width=256):
            v = w.rearrange("(k p) n -> p k n", p=P)
            return lambda i, r, h: v[:, :, ds(i * (R * width) + (r * width + c0), width)]

        def w_gate_up(w):
            v = w.rearrange("(k p) (h n) -> h p k n", p=P, h=2)
            return lambda i, r, h: v[h, :, :, ds(i * (R * P) + r * P, P)]

        def w_half_rows(w):
            v = w.rearrange("(q k p) n -> q p k n", p=P, q=2)
            return lambda i, r, h: v[r % 2, :, :, ds(i * (R // 2 * 256) + r // 2 * 256, 256)]

        w_in = A["w_in"][0]
        dn_qk = Gemm(w_cols(w_in, C_DQ), 8, KD, 256)
        dn_v = Gemm(w_cols(w_in, C_DV), 8, KD, 256)
        dn_z = Gemm(w_cols(w_in, C_DZ), 8, KD, 256)
        sb_qk = Gemm(w_cols(w_in, C_SQ), 8, KD, 256)
        sb_v = Gemm(w_cols(w_in, C_SV), 4, KD, 256, per=NT + 1)
        gate_dn = Gemm(w_cols(w_in, C_GD), 4, KD, 256)
        branch_dn = Gemm(w_cols(A["w_branch_dn"][0], 0, P), 8, 2 * KD, P, per=1)
        gate_sb = Gemm(w_cols(w_in, C_GS), 4, KD, 256)
        branch_sb = Gemm(w_cols(A["w_branch_sb"][0], 0), 4, KD, 256)
        mix_out = Gemm(w_cols(A["w_out"][0], 0), 4, KD, 256)
        ffn_in = Gemm(w_gate_up(A["w_ffn_in"][0]), KF, KD, 256, parts=2)
        ffn_out = Gemm(w_half_rows(A["w_ffn_out"][0]), 8, KF // 2, 256, per=1, pair=True)

        def groups(eng, gm):
            n = gm.nslab // R
            if n > 1:
                with eng.Fori(0, n) as i:
                    yield i, range(R)
            elif n:
                yield 0, range(R)
            if gm.nslab % R:
                yield n, range(gm.nslab % R)

        def pe_tile(pe, gm, i, r, m, rhs, halves):
            t = gm.per * r + m
            b = gm.buf(t)
            if m == 0:
                pe.wait_ge(slot_full[gm.slot(r)], i * (16 * gm.parts) + gm.full(r))
            pe.wait_ge(acc_free[b], i * (R * gm.per // 2) + gm.free(t))
            w = gm.view(r)
            for k in range(gm.kt):
                lhs = w[:, k, m * P:(m + 1) * P]
                x = rhs(k)
                if halves:
                    for h in range(2):
                        mm = pe.matmul(ps[:, 2 * b + h, 0:TH], lhs, x[:, h * TH:(h + 1) * TH],
                                       start=k == 0, stop=k == gm.kt - 1)
                else:
                    mm = pe.matmul(ps[:, 2 * b, :], lhs, x, start=k == 0, stop=k == gm.kt - 1)
            mm.then_inc(acc_ready, 1)

        def wide(ap, n=P):
            return ap.unsqueeze(2).broadcast_to([ap.shape[0], ap.shape[1], n])

        def heads_of(ap, n):
            return ap.unsqueeze(1).broadcast_to([ap.shape[0], n, ap.shape[1]])

        ada = [Gemm(w_cols(A["ada_w_2"][l], 0), 24, KD, 256, evac=False) for l in range(2)]
        gq_qk = Gemm(w_cols(A["attn_w_qkv_2"][0], 0), 5, KD, 256)
        gq_v = Gemm(w_cols(A["attn_w_qkv_2"][0], (QH + KVH) * HD), 1, KD, 256, per=NT)
        gq_out = Gemm(w_cols(A["attn_w_o_2"][0], 0), 4, KD, 256)
        fc_in, fc_out = [None, None], [None, None]

        def conv_ffn(l):
            fc_in[l] = Gemm(w_gate_up(A["ffn_w_up_2"][l]), KF, KD, 256, parts=2)
            fc_out[l] = Gemm(w_half_rows(A["ffn_w_down_2"][l]), 8, KF // 2, 256, per=1, pair=True)

        conv_ffn(0)
        hy_in = Gemm(w_cols(A["hy_w_in_2"][0], 0), 12, KD, 256)
        dft_parts = [A["t_fwd"][:, 0:NT * SEQ], A["t_fwd"][:, NT * SEQ:], A["t_inv"][:, 0:NT * SEQ], A["t_inv"][:, NT * SEQ:]]
        dft = Gemm(lambda i, r, h: dft_parts[r].rearrange("p (k n) -> p k n", k=NT), 4, NT, SEQ, per=1, evac=False)
        hy_out = Gemm(w_cols(A["hy_w_out_2"][0], 0), 4, KD, 256)
        conv_ffn(1)

        def taken(eng, gm, i, t):
            eng.wait_ge(acc_free[gm.buf(t)], i * (R * gm.per // 2) + gm.freed(t))

        def acc_in(eng, gm, i, t):
            eng.wait_ge(acc_ready, i * (R * gm.per) + gm.ready(t))
            return gm.buf(t)

        def norm_act(act, u, x, n):
            for k in range(KD):
                if k >= 2:
                    act.wait_ge(n_sum, KD * u + k - 1)
                act.activation(NSQ[:, k % 2, 0:n], x(k), ACT.Square).then_inc(n_sq, 1)
            act.wait_ge(n_sum, KD * (u + 1))
            src = half(6) if n == T else ps[:, 6, 0:n]
            dst = split(NRS[:, 0:n]) if n == T else NRS[:, 0:n]
            if u:
                act.wait_ge(n_out, KD * u)
            act.activation(dst, src, ACT.Ln, bias=eps, scale=1.0 / D)
            act.drain()
            act.activation(NRS[:, 0:n], NRS[:, 0:n], ACT.Exp, bias=zero, scale=-0.5).then_inc(n_rs, 1)

        def norm_pe(pe, u, n):
            for k in range(KD):
                pe.wait_ge(n_sq, KD * u + k + 1)
                if n == T:
                    for h in range(2):
                        mm = pe.matmul(ps[:, 6 + h, 0:TH], ones[:, :], NSQ[:, k % 2, h * TH:(h + 1) * TH],
                                       start=k == 0, stop=k == KD - 1)
                else:
                    mm = pe.matmul(ps[:, 6, 0:n], ones[:, :], NSQ[:, k % 2, 0:n], start=k == 0, stop=k == KD - 1)
                mm.then_inc(n_sum, 1)

        def norm_dve(dve, u, x, gain, n, y):
            dve.wait_ge(n_rs, u + 1)
            for k in range(KD):
                dve.scalar_tensor_tensor(y(k), x(k), gain(k), NRS[:, 0:n], ALU.mult, ALU.mult).then_inc(n_out, 1)

        def shift_dve(dve, u, l, n):
            dve.wait_ge(n_rs, u + 1)
            for k in range(KD):
                dve.scalar_tensor_tensor(HN[:, k, 0:SEQ], H[:, k, META:T], gsc[:, l, n, k:k + 1], NRS[:, 0:SEQ], ALU.mult, ALU.mult)
            dve.drain()
            for k in range(KD):
                c = n * 3 * KD + k
                dve.tensor_scalar(HN[:, k, 0:SEQ], HN[:, k, 0:SEQ], mod[:, l, c:c + 1], None, ALU.add).then_inc(n_out, 1)

        def head_pe(pe, gm, i, t, n):
            pe.wait_ge(h_sq, n + 1)
            pe.wait_ge(h_rs, n + 1)
            for h in range(2):
                mm = pe.matmul(ps[:, 6 + h, 0:TH], ones[:, :], NSQ[:, t % 2, h * TH:(h + 1) * TH], start=True, stop=True)
            mm.then_inc(h_sum, 1)

        def pe_gemm(pe, gm, rhs):
            for i, slabs in groups(pe, gm):
                for r in slabs:
                    for m in range(gm.per):
                        pe_tile(pe, gm, i, r, m, rhs, False)

        def pe_gemm_pair(pe, gm, rhs):
            for i, slabs in groups(pe, gm):
                for j in range(len(slabs) // 2):
                    for q in range(2):
                        pe.wait_ge(slot_full[gm.slot(2 * j + q)], i * 16 + gm.full(2 * j + q))
                    for m in range(2):
                        t = 2 * j + m
                        b = gm.buf(t)
                        pe.wait_ge(acc_free[b], i * (R // 2) + gm.free(t))
                        for q in range(2):
                            for k in range(gm.kt):
                                mm = pe.matmul(ps[:, 2 * b, :], gm.view(2 * j + q)[:, k, m * P:(m + 1) * P],
                                               rhs(q * gm.kt + k), start=q + k == 0, stop=q == 1 and k == gm.kt - 1)
                        mm.then_inc(acc_ready, 1)

        def tiles(gm, slabs):
            return range(len(slabs) * gm.per)

        SB = [(0, 0, META, P), (4 * P, P, META + P, P), (7 * P, 3 * P, META + 3 * P, P), (8 * P, 2 * P, META + 2 * P, P),
              (10 * P, 0, 0, META)]
        SB_V = [0, 1, 3, 2, NT]

        def sb_bank(b, n):
            c, q0, _, m = SB[n]
            c = c if n < 4 else 12 * P
            return ps[0:m, b + c // 512, c % 512:c % 512 + SEQ - q0]

        def sb_keys(x, n):
            c, q0, _, m = SB[n]
            return x[0:m, c:c + SEQ - q0]

        def sb_logits(pe, i, par):
            n = i * 2 + par
            pe.wait_ge(sb_k, n + 1)
            pe.wait_ge(sb_zs, n + 2)
            pe.wait_ge(sb_oc, n + 1)
            for t in (1, 2, 3, 4, 0):
                c, q0, k0, m = SB[t]
                mm = pe.matmul(sb_bank(0, t), sbk[:, k0:k0 + m],
                               QSK[:, ds(n, 1), META + q0:T].rearrange("p a n -> p (a n)"), start=True, stop=True)
            mm.then_inc(sb_z, 1)

        SMALL = 30
        block = ctx.enter_context(nc.Block())

        @block.sync
        def _(sp):
            done = []
            for gm in plan:
                def load(i, r):
                    n = gm.width // gm.parts
                    for h in range(gm.parts):
                        sp.dma_start(gm.view(r)[:, :, h * n:(h + 1) * n], gm.src(i, r, h))\
                            .then_inc(slot_full[gm.slot(r)], 16)

                def reread(i, r):
                    sp.wait_ge(acc_ready, i * (R * gm.per) + (gm.last(r) - R * gm.per))

                for r in range(min(R, gm.nslab)):
                    if gm.s0 + r >= R:
                        sp.wait_ge(acc_ready, done[gm.s0 + r - R])
                    load(0, r)
                turns, rest = gm.nslab // R, gm.nslab % R
                if turns > 1:
                    with sp.Fori(1, turns) as i:
                        for r in range(R):
                            reread(i, r)
                            load(i, r)
                for r in range(rest if turns else 0):
                    reread(turns, r)
                    load(turns, r)
                done += [gm.last(r) for r in range(gm.nslab)]

        @block.gpsimd
        def _(pool):
            pool.dma_start(xt[:, :, :], A["x"][0].rearrange("(n p) d -> p n d", p=P)).then_inc(x_in, 16)
            pool.dma_start(mt[:, :], A["meta_tokens"]).then_inc(x_in, 16)
            pool.dma_start(square[:, :, :].rearrange("p a b -> p (a b)"), A["t_square"]).then_inc(table_in, 16)
            pool.memset(ones[:, :], 1.0)
            pool.memset(tiny[:, 0:1], EPS)
            pool.memset(tiny[:, 1:2], 0.0)
            pool.memset(prow[:, :, :], 0.0)
            pool.memset(xpad[:, :, 0:3], 0.0).then_inc(cleared, 1)
            pool.wait_ge(cleared, 1)
            small = []

            def rows(name, src):
                r, n = ROWS[name]
                pool.dma_start(prow[r % P:r % P + n, r // P, 0:src.shape[-1]], src).then_inc(small_in, 16)
                small.append(name)

            tile = lambda ap: ap.rearrange("j (k p) -> (j k) p", p=P)
            one = lambda ap: ap.rearrange("(j k) -> j k", j=1)
            rows("conv_q", tile(A["conv_q"][0]))
            rows("conv_k", tile(A["conv_k"][0]))
            rows("conv_v", tile(A["conv_v"][0]))
            rows("norm_mix", tile(A["norm_mix_gain"]))
            rows("dn_gain", tile(A["dn_out_norm_gain"]))
            rows("sbq", A["sb_q_norm_gain"])
            rows("sbk", A["sb_k_norm_gain"])
            rows("norm_ffn", tile(A["norm_ffn_gain"]))
            rows("norm1", tile(A["norm1_g_2"]))
            rows("norm2", tile(A["norm2_g_2"]))
            rows("final", tile(one(A["final_g_2"])))
            for part in range(2):
                for name, src in (("gq", A["attn_q_gain_2"]), ("gk", A["attn_k_gain_2"])):
                    r = ROWS[name][0]
                    pool.dma_start(prow[r % P:r % P + 1, r // P, part * HD:(part + 1) * HD], src).then_inc(small_in, 16)
                    small.append(name)
            rows("freq", A["hy_f_freq_2"])
            rows("b1", A["hy_f_b1_2"])
            rows("b2", A["hy_f_b2_2"])
            rows("c", tile(A["c_2"]))
            rows("skip", tile(A["hy_skip_2"][0]))
            rows("hy_w", tile(A["hy_conv_w_2"][0]))
            rows("hy_b", tile(A["hy_conv_b_2"]))
            rows("ada_b", tile(A["ada_b_2"]))
            for l in range(2):
                rows(f"fc_w{l}", tile(A["ffn_conv_w_2"][l]))
                rows(f"fc_b{l}", tile(A["ffn_conv_b_2"][l:l + 1]))
            pool.dma_start(wab[:, :, :], w_cols(w_in, C_AB, 16)(0, 0, 0)).then_inc(small_in, 16)
            pool.dma_start(abrow[:, 0:8], A["dn_a_log"]).then_inc(small_in, 16)
            pool.dma_start(abrow[:, 8:16], A["dn_dt_bias"]).then_inc(small_in, 16)
            assert len(small) + 3 == SMALL
            pool.wait_ge(l2_done, 1 + 16)
            pool.wait_ge(vt_done, 2 + 32)
            pool.dma_start(masks[:, :, :].rearrange("p a b -> p (a b)"), A["t_delta"]).then_inc(mask_in, 16)
            pool.wait_ge(mask_in, 16)
            with pool.Fori(0, NT) as c:
                for l in range(LEVELS):
                    for g in range(2):
                        G, E = group[g], chunk[g]
                        if l == 0:
                            pool.wait_ge(E["lower"], c + 1)
                        if l == 2:
                            pool.wait_ge(E["inv"], c * LEVELS + 1)
                        if l >= 2:
                            pool.wait_ge(E["prod"], c * LEVELS + l - 1)
                        pool.tensor_tensor(G["lm"][:, l % 2, :, :], G["lp"][:, 0, :, :],
                                           heads_of(masks[:, 2 + l, :], G4), ALU.mult).then_inc(E["masked"], 1)
            pool.wait_ge(h_done, 1 + 2 * HEADS)
            pool.wait_ge(sv_done, 4 * (NT + 1))

            def stage_head(n):
                pool.tensor_copy(sbk[:, :].unsqueeze(1), QSK[:, ds(n + HEADS, 1), :]).then_inc(sb_k, 1)

            def stage_v(n):
                pool.tensor_copy(sbv[:, 0:NT, :], SV[:, 0:NT, ds(n * P, P)]).then_inc(sb_v_in, 1)
                pool.tensor_copy(sbv[0:META, NT, :], SV[0:META, NT, ds(n * P, P)]).then_inc(sb_v_in, 1)

            stage_head(0)
            stage_v(0)
            with pool.Fori(1, HEADS) as n:
                pool.wait_ge(sb_z, n)
                stage_head(n)
                pool.wait_ge(sb_o, n + 1)
                stage_v(n)

            taken(pool, ffn_out, 1, 2 * R - 1 - R)
            taken(pool, ffn_out, 1, 2 * R - 2 - R)
            pool.dma_start(ropes[:, :, :].rearrange("p a n -> p (a n)"), A["t_rope"]).then_inc(a_in, 16)
            pool.wait_ge(a_done, 10)
            pool.wait_ge(a_dupc, KVH)
            taken(pool, gq_v, 0, NT - 1)
            taken(pool, gq_v, 0, NT - 2)

            def stage_qk(g):
                pool.tensor_copy(qst[:, :, :], QG[:, ds(g * 2, 2), :]).then_inc(a_qk, 1)
                pool.tensor_copy(kst[:, :].unsqueeze(1), KDUP[:, ds(g, 1), :]).then_inc(a_qk, 1)

            def stage_vg(g):
                pool.tensor_copy(vst[:, :, :], VG[:, :, ds(g * HD, HD)]).then_inc(a_v, 1)

            stage_qk(0)
            stage_vg(0)
            with pool.Fori(1, KVH) as g:
                pool.wait_ge(a_s, g * 4)
                stage_qk(g)
                pool.wait_ge(a_o, g * 4 + 2)
                stage_vg(g)

            taken(pool, fc_out[0], 1, R - 1)
            taken(pool, fc_out[0], 1, R - 2)
            pool.dma_start(POS[:, :], A["t_pos"]).then_inc(y_in, 16)
            pool.dma_start(W1[:, :], A["hy_f_w1_2"][0]).then_inc(y_in, 16)
            pool.dma_start(W2[:, :], A["hy_f_w2_2"][0]).then_inc(y_in, 16)
            w3 = A["hy_f_w3_2"][0].rearrange("p (o s d) -> o p s d", o=ORDERS, s=2)
            dec = A["t_decay"].rearrange("(n p) d -> p n d", p=P)
            for u in range(2 * ORDERS):
                half_d = slice(u % 2 * SEQ, (u % 2 + 1) * SEQ)
                pool.wait_ge(y_f, u * NT + 2)
                pool.dma_start(W3[:, :, :], w3[u // 2][:, :, half_d]).then_inc(y_w, 16)
                pool.wait_ge(y_pm, u * NT + 2)
                pool.dma_start(DEC[:, :, :], dec[:, :, half_d]).then_inc(y_w, 16)

        @block.tensor
        def _(pe):
            pe.sem_inc(vt_ready, 4)
            pe.sem_inc(l2_sum, 2)
            pe.sem_inc(h_sum, 2)
            pe.sem_inc(sb_c, 1)
            pe.sem_inc(sb_o, 1)
            pe.sem_inc(a_t, 5)
            pe.sem_inc(a_o, 2)
            pe.sem_inc(y_f, 2)
            pe.wait_ge(x_in, 32)
            pe.wait_ge(table_in, 16)
            for k in range(KD):
                if k >= 2:
                    pe.wait_ge(t_done, 2 * (k - 1))
                for n in range(NT):
                    mm = pe.transpose(ps[:, k % 2, n * P:(n + 1) * P], xt[:, n, k * P:(k + 1) * P], ident)
                mm.then_inc(t_ready, 1)
                pe.transpose(ps[:, 2 + k % 2, 0:META], mt[:, k * P:(k + 1) * P], ident[0:META, 0:META])\
                    .then_inc(t_ready, 1)
            pe.wait_ge(small_in, 16 * SMALL)
            for n in range(PT):
                mm = pe.transpose(ps[:, 4 + n // 4, n % 4 * P:(n % 4 + 1) * P], prow[:, n, :], ident)
            mm.then_inc(t_ready, 1)
            norm_pe(pe, 0, T)
            pe.wait_ge(n_out, KD)
            pe.wait_ge(t_done, 2 * KD + 1)
            for n in range(NT + 1):
                m, c0 = (P, META + n * P) if n < NT else (META, 0)
                for k in range(KD):
                    pe.matmul(ps[0:m, 4, n * 16:(n + 1) * 16], HN[:, k, c0:c0 + m], wab[:, k, :],
                              start=k == 0, stop=k == KD - 1)
            pe.matmul(ps[:, 5, 0:16], ones[0:1, :], abrow[:, :], start=True, stop=True).then_inc(ab_ready, 1)
            for i, slabs in groups(pe, dn_qk):
                for r in slabs:
                    for m in range(2):
                        pe_tile(pe, dn_qk, i, r, m, lambda k: HN[:, k, :], True)

            def v_turn(i, t):
                n = i * (2 * R) + t
                src = cv[:, t % 2, :]
                pe.wait_ge(silu_done, n + 2 + 16 + 1)
                pe.wait_ge(vt_done, n * 2 + 2)
                for c in range(NT):
                    mm = pe.transpose(ps[:, 6, c * P:(c + 1) * P], src[:, META + c * P:META + (c + 1) * P], ident)
                mm.then_inc(vt_ready, 1)
                pe.transpose(ps[0:META, 7, 0:P], src[:, 0:META], ident).then_inc(vt_ready, 1)

            pe.wait_ge(ab_x, 1)
            for i, slabs in groups(pe, dn_v):
                for r in slabs:
                    for m in range(2):
                        t = 2 * r + m
                        n = i * (2 * R) + t
                        pe_tile(pe, dn_v, i, r, m, lambda k: HN[:, k, :], True)
                        pe.wait_ge(l2_sq, n + 1)
                        pe.wait_ge(l2_rs, n + 1)
                        for h in range(2):
                            mm = pe.matmul(ps[:, 4 + h, 0:TH], ones[:, :], NSQ[:, t % 2, h * TH:(h + 1) * TH],
                                           start=True, stop=True)
                        mm.then_inc(l2_sum, 1)
                        if t:
                            v_turn(i, t - 1)
                v_turn(i, 2 * R - 1)

            m = META
            pe.wait_ge(l2_done, 1 + 16)
            pe.wait_ge(vt_done, 2 + 32)
            pe.wait_ge(m_dve, 1)
            for h in range(HEADS):
                pe.matmul(ps[0:m, 0, h * m:(h + 1) * m], gmb[:, h, :], triu[0:m, 0:m], start=True, stop=True)
            pe.matmul(ps[0:m, 1, 0:HEADS], triu[0:m, 0:m], gmb[:, :, 0], start=True, stop=True)
            for h in range(HEADS):
                kh = KC[:, h, 0:m]
                pe.matmul(ps[0:m, 2, h * m:(h + 1) * m], kh, kh, start=True, stop=True)
            for h in range(HEADS):
                mm = pe.transpose(ps[0:m, 3 + h // 4, h % 4 * P:(h % 4 + 1) * P], KC[:, h, 0:m], ident)
            mm.then_inc(m_pe, 1)
            for l in range(4):
                pe.wait_ge(m_dve, 4 + 3 * l)
                for h in range(HEADS):
                    mm = pe.matmul(ps[0:m, 0, h * m:(h + 1) * m], mlm[:, h, :], my[:, h, :] if l else ident[0:m, 0:m],
                                   start=True, stop=True)
                mm.then_inc(m_pe, 1)
                if l:
                    pe.wait_ge(m_dve, 5 + 3 * l)
                    for h in range(HEADS):
                        mm = pe.matmul(ps[0:m, 1, h * m:(h + 1) * m], mx[:, h, :], mp[:, h, :], start=True, stop=True)
                    for h in range(HEADS):
                        mm = pe.matmul(ps[0:m, 2, h * m:(h + 1) * m], mp[:, h, :], mx[:, h, :], start=True, stop=True)
                    mm.then_inc(m_pe, 1)
            pe.wait_ge(m_dve, 16)
            for h in range(HEADS):
                mm = pe.matmul(ps[0:m, 4 + h // 2, h % 2 * DV:(h % 2 + 1) * DV], my[:, h, :], vmb[:, h, :],
                               start=True, stop=True)
            mm.then_inc(m_pe, 1)
            pe.wait_ge(m_dve, 17)
            for h in range(HEADS):
                mm = pe.matmul(ps[:, h // 2, h % 2 * DV:(h % 2 + 1) * DV], km[:, h, :], vm[:, h, :], start=True, stop=True)
            mm.then_inc(m_pe, 1)

            pe.wait_ge(m_dve, 18)
            with pe.Fori(0, NT) as c:
                for g in range(2):
                    G, E, b = group[g], chunk[g], 4 * g
                    pe.wait_ge(E["staged"], c + 1)
                    pe.wait_ge(E["oc"], c + 1)
                    for h in range(G4):
                        pe.matmul(ps[:, b, h * P:(h + 1) * P], G["gb"][:, h, :], triu, start=True, stop=True)
                    pe.matmul(ps[:, b + 1, 0:G4], triu, G["gb"][:, :, 0], start=True, stop=True)
                    for h in range(G4):
                        pe.matmul(ps[:, b + 2, h * P:(h + 1) * P], G["k"][:, h, :], G["k"][:, h, :], start=True, stop=True)
                    for h in range(G4):
                        mm = pe.matmul(ps[:, b + 3, h * P:(h + 1) * P], G["k"][:, h, :], G["q"][:, h, :],
                                       start=True, stop=True)
                    mm.then_inc(E["gates"], 1)
                for l in range(LEVELS):
                    for g in range(2):
                        G, E, b = group[g], chunk[g], 4 * g
                        pe.wait_ge(E["masked"], c * LEVELS + l + 1)
                        if l:
                            pe.wait_ge(E["inv"], c * LEVELS + l)
                        for h in range(G4):
                            mm = pe.matmul(ps[:, b, h * P:(h + 1) * P], G["lm"][:, l % 2, h, :],
                                           G["y"][:, h, :] if l else ident, start=True, stop=True)
                        mm.then_inc(E["prod"], 1)
                        if l == 0:
                            for h in range(G4):
                                mm = pe.transpose(ps[:, b + 1, h * P:(h + 1) * P], G["k"][:, h, :], ident)
                            mm.then_inc(E["ktok"], 1)
                    for g in range(2):
                        G, E, b = group[g], chunk[g], 4 * g
                        if l:
                            pe.wait_ge(E["pcopy"], c * (LEVELS - 1) + l)
                            for h in range(G4):
                                mm = pe.matmul(ps[:, b + 2, h * P:(h + 1) * P], G["x"][:, h, :], G["lp"][:, 1, h, :],
                                               start=True, stop=True)
                            if l < LEVELS - 1:
                                for h in range(G4):
                                    mm = pe.matmul(ps[:, b + 3, h * P:(h + 1) * P], G["lp"][:, 1, h, :], G["x"][:, h, :],
                                                   start=True, stop=True)
                            mm.then_inc(E["delta"], 1)
                for g in range(2):
                    G, E, b = group[g], chunk[g], 4 * g
                    pe.wait_ge(E["inv"], c * LEVELS + LEVELS)
                    pe.wait_ge(E["kbg"], c + 1)
                    for h in range(G4):
                        mm = pe.matmul(ps[:, b, h * P:(h + 1) * P], G["gb"][:, h, :], G["y"][:, h, :], start=True, stop=True)
                    mm.then_inc(E["wt"], 1)
                for g in range(2):
                    G, E, b = group[g], chunk[g], 4 * g
                    pe.wait_ge(E["vb"], c + 1)
                    pe.wait_ge(E["nw"], c + 1)
                    pe.wait_ge(E["state"], c + 1)
                    for h in range(G4):
                        dst = ps[:, b + 2 + h // 2, h % 2 * DV:(h % 2 + 1) * DV]
                        vb = G["lm"][:, h // 2, h % 2 * 2:h % 2 * 2 + 2, :].rearrange("p a n -> p (a n)")
                        pe.matmul(dst, G["y"][:, h, :], vb, start=True, stop=False)
                        mm = pe.matmul(dst, G["x"][:, h, :], S[:, g * G4 + h, :], start=False, stop=True)
                    mm.then_inc(E["vn"], 1)
                for g in range(2):
                    G, E, b = group[g], chunk[g], 4 * g
                    pe.wait_ge(E["vnc"], c + 1)
                    for h in range(G4):
                        for e in range(2):
                            dst = ps[:, b + h // 2, (h % 2 * 2 + e) * P:(h % 2 * 2 + e + 1) * P]
                            pe.matmul(dst, S[:, g * G4 + h, e * P:(e + 1) * P], G["q"][:, h, :], start=True, stop=False)
                            mm = pe.matmul(dst, G["lp"][:, h // 2, h % 2 * 2 + e, :], G["dt"][:, h, :], start=False, stop=True)
                    mm.then_inc(E["o"], 1)
                    for h in range(G4):
                        dst = ps[:, b + 2 + h // 2, h % 2 * DV:(h % 2 + 1) * DV]
                        vn = G["lp"][:, h // 2, h % 2 * 2:h % 2 * 2 + 2, :].rearrange("p a n -> p (a n)")
                        mm = pe.matmul(dst, G["k"][:, h, :], vn, start=True, stop=True)
                    mm.then_inc(E["sd"], 1)

            for g in range(2):
                pe.wait_ge(chunk[g]["oc"], 1 + NT)
                pe.wait_ge(chunk[g]["state"], 1 + NT)
            for i, slabs in groups(pe, dn_z):
                for r in slabs:
                    for m in range(2):
                        pe_tile(pe, dn_z, i, r, m, lambda k: HN[:, k, META:T], False)
                    n = i * R + r
                    pe.wait_ge(o_sq, n + 1)
                    pe.wait_ge(o_rs, n + 1)
                    for e in range(2):
                        mm = pe.matmul(ps[:, 6, :], ones[:, :], NSQ[:, e, 0:SEQ], start=e == 0, stop=e == 1)
                    mm.then_inc(o_sum, 1)
            pe.wait_ge(z_done, 2 + 2 * HEADS)
            for i, slabs in groups(pe, sb_qk):
                for r in slabs:
                    for m in range(2):
                        t = 2 * r + m
                        pe_tile(pe, sb_qk, i, r, m, lambda k: HN[:, k, :], True)
                        if t:
                            head_pe(pe, sb_qk, i, t - 1, i * (2 * R) + (t - 1))
                head_pe(pe, sb_qk, i, 2 * R - 1, i * (2 * R) + (2 * R - 1))
            for r in range(sb_v.nslab):
                pe.wait_ge(slot_full[sb_v.slot(r)], sb_v.full(r))
                for n in range(NT + 1):
                    t = r * (NT + 1) + n
                    b = sb_v.buf(t)
                    pe.wait_ge(acc_free[b], sb_v.free(t))
                    m, c0 = (P, META + n * P) if n < NT else (META, 0)
                    for k in range(KD):
                        mm = pe.matmul(ps[0:m, 2 * b, 0:256], HN[:, k, c0:c0 + m], sb_v.view(r)[:, k, :],
                                       start=k == 0, stop=k == KD - 1)
                    mm.then_inc(acc_ready, 1)
            taken(pe, sb_v, 0, sb_v.nslab * (NT + 1) - 1)
            taken(pe, sb_v, 0, sb_v.nslab * (NT + 1) - 2)
            pe.wait_ge(h_done, 1 + 2 * HEADS)

            def sb_turn(i, par, more):
                n = i * 2 + par
                zs = sbz[:, par, :]
                if more:
                    sb_logits(pe, i, par + 1)
                pe.wait_ge(sb_n, n + 1)
                pe.wait_ge(sb_lw, n + 1)
                later = {0: (1, 3, 2), 4: (0, 1, 3, 2), 1: (3, 2), 3: (2,), 2: ()}
                for t, after in later.items():
                    c, q0, k0, m = SB[t]
                    dst = sb_bank(4, t)
                    mm = pe.matmul(dst, tril[0:m, 0:m], sb_keys(sbn, t), start=True, stop=not after)
                    for a in after:
                        qa = SB[a][1]
                        mm = pe.matmul(dst[:, qa - q0:], ones[:, 0:m], sb_keys(sbn, a), start=False, stop=a == after[-1])
                mm.then_inc(sb_c, 1)
                pe.wait_ge(sb_w, n + 1)
                pe.wait_ge(sb_v_in, n * 2 + 2)
                if more:
                    pe.wait_ge(sb_zs, n + 4)
                for a, t in enumerate((0, 4, 1, 3, 2)):
                    c, q0, k0, m = SB[t]
                    mm = pe.matmul(ps[:, 0, q0:SEQ], sbv[0:m, SB_V[t], :], sb_keys(zs, t), start=a == 0, stop=a == 4)
                mm.then_inc(sb_o, 1)

            sb_logits(pe, 0, 0)
            with pe.Fori(0, HEADS // 2 - 1) as i:
                sb_turn(i, 0, True)
                sb_turn(i, 1, True)
            sb_turn(HEADS // 2 - 1, 0, True)
            sb_turn(HEADS // 2 - 1, 1, False)
            pe.wait_ge(sb_oc, 2 + HEADS)
            x_hn = lambda k: HN[:, k, META:T]
            pe_gemm(pe, gate_dn, x_hn)
            pe_gemm(pe, branch_dn, lambda k: VO[:, :, k // 2, k % 2 * P:(k % 2 + 1) * P])
            pe_gemm(pe, gate_sb, x_hn)
            pe_gemm(pe, branch_sb, lambda k: QSK[:, k, 0:SEQ])
            pe.wait_ge(merged, KD)
            pe_gemm(pe, mix_out, lambda k: MG[:, k, :])
            norm_pe(pe, 1, SEQ)
            pe.wait_ge(n_out, 2 * KD)
            pe_gemm(pe, ffn_in, lambda k: HN[:, k, 0:SEQ])
            taken(pe, ffn_in, 0, 2 * KF - 1)
            pe_gemm_pair(pe, ffn_out, lambda k: ACTF[:, k, :])

            taken(pe, ffn_out, 1, R - 1)
            taken(pe, ffn_out, 1, R - 2)
            pe.wait_ge(silu_c, 1)
            for l in range(2):
                for i, slabs in groups(pe, ada[l]):
                    for r in slabs:
                        pe.wait_ge(slot_full[ada[l].slot(r)], i * 16 + ada[l].full(r))
                        for m in range(2):
                            for k in range(KD):
                                mm = pe.matmul(ps[:, 4 + l, ds(i * (2 * R) + (2 * r + m), 1)], ada[l].view(r)[:, k, m * P:(m + 1) * P],
                                               csil[:, k:k + 1], start=k == 0, stop=k == KD - 1)
                            mm.then_inc(acc_ready, 1)
            norm_pe(pe, 2, SEQ)
            pe.wait_ge(n_out, 3 * KD)
            pe.wait_ge(mod_done, 1)
            x_hn = lambda k: HN[:, k, 0:SEQ]

            def qk_sum(t):
                pe.wait_ge(h_sq, 2 * HEADS + t + 1)
                pe.wait_ge(h_rs, 2 * HEADS + t + 1)
                pe.matmul(ps[:, 6, :], pair_ones, NSQ[:, t % 2, 0:SEQ], start=True, stop=True).then_inc(h_sum, 1)

            def qk_rot(t):
                pe.wait_ge(a_nrm, t + 1)
                if t:
                    pe.wait_ge(a_done, t)
                pe.matmul(ps[:, 7, :], rot, QG[:, t, :], start=True, stop=True).then_inc(a_rot, 1)

            for t in range(10):
                pe_tile(pe, gq_qk, t // (2 * R), t // 2 % R, t % 2, x_hn, False)
                if t >= 1:
                    qk_sum(t - 1)
                if t >= 2:
                    qk_rot(t - 2)
            qk_sum(9)
            qk_rot(8)
            pe.wait_ge(slot_full[gq_v.slot(0)], gq_v.full(0))
            for n in range(NT):
                b = gq_v.buf(n)
                pe.wait_ge(acc_free[b], gq_v.free(n))
                for k in range(KD):
                    mm = pe.matmul(ps[:, 2 * b, 0:256], HN[:, k, n * P:(n + 1) * P], gq_v.view(0)[:, k, :],
                                   start=k == 0, stop=k == KD - 1)
                mm.then_inc(acc_ready, 1)
            qk_rot(9)
            for g in range(KVH):
                pe.wait_ge(a_done, 9 + g // 2)
                if g >= 2:
                    pe.wait_ge(a_dupc, g - 1)
                pe.matmul(ps[:, 4 + g % 2, :], (dup0, dup1)[g % 2], QG[:, 8 + g // 2, :], start=True, stop=True).then_inc(a_dup, 1)
            pe.wait_ge(a_dupc, KVH)
            taken(pe, gq_v, 0, NT - 1)
            taken(pe, gq_v, 0, NT - 2)

            def scores(g, j):
                n = g * 4 + j
                pe.wait_ge(a_qk, g * 2 + 2)
                pe.wait_ge(a_e, n + 1)
                x = slice(j % 2 * HD, (j % 2 + 1) * HD)
                for q in range(NT):
                    mm = pe.matmul(ps[:, q, :], qst[x, j // 2, q * P:(q + 1) * P], kst[x, :], start=True, stop=True)
                mm.then_inc(a_s, 1)

            def gq_turn(g, more):
                for j in range(4):
                    n = g * 4 + j
                    if j < 3:
                        scores(g, j + 1)
                    elif more:
                        scores(g + 1, 0)
                    pe.wait_ge(a_p, n + 1)
                    for q in range(NT):
                        pe.wait_ge(a_tc, n * NT + q + 1)
                        for kt in range(NT):
                            mm = pe.transpose(ps[:, 4 + q % 2, kt * P:(kt + 1) * P], PB[:, j % 2, q, kt * P:(kt + 1) * P], ident)
                        mm.then_inc(a_t, 1)
                    pe.wait_ge(a_tc, n * NT + NT + 2)
                    pe.wait_ge(a_v, g + 1)
                    pe.wait_ge(a_oc, g * 2 + j // 2 + 1)
                    x = slice(j % 2 * HD, (j % 2 + 1) * HD)
                    for kt in range(NT):
                        mm = pe.matmul(ps[x, 6 + j // 2, :], vst[:, kt, :], PTB[:, j % 2, kt, :], start=kt == 0, stop=kt == NT - 1)
                    mm.then_inc(a_o, 1)

            scores(0, 0)
            with pe.Fori(0, KVH - 1) as g:
                gq_turn(g, True)
            gq_turn(KVH - 1, False)
            pe.wait_ge(a_e, 1 + QH)
            pe.wait_ge(a_oc, 2 + QH // 2)
            pe_gemm(pe, gq_out, lambda k: OG[:, k, :])

            def pe_conv_ffn(l, u):
                norm_pe(pe, u, SEQ)
                pe.wait_ge(n_out, (u + 1) * KD)
                pe_gemm(pe, fc_in[l], x_hn)
                taken(pe, fc_in[l], 0, 2 * KF - 1)
                pe_gemm_pair(pe, fc_out[l], lambda k: ACTF[:, k, :])

            pe_conv_ffn(0, 3)
            norm_pe(pe, 4, SEQ)
            pe.wait_ge(n_out, 5 * KD)
            pe_gemm(pe, hy_in, x_hn)
            pe.wait_ge(y_in, 48)
            pe.matmul(ps[0:FW, 6, :], W1[:, :], POS[:, :], start=True, stop=True).then_inc(y_mlp, 1)
            pe.wait_ge(y_sin, 1)
            pe.matmul(ps[0:FW, 7, :], W2[:, :], A1[:, 0, :], start=True, stop=True).then_inc(y_mlp, 1)
            pe.wait_ge(y_sin, 2)
            taken(pe, hy_in, 2, 2 * R - 1)
            taken(pe, hy_in, 2, 2 * R - 2)
            pe.wait_ge(y_conv, 3 * KD)
            for r in range(4):
                pe.wait_ge(slot_full[dft.slot(r)], dft.full(r))
            table = [dft.view(r) for r in range(4)]
            with pe.Fori(0, ORDERS) as o:
                for dh in range(2):
                    u = o * 2 + dh
                    pe.wait_ge(y_w, u * 32 + 32)
                    pe.wait_ge(y_z, u * NT + 1)

                    def sums(t):
                        pe.wait_ge(y_ab, u * NT + t + 1)
                        for c in range(NT):
                            for s in range(2):
                                mm = pe.matmul(ps[:, 4, c:c + 1], AB[:, s, c * P:(c + 1) * P], ones[:, 0:1],
                                               start=t + c + s == 0, stop=t == NT - 1 and c == NT - 1 and s == 1,
                                               skip_group_check=True)
                        mm.then_inc(y_n, 1)

                    for t in range(NT):
                        if t >= 2:
                            pe.wait_ge(y_pm, u * NT + t + 1)
                        for s in range(2):
                            mm = pe.matmul(ps[:, t % 2 * 2 + s, :], A1[:, 1, t * P:(t + 1) * P], W3[:, s, :], start=True, stop=True)
                        mm.then_inc(y_f, 1)
                        if t:
                            sums(t - 1)
                    sums(NT - 1)
                    for t in range(NT):
                        if t >= 2:
                            pe.wait_ge(y_tc, u * NT + t - 1)
                        for c in range(NT):
                            mm = pe.transpose(ps[:, 5 + t % 2, c * P:(c + 1) * P], U[:, dh * NT + c, t * P:(t + 1) * P], ident)
                        mm.then_inc(y_t, 1)
                    pe.wait_ge(y_pm, u * NT + NT + 2)
                    pe.wait_ge(y_rn, u + 1)
                    pe.wait_ge(y_tc, u * NT + NT)
                    for f in range(NT):
                        b = f % 2 * 4
                        if f >= 2:
                            pe.wait_ge(y_y, u * NT + f - 1)
                        for s in range(2):
                            for t in range(NT):
                                pe.matmul(ps[:, b + s, :], table[s][:, t, f * P:(f + 1) * P], PM[:, s, t, :],
                                          start=t == 0, stop=t == NT - 1)
                        for s in range(2):
                            for t in range(NT):
                                mm = pe.matmul(ps[:, b + 2 + s, :], table[s][:, t, f * P:(f + 1) * P], ZK[:, t, :],
                                               start=t == 0, stop=t == NT - 1)
                        mm.then_inc(y_dft, 1)
                    pe.wait_ge(y_y, u * NT + NT)
                    for c in range(NT):
                        if c >= 2:
                            pe.wait_ge(y_z, u * NT + c)
                        for s in range(2):
                            for f in range(NT):
                                mm = pe.matmul(ps[:, c % 2, :], YF[:, s, f, c * P:(c + 1) * P], table[2 + s][:, f, :],
                                               start=s + f == 0, stop=s == 1 and f == NT - 1)
                        mm.then_inc(y_inv, 1)
            pe.wait_ge(y_z, 1 + 4 * NT)
            pe.transpose(ps[:, 7, 0:P], ident, ident).then_inc(acc_ready, 4)
            pe_gemm(pe, hy_out, lambda k: U[:, k, :])
            pe_conv_ffn(1, 5)
            norm_pe(pe, 6, SEQ)
            for n in range(NT):
                for h in range(2):
                    pe.wait_ge(n_out, 6 * KD + (KD if n else 4 * (h + 1)))
                    if n >= 1:
                        pe.wait_ge(f_out, 2 * n + h - 1)
                    for k in range(4):
                        mm = pe.transpose(ps[:, 4 + h, k * P:(k + 1) * P], HN[:, 4 * h + k, n * P:(n + 1) * P], ident)
                    mm.then_inc(f_t, 1)

        @block.scalar
        def _(act):
            act.sem_inc(silu_done, 2)
            act.sem_inc(l2_rs, 1)
            act.sem_inc(o_rs, 1)
            act.sem_inc(h_rs, 1)
            act.sem_inc(sb_zs, 2)
            act.sem_inc(sb_oc, 2)
            act.sem_inc(a_e, 1)
            act.sem_inc(a_tc, 2)
            act.sem_inc(a_oc, 2)
            for g in range(2):
                act.sem_inc(chunk[g]["oc"], 1)
            act.wait_ge(t_done, 2 * KD + 1)
            act.wait_ge(cleared, 1)
            norm_act(act, 0, lambda k: H[:, k, :], T)
            act.wait_ge(ab_x, 1)
            act.activation(soft[:, 1, :, 0:8], soft[:, 1, :, 0:8], ACT.Exp, bias=zero, scale=-1.0)
            act.drain()
            act.activation(soft[:, 1, :, 0:8], soft[:, 1, :, 0:8], ACT.Ln, bias=ones[:, 0:1], scale=1.0)
            act.activation(ab[:, 0:8], ab[:, 0:8], ACT.Exp, bias=zero, scale=1.0)
            act.activation(b_tok[:, :, :], soft[:, 0, :, 8:16], ACT.Sigmoid, bias=zero, scale=1.0).then_inc(ab_l, 1)

            def conv_in(gm, i, t):
                b = acc_in(act, gm, i, t)
                act.activation(split(xpad[:, t % 2, 3:3 + T]), half(2 * b), ACT.Copy).then_inc(acc_free[b], 1)

            for i, slabs in groups(act, dn_qk):
                for t in range(2 * R):
                    conv_in(dn_qk, i, t)
                    act.wait_ge(conv_done, i * (2 * R) + t + 1)
                    act.activation(QK[:, ds(i * (2 * R) + t, 1), :], cv[:, t % 2:t % 2 + 1, :], ACT.Silu)\
                        .then_inc(silu_done, 1)
            for i, slabs in groups(act, dn_v):
                for t in range(2 * R):
                    n = i * (2 * R) + t
                    act.wait_ge(silu_done, 2 + 16)
                    act.wait_ge(l2_sum, n + 1)
                    act.activation(NSQ[:, t % 2:t % 2 + 1, :], QK[:, ds(n, 1), :], ACT.Square).then_inc(l2_sq, 1)
                    conv_in(dn_v, i, t)
                    act.wait_ge(conv_done, n + 17)
                    act.activation(cv[:, t % 2, :], cv[:, t % 2, :], ACT.Silu).then_inc(silu_done, 1)
                    act.wait_ge(l2_sum, n + 3)
                    act.wait_ge(l2_done, n + 1)
                    act.activation(split(RSB[:, :]), half(4), ACT.Ln, bias=eps, scale=1.0)
                    act.drain()
                    act.activation(RSB[:, :], RSB[:, :], ACT.Exp, bias=zero, scale=-0.5).then_inc(l2_rs, 1)

            act.wait_ge(m_dve, 3)
            act.activation(ml[:, :, :], ml[:, :, :], ACT.Exp, bias=zero[0:META], scale=1.0)
            act.activation(msm[:, 1, :], msm[:, 1, :], ACT.Exp, bias=zero[0:META], scale=1.0).then_inc(m_act, 1)
            with act.Fori(0, NT) as c:
                for g in range(2):
                    G, E, b = group[g], chunk[g], 4 * g
                    act.wait_ge(E["expin"], c + 1)
                    act.activation(G["dt"][:, :, :], G["dt"][:, :, :], ACT.Exp, bias=zero, scale=1.0)
                    act.activation(G["lp"][:, 0, :, :], G["lp"][:, 0, :, :], ACT.Exp, bias=zero, scale=1.0)
                    act.activation(G["x"][:, :, :], ps[:, b, :].rearrange("p (h n) -> p h n", h=G4), ACT.Exp, bias=zero, scale=1.0)
                    act.activation(G["sm"][:, 2:4, :], G["sm"][:, 0:2, :], ACT.Exp, bias=zero, scale=1.0).then_inc(E["expd"], 1)
                for l in range(1, LEVELS):
                    for g in range(2):
                        G, E, b = group[g], chunk[g], 4 * g
                        act.wait_ge(E["prod"], c * LEVELS + l + 1)
                        act.activation(G["lp"][:, 1, :, :], ps[:, b, :].rearrange("p (h n) -> p h n", h=G4), ACT.Copy)\
                            .then_inc(E["pcopy"], 1)
                for g in range(2):
                    G, E, b = group[g], chunk[g], 4 * g
                    act.wait_ge(E["wt"], c + 1)
                    act.activation(G["x"][:, :, :], ps[:, b, :].rearrange("p (h n) -> p h n", h=G4), ACT.Copy, scale=-1.0)\
                        .then_inc(E["nw"], 1)
                for g in range(2):
                    G, E, b = group[g], chunk[g], 4 * g
                    act.wait_ge(E["vn"], c + 1)
                    act.activation(G["lp"][:, :, :, :].rearrange("p a h n -> p a (h n)"), ps[:, b + 2:b + 4, :], ACT.Copy)\
                        .then_inc(E["vnc"], 1)
                for g in range(2):
                    G, E, b = group[g], chunk[g], 4 * g
                    act.wait_ge(E["o"], c + 1)
                    act.activation(VO[:, ds(c, 1), g * G4:(g + 1) * G4, :].rearrange("p c h n -> p (c h n)"),
                                   ps[:, b:b + 2, :].rearrange("p a n -> p (a n)"), ACT.Copy).then_inc(E["oc"], 1)

            act.drain()
            for i, slabs in groups(act, dn_z):
                for t in range(2 * R):
                    n = i * R + t // 2
                    if t % 2 == 0:
                        if t:
                            act.wait_ge(o_sum, n)
                        act.activation(NSQ[:, :, 0:SEQ].rearrange("p e (c n) -> p e c n", n=P),
                                       VO[:, :, ds(n, 1), :].rearrange("p c a (e n) -> p e (c a) n", e=2), ACT.Square)\
                            .then_inc(o_sq, 1)
                    act.wait_ge(z_done, i * (2 * R) + t + 1)
                    b = acc_in(act, dn_z, i, t)
                    act.activation(ZT[:, t % 2, :], ps[:, 2 * b, :], ACT.Silu).then_inc(acc_free[b], 1)
                    if t % 2 == 0:
                        act.wait_ge(o_sum, n + 1)
                        act.wait_ge(z_done, n * 2 + 2)
                        act.activation(NRS[:, 0:SEQ], ps[:, 6, :], ACT.Ln, bias=eps, scale=1.0 / DV)
                        act.drain()
                        act.activation(NRS[:, 0:SEQ], NRS[:, 0:SEQ], ACT.Exp, bias=zero, scale=-0.5).then_inc(o_rs, 1)

            def head_rs(i, t, scale):
                n = i * (2 * R) + t
                act.wait_ge(h_sum, n + 3)
                act.wait_ge(h_done, n + 1)
                act.activation(split(NRS[:, :]), half(6), ACT.Ln, bias=eps, scale=scale)
                act.drain()
                act.activation(NRS[:, :], NRS[:, :], ACT.Exp, bias=zero, scale=-0.5).then_inc(h_rs, 1)

            act.wait_ge(z_done, 2 + 2 * HEADS)
            for i, slabs in groups(act, sb_qk):
                for t in range(2 * R):
                    n = i * (2 * R) + t
                    act.wait_ge(h_sum, n + 1)
                    b = acc_in(act, sb_qk, i, t)
                    act.activation(split(NSQ[:, t % 2, :]), half(2 * b), ACT.Square).then_inc(h_sq, 1)
                    act.activation(split(QSK[:, ds(n, 1), :].rearrange("p a n -> p (a n)")), half(2 * b), ACT.Copy)\
                        .then_inc(acc_free[b], 1)
                    if t:
                        head_rs(i, t - 1, 1.0 / P)
                head_rs(i, 2 * R - 1, 1.0 / P)

            def sb_evac(n, par):
                act.wait_ge(sb_z, n + 1)
                if not isinstance(n, int) or n:
                    act.wait_ge(sb_o, n)
                s = float(P) ** -0.5
                act.activation(sbz[:, par, 0:8 * P].rearrange("p (a n) -> p a n", a=2), ps[:, 0:2, :], ACT.Copy, scale=s)
                act.activation(sbz[:, par, 8 * P:SBX], ps[:, 2, 0:2 * P], ACT.Copy, scale=s)
                act.activation(sbz[0:META, par, SBX:SBW], ps[0:META, 3, :], ACT.Copy, scale=s).then_inc(sb_zs, 1)

            def sb_log(n):
                act.wait_ge(sb_abs, n + 1)
                act.activation(sbe[:, :], sbe[:, :], ACT.Exp, bias=zero, scale=-1.0)
                act.drain()
                act.activation(sbe[:, :], sbe[:, :], ACT.Ln, bias=ones[:, 0:1], scale=1.0).then_inc(sb_ln, 1)

            def sb_turn(i, par, more):
                n = i * 2 + par
                if more:
                    sb_evac(n + 1, 1 - par)
                    sb_log(n + 1)
                act.wait_ge(sb_lw, n + 2)
                act.activation(sbz[:, par, 0:SBX], sbz[:, par, 0:SBX], ACT.Exp, bias=zero, scale=1.0)
                act.activation(sbz[0:META, par, SBX:SBW], sbz[0:META, par, SBX:SBW], ACT.Exp, bias=zero[0:META], scale=1.0)\
                    .then_inc(sb_w, 1)
                act.wait_ge(sb_o, n + 2)
                act.activation(QSK[:, ds(n, 1), 0:SEQ].rearrange("p a n -> p (a n)"), ps[:, 0, :], ACT.Copy).then_inc(sb_oc, 1)

            act.wait_ge(sv_done, 4 * (NT + 1) + 1)
            sb_evac(0, 0)
            sb_log(0)
            with act.Fori(0, HEADS // 2 - 1) as i:
                sb_turn(i, 0, True)
                sb_turn(i, 1, True)
            sb_turn(HEADS // 2 - 1, 0, True)
            sb_turn(HEADS // 2 - 1, 1, False)
            for t in range(KD):
                b = acc_in(act, gate_dn, 0, t)
                act.activation(GT[:, t, :], ps[:, 2 * b, :], ACT.Sigmoid).then_inc(acc_free[b], 1)
            for t in range(KD):
                taken(act, branch_dn, t // R, t % R)
                b = acc_in(act, gate_sb, 0, t)
                act.activation(GT[:, t, :], ps[:, 2 * b, :], ACT.Sigmoid).then_inc(acc_free[b], 1)
            for t in range(KD):
                taken(act, mix_out, 0, t)
            norm_act(act, 1, lambda k: H[:, k, META:T], SEQ)
            for i, slabs in groups(act, ffn_in):
                for r in slabs:
                    taken(act, ffn_in, i, 2 * r - 3)
                    b = acc_in(act, ffn_in, i, 2 * r)
                    act.activation(SG[:, r % 2, :], ps[:, 2 * b, :], ACT.Silu).then_inc(acc_free[b], 1)

            act.activation(csil[:, :], cols("c", 0, KD), ACT.Silu).then_inc(silu_c, 1)

            def residual(gm, i):
                for t in range(R):
                    taken(act, gm, i, t)

            residual(ffn_out, 1)
            norm_act(act, 2, lambda k: H[:, k, META:T], SEQ)

            def qk_rs(t):
                act.wait_ge(h_sum, 2 + 2 * HEADS + t + 1)
                act.wait_ge(h_done, 1 + 2 * HEADS + t)
                act.activation(NRS[:, 0:SEQ], ps[:, 6, :], ACT.Ln, bias=eps, scale=1.0 / HD)
                act.drain()
                act.activation(NRS[:, 0:SEQ], NRS[:, 0:SEQ], ACT.Exp, bias=zero, scale=-0.5).then_inc(h_rs, 1)

            act.wait_ge(n_out, 3 * KD)
            for t in range(10):
                i, tt = t // (2 * R), t % (2 * R)
                act.wait_ge(h_sum, 2 * HEADS + t + 1)
                b = acc_in(act, gq_qk, i, tt)
                act.activation(NSQ[:, t % 2, 0:SEQ], ps[:, 2 * b, :], ACT.Square).then_inc(h_sq, 1)
                act.activation(QG[:, t, :], ps[:, 2 * b, :], ACT.Copy).then_inc(acc_free[b], 1)
                if t:
                    qk_rs(t - 1)
            qk_rs(9)
            for g in range(KVH):
                act.wait_ge(a_dup, g + 1)
                act.activation(KDUP[:, g, :], ps[:, 4 + g % 2, :], ACT.Copy).then_inc(a_dupc, 1)

            def exps(g, j):
                n = g * 4 + j
                act.wait_ge(a_mx, n + 1)
                act.wait_ge(a_t, n * NT + 1)
                for q in range(NT):
                    ins = act.activation(PB[:, j % 2, q, :], ps[:, q, :], ACT.Exp, bias=asm[:, j % 2, 1, q:q + 1],
                                         scale=float(HD) ** -0.5, accum_out=asm[:, j % 2, 2, q:q + 1])
                ins.then_inc(a_e, 1)

            def gq_turn(g, more):
                for j in range(4):
                    n = g * 4 + j
                    if j < 3:
                        exps(g, j + 1)
                    elif more:
                        exps(g + 1, 0)
                    act.wait_ge(a_o, n + 1)
                    for q in range(NT):
                        act.wait_ge(a_t, n * NT + q + 6)
                        act.activation(PTB[:, j % 2, :, q * P:(q + 1) * P], ps[:, 4 + q % 2, :].rearrange("p (k n) -> p k n", k=NT),
                                       ACT.Copy).then_inc(a_tc, 1)
                    if j % 2:
                        act.wait_ge(a_o, n + 3)
                        act.activation(OG[:, ds(g * 2 + j // 2, 1), :].rearrange("p a n -> p (a n)"), ps[:, 6 + j // 2, :], ACT.Copy)\
                            .then_inc(a_oc, 1)

            exps(0, 0)
            with act.Fori(0, KVH - 1) as g:
                gq_turn(g, True)
            gq_turn(KVH - 1, False)

            def act_conv_ffn(l, u):
                for t in range(KD):
                    taken(act, (gq_out, hy_out)[l], 0, t)
                norm_act(act, u, lambda k: H[:, k, META:T], SEQ)
                act.wait_ge(n_out, (u + 1) * KD)
                for i, slabs in groups(act, fc_in[l]):
                    for r in slabs:
                        b = acc_in(act, fc_in[l], i, 2 * r)
                        act.activation(GP[:, r % 2, 1:SEQ + 1], ps[:, 2 * b, :], ACT.Copy).then_inc(acc_free[b], 1)
                        act.wait_ge(fc_conv, i * R + (l * KF + r + 1))
                        act.activation(SG[:, r % 2, :], SG[:, r % 2, :], ACT.Silu).then_inc(fc_silu, 1)

            act_conv_ffn(0, 3)
            residual(fc_out[0], 1)
            norm_act(act, 4, lambda k: H[:, k, META:T], SEQ)
            act.wait_ge(n_out, 5 * KD)
            for i, slabs in groups(act, hy_in):
                for t in range(2 * R):
                    if t >= 2:
                        act.wait_ge(y_conv, i * (2 * R) + (t - 1))
                    b = acc_in(act, hy_in, i, t)
                    act.activation(UP[:, t % 2, 1:SEQ + 1], ps[:, 2 * b, :], ACT.Copy).then_inc(acc_free[b], 1)
                act.wait_ge(y_conv, i * (2 * R) + 2 * R)
            for n in range(2):
                act.wait_ge(y_arg, n + 1)
                act.activation(A1[:, n, :], A1[:, n, :], ACT.Sin, bias=zero[0:FW], scale=1.0).then_inc(y_sin, 1)
            with act.Fori(0, ORDERS) as o:
                for dh in range(2):
                    u = o * 2 + dh
                    for t in range(NT):
                        act.wait_ge(y_fb, u * NT + t + 1)
                        if t:
                            act.wait_ge(y_n, u * NT + t)
                        act.activation(AB[:, :, :], FB[:, :, :], ACT.Abs).then_inc(y_ab, 1)
                    for t in range(NT):
                        act.wait_ge(y_t, u * NT + t + 1)
                        act.activation(ZK[:, t, :], ps[:, 5 + t % 2, :], ACT.Copy).then_inc(y_tc, 1)
                    for f in range(NT):
                        b = f % 2 * 4
                        act.wait_ge(y_dft, u * NT + f + 1)
                        if f >= 2:
                            act.wait_ge(y_y, u * NT + f - 1)
                        act.activation(KS[:, f % 2, :, :], ps[:, b:b + 2, :], ACT.Copy).then_inc(y_kc, 1)
            act_conv_ffn(1, 5)
            residual(fc_out[1], 1)
            norm_act(act, 6, lambda k: H[:, k, META:T], SEQ)
            for n in range(NT):
                act.wait_ge(f_out, 2 * n + 2)
                act.dma_start(out[n * P:(n + 1) * P, :], OUT[:, n, :]).then_inc(stored, 16)
            act.wait_ge(stored, 16 * NT)

        @block.vector
        def _(dve):
            for b in range(2):
                dve.sem_inc(acc_free[b], 1)
            dve.sem_inc(vt_done, 2)
            dve.sem_inc(l2_done, 1)
            dve.sem_inc(z_done, 2)
            dve.sem_inc(h_done, 1)
            dve.sem_inc(sb_lw, 1)
            dve.sem_inc(y_pm, 2)
            dve.sem_inc(y_z, 1)
            for k in range(KD):
                dve.wait_ge(t_ready, 2 * k + 1)
                dve.tensor_copy(H[:, k, META:T], ps[:, k % 2, :]).then_inc(t_done, 1)
                dve.wait_ge(t_ready, 2 * k + 2)
                dve.tensor_copy(H[:, k, 0:META], ps[:, 2 + k % 2, 0:META]).then_inc(t_done, 1)
            dve.wait_ge(t_ready, 2 * KD + 1)
            dve.tensor_copy(pcol[:, :, :].rearrange("p a b -> p (a b)"),
                            ps[:, 4:6, :].rearrange("p a b -> p (a b)")[:, 0:PT * P]).then_inc(t_done, 1)
            dve.memset(soft[:, :, :, :], 0.0)
            dve.drain()
            norm_dve(dve, 0, lambda k: H[:, k, :], lambda k: col("norm_mix", k), T, lambda k: HN[:, k, :])
            dve.wait_ge(ab_ready, 1)
            dve.tensor_copy(soft[:, 0, 0:NT, :], ps[:, 4, 0:NT * 16].rearrange("p (n c) -> p n c", c=16))
            dve.tensor_copy(soft[0:META, 0, NT, :], ps[0:META, 4, NT * 16:(NT + 1) * 16])
            dve.tensor_copy(ab[:, :], ps[:, 5, 0:16])
            dve.drain()
            dve.tensor_tensor(soft[:, 0, :, 0:8], soft[:, 0, :, 0:8], heads_of(ab[:, 8:16], NT + 1), ALU.add)
            dve.drain()
            dve.scalar_tensor_tensor(soft[:, 1, :, 0:8], soft[:, 0, :, 0:8], -1.0, soft[:, 0, :, 0:8], ALU.mult, ALU.max)\
                .then_inc(ab_x, 1)
            dve.wait_ge(ab_l, 1)
            dve.scalar_tensor_tensor(soft[:, 0, :, 0:8], soft[:, 0, :, 0:8], 0.0, soft[:, 1, :, 0:8], ALU.max, ALU.add)
            dve.drain()
            dve.scalar_tensor_tensor(g_tok[:, :, :], soft[:, 0, :, 0:8], -1.0, heads_of(ab[:, 0:8], NT + 1), ALU.mult, ALU.mult)

            def conv(gm, i, t, taps):
                taken(dve, gm, i, t)
                x, y = xpad[:, t % 2, :], cv[:, t % 2, :]
                dve.tensor_scalar(y, x[:, 0:T], taps(0), None, ALU.mult)
                for j in range(1, 4):
                    dve.drain()
                    ins = dve.scalar_tensor_tensor(y, x[:, j:j + T], taps(j), y, ALU.mult, ALU.add)
                ins.then_inc(conv_done, 1)

            for i, slabs in groups(dve, dn_qk):
                for t in range(2 * R):
                    dve.wait_ge(silu_done, i * (2 * R) + t + 1)
                    conv(dn_qk, i, t, lambda j: dcol("conv_q", i * 32 + (j * 8 + t)))

            def v_out(i, t):
                n = i * (2 * R) + t
                dve.wait_ge(vt_ready, n * 2 + 4 + 1)
                dve.tensor_copy(VO[:, :, :, :].rearrange("p c h (e n) -> p c (h e) n", e=2)[:, :, ds(n, 1), :],
                                ps[:, 6, :].rearrange("p (c a n) -> p c a n", c=NT, a=1)).then_inc(vt_done, 1)
                dve.wait_ge(vt_ready, n * 2 + 4 + 2)
                dve.tensor_copy(vm[:, :, :].rearrange("p h (e n) -> p (h e) n", e=2)[:, ds(n, 1), :],
                                ps[0:META, 7, 0:P].unsqueeze(1)).then_inc(vt_done, 1)

            for i, slabs in groups(dve, dn_v):
                for t in range(2 * R):
                    n = i * (2 * R) + t
                    dve.wait_ge(silu_done, n + 16 + 1)
                    dve.wait_ge(vt_ready, n * 2 + 2)
                    conv(dn_v, i, t, lambda j: dcol("conv_v", i * 8 + (j * 16 + t)))
                    dve.wait_ge(l2_rs, n + 2)
                    dve.tensor_tensor(QK[:, ds(n, 1), :], QK[:, ds(n, 1), :], RSB[:, :].unsqueeze(1), ALU.mult)\
                        .then_inc(l2_done, 1)
                    if t:
                        v_out(i, t - 1)
                v_out(i, 2 * R - 1)

            m = META
            dve.drain()
            dve.tensor_copy(gmb[:, :, :], wide(g_tok[0:m, NT, :], m)).then_inc(m_dve, 1)
            dve.wait_ge(m_pe, 1)
            dve.wait_ge(mask_in, 16)
            dve.tensor_copy(msm[:, 0, :], ps[0:m, 1, 0:HEADS])
            dve.drain()
            h16 = lambda b: ps[0:m, b, 0:HEADS * m].rearrange("p (h n) -> p h n", h=HEADS)
            dve.tensor_tensor(ml[:, :, :], wide(msm[:, 0, :], m), h16(0), ALU.subtract)
            dve.tensor_tensor(msm[:, 1, :], h16(0)[:, :, m - 1], msm[:, 0, :], ALU.subtract).then_inc(m_dve, 1)
            dve.drain()
            dve.tensor_tensor(ml[:, :, :], ml[:, :, :], heads_of(masks[0:m, 1, 0:m], HEADS), ALU.add).then_inc(m_dve, 1)
            dve.wait_ge(m_act, 1)
            dve.tensor_tensor(ml[:, :, :], ml[:, :, :], wide(b_tok[0:m, NT, :], m), ALU.mult)
            dve.drain()
            dve.tensor_tensor(ml[:, :, :], ml[:, :, :], h16(2), ALU.mult)
            dve.drain()
            for l in range(4):
                dve.tensor_tensor(mlm[:, :, :], ml[:, :, :], heads_of(masks[0:m, 2 + l, 0:m], HEADS), ALU.mult)\
                    .then_inc(m_dve, 1)
                dve.wait_ge(m_pe, 2 * l + 2 - (1 if l else 0))
                if l == 0:
                    idn = heads_of(ident[0:m, 0:m], HEADS)
                    dve.tensor_tensor(mx[:, :, :], idn, mlm[:, :, :], ALU.subtract).then_inc(m_dve, 1)
                    dve.tensor_tensor(my[:, :, :], idn, h16(0), ALU.subtract).then_inc(m_dve, 1)
                else:
                    dve.tensor_copy(mp[:, :, :], h16(0)).then_inc(m_dve, 1)
                    dve.wait_ge(m_pe, 2 * l + 2)
                    dve.tensor_tensor(my[:, :, :], my[:, :, :], h16(1), ALU.subtract)
                    dve.tensor_tensor(mx[:, :, :], mx[:, :, :], h16(2), ALU.subtract).then_inc(m_dve, 1)
                dve.drain()
            kt = lambda: ps[0:m, 3:5, :].rearrange("p a (h n) -> p (a h) n", n=P)
            dve.tensor_tensor(km[:, :, :], kt(), wide(msm[:, 1, :]), ALU.mult)
            dve.tensor_tensor(vmb[:, :, :], vm[:, :, :], wide(b_tok[0:m, NT, :], DV), ALU.mult).then_inc(m_dve, 1)
            dve.wait_ge(m_pe, 9)
            dve.tensor_copy(vm[:, :, :], ps[0:m, 4:8, :].rearrange("p a (h n) -> p (a h) n", n=DV)).then_inc(m_dve, 1)
            dve.wait_ge(m_pe, 10)
            dve.tensor_copy(S[:, :, :], ps[:, 0:4, :].rearrange("p a (h n) -> p (a h) n", n=DV)).then_inc(m_dve, 1)
            dve.drain()
            for g in range(2):
                dve.sem_inc(chunk[g]["state"], 1)
            with dve.Fori(0, NT) as c:
                for g in range(2):
                    G, E, b = group[g], chunk[g], 4 * g
                    hs = slice(g * G4, (g + 1) * G4)
                    dve.tensor_copy(G["k"][:, :, :], KC[:, hs, ds(c * P + META, P)])
                    dve.tensor_scalar(G["q"][:, :, :], QC[:, hs, ds(c * P + META, P)], float(P) ** -0.5, None, ALU.mult)
                    dve.tensor_copy(G["sm"][:, 6, :], b_tok[:, ds(c, 1), hs].rearrange("p c h -> p (c h)"))
                    dve.tensor_copy(G["sm"][:, 7, :], g_tok[:, ds(c, 1), hs].rearrange("p c h -> p (c h)"))
                    dve.drain()
                    dve.tensor_copy(G["gb"][:, :, :], wide(G["sm"][:, 7, :])).then_inc(E["staged"], 1)
                for g in range(2):
                    G, E, b = group[g], chunk[g], 4 * g
                    h4 = lambda bb: ps[:, bb, :].rearrange("p (h n) -> p h n", h=G4)
                    dve.wait_ge(E["gates"], c + 1)
                    dve.tensor_copy(G["sm"][:, 0, :], ps[:, b + 1, 0:G4])
                    dve.drain()
                    dve.tensor_tensor(G["dt"][:, :, :], h4(b), wide(G["sm"][:, 0, :]), ALU.subtract)
                    dve.tensor_tensor(G["sm"][:, 1, :], h4(b)[:, :, P - 1], G["sm"][:, 0, :], ALU.subtract)
                    dve.drain()
                    dve.tensor_tensor(G["lp"][:, 0, :, :], heads_of(masks[:, 1, :], G4), G["dt"][:, :, :], ALU.subtract)
                    dve.tensor_tensor(G["dt"][:, :, :], G["dt"][:, :, :], heads_of(masks[:, 0, :], G4), ALU.add)\
                        .then_inc(E["expin"], 1)
                for g in range(2):
                    G, E, b = group[g], chunk[g], 4 * g
                    h4 = lambda bb: ps[:, bb, :].rearrange("p (h n) -> p h n", h=G4)
                    dve.wait_ge(E["expd"], c + 1)
                    dve.tensor_tensor(G["lp"][:, 0, :, :], G["lp"][:, 0, :, :], wide(G["sm"][:, 6, :]), ALU.mult)
                    dve.tensor_tensor(G["dt"][:, :, :], G["dt"][:, :, :], h4(b + 3), ALU.mult)
                    dve.tensor_tensor(G["sm"][:, 4, :], G["sm"][:, 6, :], G["sm"][:, 2, :], ALU.mult)
                    dve.tensor_tensor(G["q"][:, :, :], G["q"][:, :, :], G["x"][:, :, :], ALU.mult)
                    dve.tensor_copy(G["sm"][:, 5, :], G["x"][:, :, P - 1])
                    dve.drain()
                    dve.tensor_tensor(G["lp"][:, 0, :, :], G["lp"][:, 0, :, :], h4(b + 2), ALU.mult).then_inc(E["lower"], 1)
                for l in range(LEVELS):
                    for g in range(2):
                        G, E, b = group[g], chunk[g], 4 * g
                        h4 = lambda bb: ps[:, bb, :].rearrange("p (h n) -> p h n", h=G4)
                        if l == 0:
                            dve.wait_ge(E["prod"], c * LEVELS + 1)
                            idn = heads_of(ident, G4)
                            dve.tensor_tensor(G["x"][:, :, :], idn, G["lm"][:, 0, :, :], ALU.subtract)
                            dve.tensor_tensor(G["y"][:, :, :], idn, h4(b), ALU.subtract).then_inc(E["inv"], 1)
                            dve.wait_ge(E["ktok"], c + 1)
                            dve.tensor_tensor(G["gb"][:, :, :], h4(b + 1), wide(G["sm"][:, 4, :]), ALU.mult)
                            dve.tensor_tensor(G["k"][:, :, :], h4(b + 1), wide(G["sm"][:, 3, :]), ALU.mult)\
                                .then_inc(E["kbg"], 1)
                        else:
                            dve.wait_ge(E["delta"], c * (LEVELS - 1) + l)
                            if l < LEVELS - 1:
                                dve.tensor_tensor(G["x"][:, :, :], G["x"][:, :, :], h4(b + 3), ALU.subtract)
                            dve.tensor_tensor(G["y"][:, :, :], G["y"][:, :, :], h4(b + 2), ALU.subtract).then_inc(E["inv"], 1)
                        if l == LEVELS - 1:
                            vb = G["lm"][:, :, :, :].rearrange("p a h n -> p (a h n)").rearrange("p (h n) -> p h n", h=G4)
                            vsrc = VO[:, ds(c, 1), g * G4:(g + 1) * G4, :].rearrange("p c h n -> p (c h) n")
                            dve.tensor_tensor(vb, vsrc, wide(G["sm"][:, 6, :], DV), ALU.mult).then_inc(E["vb"], 1)
                for g in range(2):
                    G, E, b = group[g], chunk[g], 4 * g
                    dve.wait_ge(E["sd"], c + 1)
                    for h in range(G4):
                        Sh = S[:, g * G4 + h, :]
                        ins = dve.scalar_tensor_tensor(Sh, Sh, G["sm"][:, 5, h:h + 1],
                                                       ps[:, b + 2 + h // 2, h % 2 * DV:(h % 2 + 1) * DV], ALU.mult, ALU.add)
                    ins.then_inc(E["state"], 1)

            for i, slabs in groups(dve, dn_z):
                for t in range(2 * R):
                    n = i * R + t // 2
                    e = t % 2
                    if e == 0:
                        dve.wait_ge(o_rs, n + 2)
                    taken(dve, dn_z, i, t)
                    dve.scalar_tensor_tensor(ZT[:, e, :], ZT[:, e, :], col("dn_gain", e), NRS[:, 0:SEQ], ALU.mult, ALU.mult)
                    dve.drain()
                    o = VO[:, :, ds(n, 1), e * P:(e + 1) * P].rearrange("p c a n -> p c (a n)")
                    dve.tensor_tensor(o, o, ZT[:, e, :].rearrange("p (c n) -> p c n", c=NT), ALU.mult).then_inc(z_done, 1)
            for i, slabs in groups(dve, sb_qk):
                for t in range(2 * R):
                    n = i * (2 * R) + t
                    dve.wait_ge(h_rs, n + 2)
                    qk = QSK[:, ds(n, 1), :]
                    dve.scalar_tensor_tensor(qk, qk, dcol("sbq", i) if not isinstance(i, int) else col("sbq", i),
                                             NRS[:, :].unsqueeze(1), ALU.mult, ALU.mult).then_inc(h_done, 1)
            for r in range(sb_v.nslab):
                for n in range(NT + 1):
                    m = P if n < NT else META
                    b = acc_in(dve, sb_v, 0, r * (NT + 1) + n)
                    dve.tensor_copy(SV[0:m, n, r * 256:(r + 1) * 256], ps[0:m, 2 * b, 0:256]).then_inc(acc_free[b], 1)
            dve.drain().then_inc(sv_done, 4 * (NT + 1))
            dve.memset(sbz[:, :, SBX:SBW], 0.0).then_inc(sv_done, 1)

            def sb_abs_of(n, par):
                dve.wait_ge(sb_zs, n + 3)
                z = sbz[:, par, :]
                dve.scalar_tensor_tensor(sbe[:, :], z, -1.0, z, ALU.mult, ALU.max).then_inc(sb_abs, 1)

            def sb_turn(i, par, more):
                n = i * 2 + par
                z = sbz[:, par, :]
                dve.wait_ge(sb_ln, n + 1)
                dve.wait_ge(sb_c, n + 1)
                dve.scalar_tensor_tensor(sbn[:, :], z, 0.0, sbe[:, :], ALU.max, ALU.add)
                dve.drain()
                for c in (0, 4, 7, 8):
                    d = sbn[:, c * P:(c + 1) * P]
                    ins = dve.tensor_tensor(d, d, vis, ALU.mult)
                ins.then_inc(sb_n, 1)
                if more:
                    sb_abs_of(n + 1, 1 - par)
                dve.wait_ge(sb_c, n + 2)
                two = lambda x: x.rearrange("p (a n) -> p a n", a=2)
                dve.tensor_tensor(two(z[:, 0:8 * P]), two(z[:, 0:8 * P]), ps[:, 4:6, :], ALU.subtract)
                dve.tensor_tensor(z[:, 8 * P:SBX], z[:, 8 * P:SBX], ps[:, 6, 0:2 * P], ALU.subtract)
                dve.tensor_tensor(z[0:META, SBX:SBW], z[0:META, SBX:SBW], ps[0:META, 7, :], ALU.subtract)
                dve.drain()
                for c in (0, 4, 7, 8):
                    d = z[:, c * P:(c + 1) * P]
                    ins = dve.tensor_tensor(d, d, vis_neg, ALU.add)
                ins.then_inc(sb_lw, 1)

            sb_abs_of(0, 0)
            with dve.Fori(0, HEADS // 2 - 1) as i:
                sb_turn(i, 0, True)
                sb_turn(i, 1, True)
            sb_turn(HEADS // 2 - 1, 0, True)
            sb_turn(HEADS // 2 - 1, 1, False)

            for i, slabs in groups(dve, branch_dn):
                for t in slabs:
                    b = acc_in(dve, branch_dn, i, t)
                    if isinstance(i, int):
                        taken(dve, gate_dn, 0, t)
                    else:
                        taken(dve, gate_dn, 0, KD - 2)
                        taken(dve, gate_dn, 0, KD - 1)
                    n = ds(i * R + t, 1)
                    dve.tensor_tensor(MG[:, n, :], ps[:, 2 * b:2 * b + 1, :], GT[:, n, :], ALU.mult).then_inc(acc_free[b], 1)
            for t in range(KD):
                b = acc_in(dve, branch_sb, 0, t)
                taken(dve, gate_sb, 0, t)
                dve.tensor_tensor(GT[:, t, :], ps[:, 2 * b, :], GT[:, t, :], ALU.mult).then_inc(acc_free[b], 1)
                dve.drain()
                dve.tensor_tensor(MG[:, t, :], MG[:, t, :], GT[:, t, :], ALU.add).then_inc(merged, 1)

            def add_residual(gm, gate=None):
                for t in range(KD):
                    b = acc_in(dve, gm, 0, t)
                    x = H[:, t, META:T]
                    if gate is None:
                        dve.tensor_tensor(x, x, ps[:, 2 * b, :], ALU.add).then_inc(acc_free[b], 1)
                    else:
                        dve.scalar_tensor_tensor(x, ps[:, 2 * b, :], gate(t), x, ALU.mult, ALU.add).then_inc(acc_free[b], 1)

            add_residual(mix_out)
            norm_dve(dve, 1, lambda k: H[:, k, META:T], lambda k: col("norm_ffn", k), SEQ, lambda k: HN[:, k, 0:SEQ])
            for i, slabs in groups(dve, ffn_in):
                for r in slabs:
                    taken(dve, ffn_in, i, 2 * r)
                    b = acc_in(dve, ffn_in, i, 2 * r + 1)
                    dve.tensor_tensor(ACTF[:, ds(i * R + r, 1), :], SG[:, r % 2, :].unsqueeze(1), ps[:, 2 * b:2 * b + 1, :], ALU.mult)\
                        .then_inc(acc_free[b], 1)
            add_residual(ffn_out)

            for l in range(2):
                dve.wait_ge(acc_ready, ada[l].ready(6 * KD - 1))
                dve.tensor_tensor(mod[:, l, :], ps[:, 4 + l, 0:6 * KD], cols("ada_b", l * 6 * KD, 6 * KD), ALU.add)
                dve.drain()
                for n, name in enumerate(("norm1", "norm2")):
                    c = (n * 3 + 1) * KD
                    ins = dve.scalar_tensor_tensor(gsc[:, l, n, :], mod[:, l, c:c + KD], 1.0, cols(name, l * KD, KD), ALU.add, ALU.mult)
            ins.then_inc(mod_done, 1)
            dve.drain()

            shift_dve(dve, 2, 0, 0)
            dve.wait_ge(a_in, 16)

            def rope(t):
                dve.wait_ge(a_rot, t + 1)
                dve.tensor_tensor(rtmp[:, :], ps[:, 7, :], ropes[:, 1, :], ALU.mult)
                dve.tensor_tensor(QG[:, t, :], QG[:, t, :], ropes[:, 0, :], ALU.mult)
                dve.drain()
                dve.tensor_tensor(QG[:, t, :], QG[:, t, :], rtmp[:, :], ALU.add).then_inc(a_done, 1)

            for t in range(10):
                dve.wait_ge(h_rs, 1 + 2 * HEADS + t + 1)
                dve.scalar_tensor_tensor(QG[:, t, :], QG[:, t, :], col("gq" if t < 8 else "gk"), NRS[:, 0:SEQ], ALU.mult, ALU.mult)\
                    .then_inc(h_done, 1)
                dve.drain().then_inc(a_nrm, 1)
                if t:
                    rope(t - 1)
            for n in range(NT):
                b = acc_in(dve, gq_v, 0, n)
                dve.tensor_copy(VG[:, n, :], ps[:, 2 * b, 0:256]).then_inc(acc_free[b], 1)
            rope(9)

            def maxima(g, j):
                n = g * 4 + j
                dve.wait_ge(a_s, n + 1)
                for q in range(NT):
                    dve.tensor_reduce(asm[:, j % 2, 0, q:q + 1], ps[:, q, :], AX.X, ALU.max)
                dve.drain()
                dve.tensor_scalar(asm[:, j % 2, 1, :], asm[:, j % 2, 0, :], -float(HD) ** -0.5, None, ALU.mult).then_inc(a_mx, 1)

            def gq_turn(g, more):
                for j in range(4):
                    n = g * 4 + j
                    if j < 3:
                        maxima(g, j + 1)
                    elif more:
                        maxima(g + 1, 0)
                    dve.wait_ge(a_e, n + 2)
                    dve.reciprocal(asm[:, j % 2, 3, :], asm[:, j % 2, 2, :])
                    dve.drain()
                    for q in range(NT):
                        ins = dve.tensor_scalar(PB[:, j % 2, q, :], PB[:, j % 2, q, :], asm[:, j % 2, 3, q:q + 1], None, ALU.mult)
                    ins.then_inc(a_p, 1)

            maxima(0, 0)
            with dve.Fori(0, KVH - 1) as g:
                gq_turn(g, True)
            gq_turn(KVH - 1, False)
            add_residual(gq_out, lambda t: mod[:, 0, 2 * KD + t:2 * KD + t + 1])

            def dve_conv_ffn(l, u):
                shift_dve(dve, u, l, 1)
                dve.memset(GP[:, :, 0:1], 0.0)
                dve.memset(GP[:, :, SEQ + 1:SEQ + 2], 0.0)
                dve.drain()
                for i, slabs in groups(dve, fc_in[l]):
                    for r in slabs:
                        j = i * R + r
                        taken(dve, fc_in[l], i, 2 * r)
                        x, y = GP[:, r % 2, :], SG[:, r % 2, :]
                        dve.tensor_scalar(y, x[:, 0:SEQ], dcol(f"fc_w{l}", j), dcol(f"fc_b{l}", j), ALU.mult, ALU.add)
                        dve.drain()
                        dve.scalar_tensor_tensor(y, x[:, 1:SEQ + 1], dcol(f"fc_w{l}", j + KF), y, ALU.mult, ALU.add)
                        dve.drain()
                        dve.scalar_tensor_tensor(y, x[:, 2:SEQ + 2], dcol(f"fc_w{l}", j + 2 * KF), y, ALU.mult, ALU.add)\
                            .then_inc(fc_conv, 1)
                        b = acc_in(dve, fc_in[l], i, 2 * r + 1)
                        dve.wait_ge(fc_silu, i * R + (l * KF + r + 1))
                        dve.tensor_tensor(ACTF[:, ds(j, 1), :], y.unsqueeze(1), ps[:, 2 * b:2 * b + 1, :], ALU.mult)\
                            .then_inc(acc_free[b], 1)
                add_residual(fc_out[l], lambda t: mod[:, l, 5 * KD + t:5 * KD + t + 1])

            dve_conv_ffn(0, 3)
            dve.memset(UP[:, :, 0:1], 0.0)
            dve.memset(UP[:, :, SEQ + 1:SEQ + 2], 0.0)
            dve.memset(later_t[:, :], 1.0)
            dve.drain()
            dve.memset(later_t[0:1, :], 0.0)
            shift_dve(dve, 4, 1, 0)
            for i, slabs in groups(dve, hy_in):
                for t in range(2 * R):
                    n = i * (2 * R) + t
                    taken(dve, hy_in, i, t)
                    x, y = UP[:, t % 2, :], U[:, ds(n, 1), :].rearrange("p a n -> p (a n)")
                    dve.tensor_scalar(y, x[:, 0:SEQ], dcol("hy_w", n), dcol("hy_b", n), ALU.mult, ALU.add)
                    dve.drain()
                    dve.scalar_tensor_tensor(y, x[:, 1:SEQ + 1], dcol("hy_w", n + 3 * KD), y, ALU.mult, ALU.add)
                    dve.drain()
                    dve.scalar_tensor_tensor(y, x[:, 2:SEQ + 2], dcol("hy_w", n + 6 * KD), y, ALU.mult, ALU.add).then_inc(y_conv, 1)
            two_pi_hi = 6.28125
            two_pi_lo = 2.0 * np.pi - two_pi_hi
            rounder = 1.5 * 2.0 ** 23
            for n in range(2):
                x, k = A1[:, n, :], A1[:, 2, :]
                dve.wait_ge(y_mlp, n + 1)
                dve.tensor_scalar(x, ps[0:FW, 6 + n, :], col(("b1", "b2")[n])[0:FW], col("freq")[0:FW], ALU.add, ALU.mult)
                dve.drain()
                dve.tensor_scalar(k, x, 1.0 / (2.0 * np.pi), rounder, ALU.mult, ALU.add)
                dve.drain()
                dve.tensor_scalar(k, k, rounder, None, ALU.subtract)
                dve.drain()
                dve.scalar_tensor_tensor(x, k, -two_pi_hi, x, ALU.mult, ALU.add)
                dve.drain()
                dve.scalar_tensor_tensor(x, k, -two_pi_lo, x, ALU.mult, ALU.add)
                dve.drain()
                dve.tensor_scalar(x, x, 3.1415925, -3.1415925, ALU.min, ALU.max).then_inc(y_arg, 1)
            with dve.Fori(0, ORDERS) as o:
                for dh in range(2):
                    u = o * 2 + dh
                    for t in range(NT):
                        b = t % 2 * 2
                        dve.drain()
                        if t == 0:
                            dve.wait_ge(y_w, u * 32 + 32)
                        dve.wait_ge(y_f, u * NT + t + 3)
                        if t:
                            dve.wait_ge(y_ab, u * NT + t)
                        dve.tensor_tensor(FB[:, 0, :], ps[:, b, :], DEC[:, t, :], ALU.mult)
                        if t == 0:
                            dve.scalar_tensor_tensor(FB[:, 1, :], ps[:, b + 1, :], later_t[:, 0:1], DEC[:, t, :], ALU.mult, ALU.mult)\
                                .then_inc(y_fb, 1)
                        else:
                            dve.tensor_tensor(FB[:, 1, :], ps[:, b + 1, :], DEC[:, t, :], ALU.mult).then_inc(y_fb, 1)
                        dve.drain()
                        dve.tensor_tensor(PM[:, 0, t, :], FB[:, 0, :], FB[:, 1, :], ALU.add)
                        dve.tensor_tensor(PM[:, 1, t, :], FB[:, 0, :], FB[:, 1, :], ALU.subtract).then_inc(y_pm, 1)
                    dve.wait_ge(y_n, u * NT + NT)
                    dve.reciprocal(rn[:, :], ps[:, 4, 0:NT]).then_inc(y_rn, 1)
                    dve.drain()
                    for f in range(NT):
                        b = f % 2 * 4
                        dve.drain()
                        dve.wait_ge(y_kc, u * NT + f + 1)
                        kc, ks = KS[:, f % 2, 0, :], KS[:, f % 2, 1, :]
                        zc, zs = ps[:, b + 2, :], ps[:, b + 3, :]
                        dve.tensor_tensor(YF[:, 0, f, :], zc, kc, ALU.mult)
                        dve.tensor_tensor(YT[:, 0, :], zs, ks, ALU.mult)
                        dve.tensor_tensor(YF[:, 1, f, :], zc, ks, ALU.mult)
                        dve.tensor_tensor(YT[:, 1, :], zs, kc, ALU.mult)
                        dve.drain()
                        dve.tensor_tensor(YF[:, 0, f, :], YF[:, 0, f, :], YT[:, 0, :], ALU.subtract)
                        dve.tensor_tensor(YF[:, 1, f, :], YF[:, 1, f, :], YT[:, 1, :], ALU.add).then_inc(y_y, 1)
                    for c in range(NT):
                        n = dh * NT + c
                        z = U[:, n, :]
                        dve.tensor_scalar(ytmp[:, c % 2, :], z, dcol("skip", o * KD + n), None, ALU.mult)
                        dve.drain()
                        dve.wait_ge(y_inv, u * NT + c + 1)
                        dve.scalar_tensor_tensor(ytmp[:, c % 2, :], ps[:, c % 2, :], rn[:, c:c + 1], ytmp[:, c % 2, :], ALU.mult, ALU.add)
                        dve.drain()
                        dve.tensor_tensor(z.unsqueeze(1), ytmp[:, c % 2:c % 2 + 1, :], U[:, ds(o * KD + (KD + n), 1), :], ALU.mult)\
                            .then_inc(y_z, 1)
            add_residual(hy_out, lambda t: mod[:, 1, 2 * KD + t:2 * KD + t + 1])
            dve_conv_ffn(1, 5)
            norm_dve(dve, 6, lambda k: H[:, k, META:T], lambda k: col("final", k), SEQ, lambda k: HN[:, k, 0:SEQ])
            for n in range(NT):
                for h in range(2):
                    dve.wait_ge(f_t, 2 * n + h + 1)
                    dve.tensor_copy(OUT[:, n, h * 4 * P:(h + 1) * 4 * P], ps[:, 4 + h, :]).then_inc(f_out, 1)


_TABLES = ("t_square", "t_delta", "t_rope", "t_fwd", "t_inv", "t_pos", "t_decay")
_SKIP = ("s5_",)


def kernel(**inputs):
    import concourse.bacc as bacc
    from concourse.bass_utils import run_bass_kernel_spmd

    nc = bacc.Bacc("TRN2", target_bir_lowering=False, num_devices=1)
    arrays, args = {}, {}
    given = {n: np.ascontiguousarray(a) for n, a in inputs.items() if not n.startswith(_SKIP)}
    for name, a in {**given, **tables()}.items():
        arrays[f"in_{name}"] = a
        args[name] = nc.dram_tensor(f"in_{name}", a.shape, F32, kind="ExternalInput").ap()
    out = nc.dram_tensor("out", (1, SEQ, D), F32, kind="ExternalOutput").ap()
    build(nc, args, out[0])
    r = run_bass_kernel_spmd(nc, [arrays], core_ids=[0])
    return r.results[0]["out"]
```

```python
from contextlib import ExitStack

import numpy as np

import concourse.bass as bass
from concourse import mybir

F32 = mybir.dt.float32
F32R = mybir.dt.float32r
ALU = mybir.AluOpType
ACT = mybir.ActivationFunctionType
AX = mybir.AxisListType
ds = bass.ds

P = 128
D = 1024
KD = D // P
SEQ = 512
META = 16
T = META + SEQ
TH = T // 2
NT = SEQ // P
HEADS = 8
DV = 256
DFF = 2816
KF = DFF // P
EPS = 1e-6
R = 4
SLOT = 11 * 256
NEG = -1e30
LEVELS = 7
QH, KVH, HD = 16, 4, 64
ORDERS = 2
EMB, FW = 33, 64

C_DQ, C_DK, C_DV, C_DZ = 0, 1024, 2048, 4096
C_AB, C_SQ, C_SK, C_SV = 6144, 6160, 7184, 8208
C_GD, C_GS = 9232, 10256

ROWS = {}


def _rows():
    tiles = [
        [("conv_q", 32), ("conv_k", 32), ("conv_v", 64)],
        [("norm_mix", 8), ("dn_gain", 2), ("sbq", 1), ("sbk", 1), ("norm_ffn", 8), ("norm1", 16),
         ("norm2", 16), ("final", 8), ("gq", 1), ("gk", 1), ("freq", 1), ("b1", 1), ("b2", 1),
         ("c", 8), ("skip", 16)],
        [("hy_w", 72), ("hy_b", 24)],
        [("ada_b", 96)],
        [("fc_w0", 66), ("fc_b0", 22)],
        [("fc_w1", 66), ("fc_b1", 22)],
    ]
    for n, tile in enumerate(tiles):
        at = n * P
        for name, rows in tile:
            ROWS[name] = (at, rows)
            at += rows
    return len(tiles)


PT = _rows()


def tables():
    i = np.arange(P)
    square = [
        np.eye(P),
        (i[:, None] <= i[None, :]),
        (i[:, None] >= i[None, :]),
        (i[:, None] // HD == i[None, :] // HD),
        (i[:, None] < i[None, :]),
        np.where(i[:, None] < i[None, :], 0.0, NEG),
        (i[:, None] == i[None, :] % HD),
        (i[:, None] == HD + i[None, :] % HD),
    ]
    rot = np.zeros((P, P))
    rot[i[1::2], i[0::2]] = -1.0
    rot[i[0::2], i[1::2]] = 1.0
    square.append(rot)
    delta = [
        np.where(i[None, :] >= i[:, None], 0.0, NEG),
        np.where(i[None, :] < i[:, None], 0.0, NEG),
    ]
    for s in range(LEVELS):
        b = i >> s
        delta.append((b[:, None] % 2 == 1) & (b[None, :] == b[:, None] - 1))
    flat = lambda a: np.ascontiguousarray(np.concatenate([np.asarray(x, np.float32) for x in a], axis=1))
    n_freq = HD // 4
    inv = (1.0 / (np.float32(10000.0) ** (np.arange(n_freq, dtype=np.float32) / np.float32(n_freq)))).astype(np.float32)
    t = np.arange(SEQ)
    ang = np.concatenate([(t // 64)[:, None].astype(np.float32) * inv, (t % 64)[:, None].astype(np.float32) * inv], 1)
    ang = np.repeat(ang.astype(np.float64), 2, axis=1).T
    rope = flat([np.tile(np.cos(ang), (2, 1)), np.tile(np.sin(ang), (2, 1))])
    f = np.arange(SEQ // 2)
    w = np.pi * ((2 * f[:, None] + 1) * t[None, :] % (4 * SEQ)) / (2 * SEQ)
    by_parity = np.concatenate([t[0::2], t[1::2]])
    rows = lambda a: flat([a[n * P:(n + 1) * P] for n in range(len(a) // P)])
    fwd = flat([rows(np.cos(w).T[by_parity]), rows(np.sin(w).T[by_parity])])
    inv_dft = flat([rows(np.cos(w)[:, by_parity] / SEQ), rows(np.sin(w)[:, by_parity] / SEQ)])
    lin = np.linspace(0.0, 1.0, SEQ, dtype=np.float32)[:, None]
    bands = (EMB - 1) // 2
    wl = (np.float32(2.0 * np.pi) * np.arange(SEQ, dtype=np.float32) / np.float32(SEQ))
    freq = np.linspace(1e-4, bands - 1, bands, dtype=np.float32)
    a = (wl[:, None] * freq[None, :]).astype(np.float32)
    pos = np.concatenate([lin, np.cos(a), -np.sin(a)], axis=1).astype(np.float32).T
    deltas = np.abs(np.linspace(np.log(1e-2) / 1.5, np.log(1e-2) / 0.3, D, dtype=np.float32))
    decay = np.exp(-lin * deltas[None, :]).astype(np.float32)[by_parity]
    return {"t_square": flat(square), "t_delta": flat(delta), "t_rope": rope, "t_fwd": fwd,
            "t_inv": inv_dft, "t_pos": np.ascontiguousarray(pos), "t_decay": decay}


def build(nc, A, out, stop=None):
    ctx = ExitStack()
    with ctx:
        top = [(nc.sbuf_base + 31) // 32 * 32]

        def at(name, shape, offset, parts=P, dtype=F32):
            return nc.alloc_sbuf_tensor_at(name, [parts, *shape], dtype, offset=top[0] + 4 * offset)

        here = [0]

        def fresh(name, *shape, parts=P, dtype=F32):
            n = int(np.prod(shape))
            t = at(name, shape, here[0], parts, dtype)
            here[0] += (n + 7) // 8 * 8
            return t

        def sem(name):
            return ctx.enter_context(nc.semaphore(name))

        raw = fresh("raw", 2, SLOT)
        spl_at = here[0]
        spl = fresh("spl", 2, 2, SLOT // 2, dtype=F32R)
        H = fresh("H", KD, T)
        hn_at = here[0]
        HNH = fresh("HNH", KD, T, dtype=F32R)
        lo_at = here[0]
        HNL = fresh("HNL", KD, T, dtype=F32R)
        HN = at("HN", [KD, T], lo_at)
        pcol = fresh("pcol", PT, P)
        square = fresh("square", 9, P)
        ident, triu, tril, pair_ones, vis, vis_neg, dup0, dup1, rot = (square[:, n, :] for n in range(9))
        ones = fresh("ones", P)
        tiny = fresh("tiny", 8)
        eps, zero = tiny[:, 0:1], tiny[:, 1:2]
        mod = fresh("mod", 2, 6 * KD)
        gsc = fresh("gsc", 2, 2, KD)
        csil = fresh("csil", KD)
        top_words = (nc.sbuf_usable_end - top[0]) // 4

        def col(name, n=0):
            c = ROWS[name][0] + n
            return pcol[:, c // P, c % P:c % P + 1]

        def cols(name, n, count):
            c = ROWS[name][0] + n
            return pcol[:, c // P, c % P:c % P + count]

        def dcol(name, n):
            c = ROWS[name][0]
            return pcol[:, c // P, ds(n + c % P, 1)]

        norm_at = here[0]
        NSQ = fresh("NSQ", 2, T)
        NRS = fresh("NRS", T)
        work = here[0]

        QK = fresh("QK", 2 * HEADS, T)
        QC, KC = QK[:, 0:HEADS, :], QK[:, HEADS:2 * HEADS, :]
        vo_at = here[0]
        VO = fresh("VO", NT, HEADS, DV)
        xt = at("xt", [NT, D], work)
        mt = at("mt", [D], work + NT * D, META)
        prow = at("prow", [PT, P], work + NT * D + D)
        gates_at = here[0]
        g_tok = fresh("g_tok", NT + 1, HEADS)
        b_tok = fresh("b_tok", NT + 1, HEADS)
        ab = fresh("ab", 16)
        wab = fresh("wab", KD, 16)
        wabh = fresh("wabh", KD, 16, dtype=F32R)
        wabl = fresh("wabl", KD, 16, dtype=F32R)
        abrow = fresh("abrow", 16, parts=1)
        soft = fresh("soft", 2, NT + 1, 16)
        scratch = here[0]
        xpad = fresh("xpad", 2, 536)
        cv = fresh("cv", 2, T)
        RSB = fresh("RSB", T)
        vm = fresh("vm", HEADS, DV, parts=META)
        km = fresh("km", HEADS, P, parts=META)
        gmb = fresh("gmb", HEADS, META, parts=META)
        ml = fresh("ml", HEADS, META, parts=META)
        mlm = fresh("mlm", HEADS, META, parts=META)
        mx = fresh("mx", HEADS, META, parts=META)
        my = fresh("my", HEADS, META, parts=META)
        mp = fresh("mp", HEADS, META, parts=META)
        msm = fresh("msm", 5, HEADS, parts=META)
        peak = [here[0]]
        here[0] = spl_at
        S = fresh("S", HEADS, DV)
        masks = fresh("masks", 2 + LEVELS, P)
        G4 = HEADS // 2
        lm = [fresh(f"lm{g}", 2, G4, P) for g in range(2)]
        vmb = at("vmb", [HEADS, DV], here[0] - 4 * G4 * P, META)
        assert here[0] <= spl_at + 2 * SLOT
        here[0] = scratch
        group = []
        for g in range(2):
            group.append(dict(
                k=fresh(f"k{g}", G4, P),
                q=fresh(f"q{g}", G4, P),
                gb=fresh(f"gb{g}", G4, P),
                dt=fresh(f"dt{g}", G4, P),
                lp=fresh(f"lp{g}", 2, G4, P),
                x=fresh(f"x{g}", G4, P),
                y=at(f"y{g}", [G4, P], norm_at + g * G4 * P),
                lm=lm[g],
                sm=fresh(f"sm{g}", 8, G4)))
        peak.append(here[0])
        assert max(peak) <= top_words, (peak, top_words)

        QSK = at("QSK", [2 * HEADS, T], work)
        OSL = at("OSL", [2 * HEADS, T], work, dtype=F32R)
        here[0] = scratch
        SV = fresh("SV", NT + 1, D)
        SBW = 14 * P
        SBX = 10 * P
        sbn = fresh("sbn", SBW)
        peak.append(here[0])
        here[0] = spl_at
        sbz = fresh("sbz", 2, SBW)
        sbe = fresh("sbe", SBW)
        assert here[0] <= spl_at + 2 * SLOT
        here[0] = norm_at
        sbk = fresh("sbk", T)
        sbv = fresh("sbv", NT + 1, P)
        assert here[0] <= work
        ZT = at("ZT", [2, SEQ], scratch)
        VOL = at("VOL", [NT, HEADS, DV], vo_at, dtype=F32R)
        VOH = at("VOH", [NT, HEADS, DV], gates_at, dtype=F32R)
        peak.append(gates_at + NT * HEADS * DV)
        mg_at = work + HEADS * T
        MG = at("MG", [KD, SEQ], mg_at)
        MGL = at("MGL", [KD, SEQ], mg_at, dtype=F32R)
        GT = at("GT", [KD, SEQ], vo_at)
        MGH = at("MGH", [KD, SEQ], vo_at + KD * SEQ, dtype=F32R)
        OSH = at("OSH", [KD, SEQ], gates_at, dtype=F32R)
        assert max(peak) <= top_words, (peak, top_words)
        here[0] = work
        AFH = fresh("AFH", KF, SEQ, dtype=F32R)
        af_at = here[0]
        AFL = fresh("AFL", KF, SEQ, dtype=F32R)
        ACTF = at("ACTF", [KF, SEQ], af_at)
        SG = at("SG", [2, SEQ], norm_at)
        ada_at = here[0]
        adw = fresh("adw", 2, KD, P)
        ads = fresh("ads", 4, P)
        assert here[0] <= top_words
        here[0] = ada_at
        GP = fresh("GP", 2, SEQ + 2)
        here[0] = work
        QG = fresh("QG", 10, SEQ)
        KDUP = fresh("KDUP", KVH, SEQ)
        VG = fresh("VG", NT, KVH * HD)
        ropes = fresh("ropes", 2, SEQ)
        rtmp = fresh("rtmp", SEQ)
        PB = fresh("PB", 2, NT, SEQ)
        PTB = fresh("PTB", 2, NT, SEQ)
        qst = fresh("qst", 2, SEQ)
        kst = fresh("kst", SEQ)
        vst = fresh("vst", NT, HD)
        asm = fresh("asm", 2, 4, NT)
        assert here[0] <= top_words
        OG = at("OG", [KD, SEQ], lo_at)
        OGH = at("OGH", [KD, SEQ], hn_at, dtype=F32R)
        OGL = at("OGL", [KD, SEQ], lo_at, dtype=F32R)
        here[0] = work
        U = fresh("U", 3 * KD, SEQ)
        ZL = at("ZL", [KD, SEQ], work, dtype=F32R)
        ZH = at("ZH", [KD, SEQ], work + KD * SEQ, dtype=F32R)
        UP_AT = here[0]
        UP = fresh("UP", 2, SEQ + 2)
        PM = fresh("PM", 2, NT, SEQ)
        fb_at = here[0]
        FB = fresh("FB", 2, SEQ)
        AB = fresh("AB", 2, SEQ)
        YT = at("YT", [2, SEQ], UP_AT)
        XZ = at("XZ", [4, SEQ], fb_at)
        DEC = fresh("DEC", NT, SEQ)
        W3 = fresh("W3", 2, SEQ, parts=FW)
        A1 = fresh("A1", 3, SEQ, parts=FW)
        POS = fresh("POS", SEQ, parts=EMB)
        W1 = fresh("W1", FW, parts=EMB)
        W2 = fresh("W2", FW, parts=FW)
        later_t = fresh("later_t", 1)
        rn = fresh("rn", 2, NT)
        assert here[0] <= top_words, here[0]
        ytmp = at("ytmp", [2, SEQ], norm_at)
        here[0] = hn_at
        YF = fresh("YF", 2, 4, SEQ)
        ZK = fresh("ZK", NT, SEQ)
        KS = fresh("KS", 4, SEQ)
        assert here[0] <= hn_at + 2 * KD * T
        here[0] = 0
        t_fwd = fresh("t_fwd", 2, NT, SEQ // 2)
        t_inv = fresh("t_inv", 2, 2, SEQ)
        KP = fresh("KP", 2, 4, SEQ)
        YB = fresh("YB", 4, SEQ)
        ZS = fresh("ZS", 2, SEQ)
        assert here[0] <= hn_at - KD * T
        OUT = at("OUT", [NT, D], work)

        ps = ctx.enter_context(nc.psum_tensor("ps", [P, 8, 512], F32))

        def half(b, m=P):
            return ps[0:m, b:b + 2, 0:TH]

        def split(ap):
            return ap.rearrange("p (h n) -> p h n", h=2)

        slot_full = [sem(f"slot_full{r}") for r in range(2)]
        split_ready = sem("split_ready")
        acc_ready = sem("acc_ready")
        split_x = sem("split_x")
        ada_in = [sem(f"ada_in{r}") for r in range(2)]
        ada_sum, ada_red = sem("ada_sum"), sem("ada_red")
        wab_split, n_y, n_hi = sem("wab_split"), sem("n_y"), sem("n_hi")
        table_full = sem("table_full")
        acc_free = [sem(f"acc_free{b}") for b in range(2)]
        x_in, small_in, table_in = sem("x_in"), sem("small_in"), sem("table_in")
        mask_in = sem("mask_in")
        cleared = sem("cleared")
        t_ready, t_done = sem("t_ready"), sem("t_done")
        n_sq, n_sum, n_rs, n_out = sem("n_sq"), sem("n_sum"), sem("n_rs"), sem("n_out")
        ab_ready = sem("ab_ready")
        conv_done, silu_done = sem("conv_done"), sem("silu_done")
        l2_sq, l2_sum, l2_rs, l2_done = sem("l2_sq"), sem("l2_sum"), sem("l2_rs"), sem("l2_done")
        vt_ready, vt_done = sem("vt_ready"), sem("vt_done")
        ab_x, ab_l = sem("ab_x"), sem("ab_l")
        m_pe, m_dve, m_act = sem("m_pe"), sem("m_dve"), sem("m_act")
        steps = ("staged", "gates", "expin", "expd", "lower", "masked", "prod", "inv", "pcopy", "delta", "ktok",
                 "kbg", "wt", "nw", "vb", "vn", "vnc", "o", "oc", "sd", "state")
        chunk = [{name: sem(f"{name}{g}") for name in steps} for g in range(2)]
        o_sq, o_sum, o_rs, z_done = sem("o_sq"), sem("o_sum"), sem("o_rs"), sem("z_done")
        h_sq, h_sum, h_rs, h_done = sem("h_sq"), sem("h_sum"), sem("h_rs"), sem("h_done")
        sv_done = sem("sv_done")
        sb_k, sb_v_in, sb_z, sb_zs, sb_abs, sb_ln = sem("sb_k"), sem("sb_v_in"), sem("sb_z"), sem("sb_zs"), sem("sb_abs"), sem("sb_ln")
        sb_n, sb_c, sb_lw, sb_w, sb_o, sb_oc = sem("sb_n"), sem("sb_c"), sem("sb_lw"), sem("sb_w"), sem("sb_o"), sem("sb_oc")
        merged = sem("merged")
        mod_done, silu_c, fc_conv, fc_silu = sem("mod_done"), sem("silu_c"), sem("fc_conv"), sem("fc_silu")
        a_in, a_nrm, a_rot, a_done, a_dup, a_dupc = sem("a_in"), sem("a_nrm"), sem("a_rot"), sem("a_done"), sem("a_dup"), sem("a_dupc")
        a_qk, a_v, a_s, a_mx, a_e, a_p = sem("a_qk"), sem("a_v"), sem("a_s"), sem("a_mx"), sem("a_e"), sem("a_p")
        a_t, a_tc, a_o, a_oc = sem("a_t"), sem("a_tc"), sem("a_o"), sem("a_oc")
        y_in, y_w, y_mlp, y_arg, y_sin = sem("y_in"), sem("y_w"), sem("y_mlp"), sem("y_arg"), sem("y_sin")
        y_conv, y_f, y_fb, y_ab, y_pm, y_n, y_rn = sem("y_conv"), sem("y_f"), sem("y_fb"), sem("y_ab"), sem("y_pm"), sem("y_n"), sem("y_rn")
        y_t, y_tc, y_k, y_kc, y_kp = sem("y_t"), sem("y_tc"), sem("y_k"), sem("y_kc"), sem("y_kp")
        y_dft, y_zc, y_x, y_cb, y_y, y_inv, y_z = sem("y_dft"), sem("y_zc"), sem("y_x"), sem("y_cb"), sem("y_y"), sem("y_inv"), sem("y_z")
        f_split = sem("f_split")
        f_t, f_out, stored = sem("f_t"), sem("f_out"), sem("stored")

        class Gemm:
            slabs = evacs = 0
            landed = [0, 0]

            def __init__(self, src, nslab, kt, width=256, pair=False, parts=1):
                self.src, self.nslab, self.kt, self.width, self.pair = src, nslab, kt, width, pair
                self.s0, self.u0, self.f0 = Gemm.slabs, 2 + 2 * Gemm.slabs, Gemm.evacs
                self.turn = R if pair else 2 * R
                Gemm.slabs += nslab
                Gemm.evacs += nslab if pair else 2 * nslab
                self.parts, self.base = parts, list(Gemm.landed)
                for r in range(nslab):
                    Gemm.landed[self.slot(r)] += 16 * parts
                plan.append(self)

            def slot(self, r):
                return (self.s0 + r) % 2

            def view(self, r):
                return raw[:, self.slot(r), 0:self.kt * self.width].rearrange("p (k n) -> p k n", k=self.kt)

            def half(self, u, part):
                return spl[:, u % 2, part, 0:self.kt * P].rearrange("p (k n) -> p k n", k=self.kt)

            def full(self, r):
                return self.base[self.slot(r)] + 16 * self.parts * (r // 2 + 1)

            def units(self, n):
                if self.pair:
                    return [(4 * j + 2 * m + q, 2 * j + q, m) for j in range(n // 2) for m in range(2) for q in range(2)]
                return [(2 * r + m, r, m) for r in range(n) for m in range(2)]

            def last(self, r):
                return self.u0 + (4 * (r // 2) + 2 + r % 2 if self.pair else 2 * r + 1) + 1

            def ready(self, t):
                return self.u0 + (t + 1) * (2 if self.pair else 1)

            def free(self, t):
                return (self.f0 + t) // 2 + 1

            def freed(self, t):
                return self.free(t) + 1

            def buf(self, t):
                return (self.f0 + t) % 2

        plan = []

        def w_cols(w, c0, width=256):
            v = w.rearrange("(k p) n -> p k n", p=P)
            return lambda i, r, h: v[:, :, ds(i * (R * width) + (r * width + c0), width)]

        def w_gate_up(w):
            v = w.rearrange("(k p) (h n) -> h p k n", p=P, h=2)
            return lambda i, r, h: v[h, :, :, ds(i * (R * P) + r * P, P)]

        def w_half_rows(w):
            v = w.rearrange("(q k p) n -> q p k n", p=P, q=2)
            return lambda i, r, h: v[r % 2, :, :, ds(i * (R // 2 * 256) + r // 2 * 256, 256)]

        w_in = A["w_in"][0]
        dn_qk = Gemm(w_cols(w_in, C_DQ), 8, KD)
        dn_v = Gemm(w_cols(w_in, C_DV), 8, KD)
        dn_z = Gemm(w_cols(w_in, C_DZ), 8, KD)
        sb_qk = Gemm(w_cols(w_in, C_SQ), 8, KD)
        sb_v = Gemm(w_cols(w_in, C_SV), 4, KD)
        gate_dn = Gemm(w_cols(w_in, C_GD), 4, KD)
        branch_dn = Gemm(w_half_rows(A["w_branch_dn"][0]), 8, KD, pair=True)
        gate_sb = Gemm(w_cols(w_in, C_GS), 4, KD)
        branch_sb = Gemm(w_cols(A["w_branch_sb"][0], 0), 4, KD)
        mix_out = Gemm(w_cols(A["w_out"][0], 0), 4, KD)
        ffn_in = Gemm(w_gate_up(A["w_ffn_in"][0]), KF, KD, parts=2)
        ffn_out = Gemm(w_half_rows(A["w_ffn_out"][0]), 8, KF // 2, pair=True)

        def groups(eng, gm):
            n = gm.nslab // R
            if n > 1:
                with eng.Fori(0, n) as i:
                    yield i, range(R)
            elif n:
                yield 0, range(R)
            if gm.nslab % R:
                yield n, range(gm.nslab % R)

        def products(pe, dst, w, x, first=True, final=True):
            pe.matmul(dst, w[0], x[0], start=first, stop=False)
            pe.matmul(dst, w[0], x[1], start=False, stop=False)
            return pe.matmul(dst, w[1], x[0], start=False, stop=final)

        def halves_of(gm, u, k):
            return gm.half(u, 0)[:, k, :], gm.half(u, 1)[:, k, :]

        def pe_tile(pe, gm, i, r, m, x, wide_t=False, ready=None):
            t = 2 * r + m
            b = gm.buf(t)
            pe.wait_ge(split_ready, i * (2 * R) + (gm.u0 + t + 1))
            pe.wait_ge(acc_free[b], i * (gm.turn // 2) + gm.free(t))
            for k in range(gm.kt):
                if ready and t == 0:
                    pe.wait_ge(*ready(k))
                w, tok = halves_of(gm, t, k), x(k)
                if wide_t:
                    for h in range(2):
                        mm = products(pe, ps[:, 2 * b + h, 0:TH], w, [y[:, h * TH:(h + 1) * TH] for y in tok],
                                      k == 0, k == gm.kt - 1)
                else:
                    mm = products(pe, ps[:, 2 * b, :], w, tok, k == 0, k == gm.kt - 1)
            mm.then_inc(acc_ready, 1)

        def wide(ap, n=P):
            return ap.unsqueeze(2).broadcast_to([ap.shape[0], ap.shape[1], n])

        def heads_of(ap, n):
            return ap.unsqueeze(1).broadcast_to([ap.shape[0], n, ap.shape[1]])

        gq_qk = Gemm(w_cols(A["attn_w_qkv_2"][0], 0), 5, KD)
        gq_v = Gemm(w_cols(A["attn_w_qkv_2"][0], (QH + KVH) * HD), 1, KD)
        gq_out = Gemm(w_cols(A["attn_w_o_2"][0], 0), 4, KD)
        fc_in, fc_out = [None, None], [None, None]

        def conv_ffn(l):
            fc_in[l] = Gemm(w_gate_up(A["ffn_w_up_2"][l]), KF, KD, parts=2)
            fc_out[l] = Gemm(w_half_rows(A["ffn_w_down_2"][l]), 8, KF // 2, pair=True)

        conv_ffn(0)
        hy_in = Gemm(w_cols(A["hy_w_in_2"][0], 0), 12, KD)
        hy_out = Gemm(w_cols(A["hy_w_out_2"][0], 0), 4, KD)
        conv_ffn(1)

        def taken(eng, gm, i, t):
            eng.wait_ge(acc_free[gm.buf(t)], i * (gm.turn // 2) + gm.freed(t))

        def acc_in(eng, gm, i, t):
            eng.wait_ge(acc_ready, i * (2 * R) + gm.ready(t))
            return gm.buf(t)

        LN_EXP, SILU = "natural_log_exp_and_others", "silu_and_others"

        def norm_act(act, u, x, n, shift=None, hi=True, tile=None):
            act.preload_act_table_set(LN_EXP)
            for k in range(KD):
                if tile:
                    tile(k)
                if k >= 2:
                    act.wait_ge(n_sum, KD * u + k - 1)
                act.activation(NSQ[:, k % 2, 0:n], x(k), ACT.Square).then_inc(n_sq, 1)
            act.wait_ge(n_sum, KD * (u + 1))
            src = half(6) if n == T else ps[:, 6, 0:n]
            dst = split(NRS[:, 0:n]) if n == T else NRS[:, 0:n]
            if u:
                act.wait_ge(n_out, KD * u)
            act.activation(dst, src, ACT.Ln, bias=eps, scale=1.0 / D)
            act.drain()
            act.activation(NRS[:, 0:n], NRS[:, 0:n], ACT.Exp, bias=zero, scale=-0.5).then_inc(n_rs, 1)
            for k in range(KD if hi else 0):
                act.wait_ge(n_y, KD * u + k + 1)
                act.activation(HNH[:, k, 0:n], HN[:, k, 0:n], ACT.Identity, bias=shift(k) if shift else zero, scale=1.0)\
                    .then_inc(n_hi, 1)

        def norm_pe(pe, u, n, tiles=range(KD)):
            for k in tiles:
                pe.wait_ge(n_sq, KD * u + k + 1)
                if n == T:
                    for h in range(2):
                        mm = pe.matmul(ps[:, 6 + h, 0:TH], ones[:, :], NSQ[:, k % 2, h * TH:(h + 1) * TH],
                                       start=k == 0, stop=k == KD - 1)
                else:
                    mm = pe.matmul(ps[:, 6, 0:n], ones[:, :], NSQ[:, k % 2, 0:n], start=k == 0, stop=k == KD - 1)
                mm.then_inc(n_sum, 1)

        def norm_after(pe, u):
            return lambda t: norm_pe(pe, u, SEQ, range(t - 1, t)) if t else None

        def norm_dve(dve, u, x, gain, n, shift=None):
            def lo(k):
                dve.wait_ge(n_hi, KD * u + k + 1)
                y = HN[:, k, 0:n]
                if shift:
                    ins = dve.scalar_tensor_tensor(HNL[:, k, 0:n], y, shift(k), HNH[:, k, 0:n], ALU.add, ALU.subtract)
                else:
                    ins = dve.tensor_tensor(HNL[:, k, 0:n], y, HNH[:, k, 0:n], ALU.subtract)
                ins.then_inc(n_out, 1)

            dve.wait_ge(n_rs, u + 1)
            for k in range(KD):
                dve.scalar_tensor_tensor(HN[:, k, 0:n], x(k), gain(k), NRS[:, 0:n], ALU.mult, ALU.mult).then_inc(n_y, 1)
                if k:
                    lo(k - 1)
            lo(KD - 1)

        def shift_of(l, n):
            return lambda k: mod[:, l, n * 3 * KD + k:n * 3 * KD + k + 1]

        def shift_dve(dve, u, l, n):
            norm_dve(dve, u, lambda k: H[:, k, META:T], lambda k: gsc[:, l, n, k:k + 1], SEQ, shift_of(l, n))

        def head_pe(pe, gm, i, t, n):
            pe.wait_ge(h_sq, n + 1)
            pe.wait_ge(h_rs, n + 1)
            for h in range(2):
                mm = pe.matmul(ps[:, 6 + h, 0:TH], ones[:, :], NSQ[:, t % 2, h * TH:(h + 1) * TH], start=True, stop=True)
            mm.then_inc(h_sum, 1)

        def pe_gemm(pe, gm, x, ready=None, after=None, tile_after=None):
            for i, slabs in groups(pe, gm):
                for r in slabs:
                    for m in range(2):
                        pe_tile(pe, gm, i, r, m, x, False, ready)
                        if tile_after:
                            tile_after(2 * r + m)
                    if after:
                        after(r)

        def pe_gemm_pair(pe, gm, x, ready=None, after=None):
            if after:
                turns = [(i, range(R)) for i in range(gm.nslab // R)]
            else:
                turns = groups(pe, gm)
            for i, slabs in turns:
                for u, r, m in gm.units(len(slabs)):
                    t, q = u // 2, u % 2
                    b = gm.buf(t)
                    if ready and u < 2:
                        pe.wait_ge(*ready(q))
                    pe.wait_ge(split_ready, i * (2 * R) + (gm.u0 + u + 1))
                    if q == 0:
                        pe.wait_ge(acc_free[b], i * (gm.turn // 2) + gm.free(t))
                    for k in range(gm.kt):
                        mm = products(pe, ps[:, 2 * b, :], halves_of(gm, u, k), x(q * gm.kt + k),
                                      q + k == 0, q == 1 and k == gm.kt - 1)
                    mm.then_inc(acc_ready, 1)
                    if after and q:
                        after(i * R + t)

        def pool_split(pool, gm):
            for i, slabs in groups(pool, gm):
                seen = set()
                for u, r, m in gm.units(len(slabs)):
                    if r not in seen:
                        pool.wait_ge(slot_full[gm.slot(r)], i * (16 * gm.parts * R // 2) + gm.full(r))
                        seen.add(r)
                    pool.wait_ge(acc_ready, i * (2 * R) + (gm.u0 + u - 1))
                    w, hi, lo = gm.view(r)[:, :, m * P:(m + 1) * P], gm.half(u, 0), gm.half(u, 1)
                    pool.tensor_tensor(hi, w, heads_of(ones[:, :], gm.kt), ALU.mult)
                    pool.drain()
                    pool.tensor_tensor(lo, w, hi, ALU.subtract).then_inc(split_ready, 1)

        def split_tile(eng, x, hi, lo):
            eng.tensor_copy(hi, x)
            eng.drain()
            return eng.tensor_tensor(lo, x, hi, ALU.subtract)

        SB = [(0, 0, META, P), (4 * P, P, META + P, P), (7 * P, 3 * P, META + 3 * P, P), (8 * P, 2 * P, META + 2 * P, P),
              (10 * P, 0, 0, META)]
        SB_V = [0, 1, 3, 2, NT]

        def sb_bank(b, n):
            c, q0, _, m = SB[n]
            c = c if n < 4 else 12 * P
            return ps[0:m, b + c // 512, c % 512:c % 512 + SEQ - q0]

        def sb_keys(x, n):
            c, q0, _, m = SB[n]
            return x[0:m, c:c + SEQ - q0]

        def sb_logits(pe, i, par):
            n = i * 2 + par
            pe.wait_ge(sb_k, n + 1)
            pe.wait_ge(sb_zs, n + 2)
            pe.wait_ge(sb_oc, n + 1)
            for t in (1, 2, 3, 4, 0):
                c, q0, k0, m = SB[t]
                mm = pe.matmul(sb_bank(0, t), sbk[:, k0:k0 + m],
                               QSK[:, ds(n, 1), META + q0:T].rearrange("p a n -> p (a n)"), start=True, stop=True)
            mm.then_inc(sb_z, 1)

        def hyena_units(eng, start, pair):
            start()
            with eng.Fori(0, ORDERS - 1) as o:
                pair(o, True)
            pair(ORDERS - 1, False)

        SMALL = 30
        block = ctx.enter_context(nc.Block())

        ADA = 2 * 6 * KD
        ADA_WITH = {gate_sb: 2, branch_sb: 2, mix_out: 3, ffn_in: 2, ffn_out: 3}
        ada_base, n_ada = {}, 0
        for gm, n in ADA_WITH.items():
            ada_base[gm] = n_ada
            n_ada += n * gm.nslab
        assert n_ada == ADA
        ADA_TURN = R * ADA_WITH[ffn_in]
        ada_w = A["ada_w_2"].rearrange("l (k p) n -> l p k n", p=P)

        def ada_units(gm, r):
            n = ADA_WITH[gm]
            return range(ada_base[gm] + r * n, ada_base[gm] + (r + 1) * n)

        def ada_load(sp, i, c):
            if c >= 2:
                sp.wait_ge(ada_sum, i * ADA_TURN + (c - 1))
            sp.dma_start(adw[:, c % 2, :, :], ada_w[c % 2][:, :, ds((i * (ADA_TURN // 2) + c // 2) * P, P)]).then_inc(ada_in[c % 2], 16)

        def ada_dve(dve, i, c):
            dve.wait_ge(ada_in[c % 2], i * (16 * ADA_TURN // 2) + 16 * (c // 2 + 1))
            dve.wait_ge(ada_red, i * ADA_TURN + (c + 1))
            w = adw[:, c % 2, :, :]
            dve.tensor_tensor(w, w, wide(csil[:, :]), ALU.mult)
            for n in (4, 2):
                dve.drain()
                dve.tensor_tensor(w[:, 0:n, :], w[:, 0:n, :], w[:, n:2 * n, :], ALU.add)
            dve.drain()
            dve.tensor_tensor(ads[:, c % 4, :], w[:, 0, :], w[:, 1, :], ALU.add).then_inc(ada_sum, 1)

        def ada_pe(pe, i, c):
            pe.wait_ge(ada_sum, i * ADA_TURN + (c + 1))
            n = i * (ADA_TURN // 2) + (c % 2 * 6 * KD + c // 2)
            pe.matmul(ps[:, 4, ds(n, 1)], ads[:, c % 4, :], ones[:, 0:1], start=True, stop=True).then_inc(ada_red, 1)

        @block.sync
        def _(sp):
            done = []
            for gm in plan:
                def load(i, r):
                    n = gm.width // gm.parts
                    for h in range(gm.parts):
                        sp.dma_start(gm.view(r)[:, :, h * n:(h + 1) * n], gm.src(i, r, h))\
                            .then_inc(slot_full[gm.slot(r)], 16)
                    if gm in ada_base:
                        if r or not isinstance(i, int) or i:
                            for c in ada_units(gm, r - 1):
                                if c == 0:
                                    sp.wait_ge(acc_ready, gate_sb.u0)
                                ada_load(sp, i, c)
                        elif gm is not gate_sb:
                            before = list(ada_base)[list(ada_base).index(gm) - 1]
                            for c in ada_units(before, before.nslab - 1):
                                ada_load(sp, 0, c)

                def reread(i, r):
                    sp.wait_ge(split_ready, i * (2 * R) + (gm.last(r - 2) if r >= 2 else gm.last(r + 2) - 2 * R))

                if gm is hy_out:
                    sp.wait_ge(acc_ready, hy_out.u0)
                    for buf, src in ((t_fwd, A["t_fwd"]), (t_inv, A["t_inv"])):
                        sp.dma_start(buf[:, :, :, :].rearrange("p s k n -> p (s k n)"), src).then_inc(table_full, 16)
                    sp.wait_ge(y_inv, 1 + 2 * ORDERS * NT)
                done += [gm.last(r) for r in range(gm.nslab)]
                turns, rest = gm.nslab // R, gm.nslab % R
                for r in range(min(R, gm.nslab)):
                    if gm.s0 + r >= 2:
                        sp.wait_ge(split_ready, done[gm.s0 + r - 2])
                    load(0, r)
                if gm is ffn_out:
                    for r in range(R, 2 * R):
                        sp.wait_ge(split_ready, gm.last(r - 2))
                        load(0, r)
                    for c in ada_units(gm, 2 * R - 1):
                        ada_load(sp, 0, c)
                elif turns > 1:
                    with sp.Fori(1, turns) as i:
                        for r in range(R):
                            reread(i, r)
                            load(i, r)
                for r in range(rest if turns else 0):
                    reread(turns, r)
                    load(turns, r)

        @block.gpsimd
        def _(pool):
            pool.sem_inc(split_ready, 2)
            pool.sem_inc(y_kp, 1)
            pool.sem_inc(y_y, 1)
            pool.dma_start(xt[:, :, :], A["x"][0].rearrange("(n p) d -> p n d", p=P)).then_inc(x_in, 16)
            pool.dma_start(mt[:, :], A["meta_tokens"]).then_inc(x_in, 16)
            pool.dma_start(square[:, :, :].rearrange("p a b -> p (a b)"), A["t_square"]).then_inc(table_in, 16)
            pool.memset(ones[:, :], 1.0)
            pool.memset(tiny[:, 0:1], EPS)
            pool.memset(tiny[:, 1:2], 0.0)
            pool.memset(prow[:, :, :], 0.0)
            pool.memset(xpad[:, :, 0:3], 0.0).then_inc(cleared, 1)
            pool.wait_ge(cleared, 1)
            small = []

            def rows(name, src):
                r, n = ROWS[name]
                pool.dma_start(prow[r % P:r % P + n, r // P, 0:src.shape[-1]], src).then_inc(small_in, 16)
                small.append(name)

            tile = lambda ap: ap.rearrange("j (k p) -> (j k) p", p=P)
            one = lambda ap: ap.rearrange("(j k) -> j k", j=1)
            rows("conv_q", tile(A["conv_q"][0]))
            rows("conv_k", tile(A["conv_k"][0]))
            rows("conv_v", tile(A["conv_v"][0]))
            rows("norm_mix", tile(A["norm_mix_gain"]))
            rows("dn_gain", tile(A["dn_out_norm_gain"]))
            rows("sbq", A["sb_q_norm_gain"])
            rows("sbk", A["sb_k_norm_gain"])
            rows("norm_ffn", tile(A["norm_ffn_gain"]))
            rows("norm1", tile(A["norm1_g_2"]))
            rows("norm2", tile(A["norm2_g_2"]))
            rows("final", tile(one(A["final_g_2"])))
            for part in range(2):
                for name, src in (("gq", A["attn_q_gain_2"]), ("gk", A["attn_k_gain_2"])):
                    r = ROWS[name][0]
                    pool.dma_start(prow[r % P:r % P + 1, r // P, part * HD:(part + 1) * HD], src).then_inc(small_in, 16)
                    small.append(name)
            rows("freq", A["hy_f_freq_2"])
            rows("b1", A["hy_f_b1_2"])
            rows("b2", A["hy_f_b2_2"])
            rows("c", tile(A["c_2"]))
            rows("skip", tile(A["hy_skip_2"][0]))
            rows("hy_w", tile(A["hy_conv_w_2"][0]))
            rows("hy_b", tile(A["hy_conv_b_2"]))
            rows("ada_b", tile(A["ada_b_2"]))
            for l in range(2):
                rows(f"fc_w{l}", tile(A["ffn_conv_w_2"][l]))
                rows(f"fc_b{l}", tile(A["ffn_conv_b_2"][l:l + 1]))
            pool.dma_start(wab[:, :, :], w_cols(w_in, C_AB, 16)(0, 0, 0)).then_inc(small_in, 16)
            pool.dma_start(abrow[:, 0:8], A["dn_a_log"]).then_inc(small_in, 16)
            pool.dma_start(abrow[:, 8:16], A["dn_dt_bias"]).then_inc(small_in, 16)
            assert len(small) + 3 == SMALL
            pool.wait_ge(small_in, 16 * SMALL)
            pool.tensor_tensor(wabh[:, :, :], wab[:, :, :], heads_of(ones[:, 0:16], KD), ALU.mult)
            pool.drain()
            pool.tensor_tensor(wabl[:, :, :], wab[:, :, :], wabh[:, :, :], ALU.subtract).then_inc(wab_split, 1)
            pool_split(pool, dn_qk)
            pool_split(pool, dn_v)
            pool.wait_ge(l2_done, 1 + 16)
            pool.wait_ge(vt_done, 2 + 32)
            pool.dma_start(masks[:, :, :].rearrange("p a b -> p (a b)"), A["t_delta"]).then_inc(mask_in, 16)
            pool.wait_ge(mask_in, 16)
            with pool.Fori(0, NT) as c:
                for l in range(LEVELS):
                    for g in range(2):
                        G, E = group[g], chunk[g]
                        if l == 0:
                            pool.wait_ge(E["lower"], c + 1)
                        if l == 2:
                            pool.wait_ge(E["inv"], c * LEVELS + 1)
                        if l >= 2:
                            pool.wait_ge(E["prod"], c * LEVELS + l - 1)
                        pool.tensor_tensor(G["lm"][:, l % 2, :, :], G["lp"][:, 0, :, :],
                                           heads_of(masks[:, 2 + l, :], G4), ALU.mult).then_inc(E["masked"], 1)
            for g in range(2):
                pool.wait_ge(chunk[g]["state"], 1 + NT)
                pool.wait_ge(chunk[g]["oc"], 1 + NT)
            pool_split(pool, dn_z)
            pool_split(pool, sb_qk)
            pool_split(pool, sb_v)
            pool.wait_ge(h_done, 1 + 2 * HEADS)
            pool.wait_ge(sv_done, 4 * (NT + 1))

            def stage_head(n):
                pool.tensor_copy(sbk[:, :].unsqueeze(1), QSK[:, ds(n + HEADS, 1), :]).then_inc(sb_k, 1)

            def stage_v(n):
                pool.tensor_copy(sbv[:, 0:NT, :], SV[:, 0:NT, ds(n * P, P)]).then_inc(sb_v_in, 1)
                pool.tensor_copy(sbv[0:META, NT, :], SV[0:META, NT, ds(n * P, P)]).then_inc(sb_v_in, 1)

            stage_head(0)
            stage_v(0)
            with pool.Fori(1, HEADS) as n:
                pool.wait_ge(sb_z, n)
                stage_head(n)
                pool.wait_ge(sb_o, n + 1)
                stage_v(n)

            pool.wait_ge(sb_oc, 2 + HEADS)
            for gm in (gate_dn, branch_dn, gate_sb, branch_sb, mix_out, ffn_in, ffn_out):
                pool_split(pool, gm)
            taken(pool, ffn_out, 1, 2 * R - 1 - R)
            taken(pool, ffn_out, 1, 2 * R - 2 - R)
            pool.dma_start(ropes[:, :, :].rearrange("p a n -> p (a n)"), A["t_rope"]).then_inc(a_in, 16)
            pool_split(pool, gq_qk)
            pool_split(pool, gq_v)
            pool.wait_ge(a_done, 10)
            pool.wait_ge(a_dupc, KVH)
            taken(pool, gq_v, 0, 1)
            taken(pool, gq_v, 0, 0)

            def stage_qk(g):
                pool.tensor_copy(qst[:, :, :], QG[:, ds(g * 2, 2), :]).then_inc(a_qk, 1)
                pool.tensor_copy(kst[:, :].unsqueeze(1), KDUP[:, ds(g, 1), :]).then_inc(a_qk, 1)

            def stage_vg(g):
                pool.tensor_copy(vst[:, :, :], VG[:, :, ds(g * HD, HD)]).then_inc(a_v, 1)

            stage_qk(0)
            stage_vg(0)
            with pool.Fori(1, KVH) as g:
                pool.wait_ge(a_s, g * 4)
                stage_qk(g)
                pool.wait_ge(a_o, g * 4 + 2)
                stage_vg(g)

            for gm in (gq_out, fc_in[0], fc_out[0]):
                pool_split(pool, gm)
            taken(pool, fc_out[0], 1, R - 1)
            taken(pool, fc_out[0], 1, R - 2)
            pool.dma_start(POS[:, :], A["t_pos"]).then_inc(y_in, 16)
            pool.dma_start(W1[:, :], A["hy_f_w1_2"][0]).then_inc(y_in, 16)
            pool.dma_start(W2[:, :], A["hy_f_w2_2"][0]).then_inc(y_in, 16)
            pool_split(pool, hy_in)
            w3 = A["hy_f_w3_2"][0].rearrange("p (o s d) -> o p s d", o=ORDERS, s=2)
            dec = A["t_decay"].rearrange("(n p) d -> p n d", p=P)

            def filter_in(o, dh):
                half_d = slice(dh * SEQ, (dh + 1) * SEQ)
                pool.dma_start(W3[:, :, :], w3[ds(o, 1), :, :, half_d].rearrange("o p s d -> (o p) s d")).then_inc(y_w, 16)
                pool.dma_start(DEC[:, :, :], dec[:, :, half_d]).then_inc(y_w, 16)

            def hyena_pair(o, more):
                for dh in range(2):
                    u = o * 2 + dh
                    for f in range(2):
                        pool.wait_ge(y_cb, u * 2 + f + 1)
                        pool.wait_ge(y_kc, u * 2 + f + 1)
                        ce, co, se, so = (KS[:, n, :] for n in range(4))
                        pool.tensor_tensor(KP[:, f, 0, :], ce, co, ALU.add)
                        pool.tensor_tensor(KP[:, f, 1, :], se, so, ALU.add)
                        pool.tensor_tensor(KP[:, f, 2, :], ce, co, ALU.subtract)
                        pool.tensor_tensor(KP[:, f, 3, :], so, se, ALU.subtract).then_inc(y_kp, 1)
                        if f == 0 and (dh == 0 or more):
                            filter_in(o + dh, 1 - dh)
                    for f in range(2):
                        pool.wait_ge(y_inv, u * NT + 1)
                        pool.wait_ge(y_cb, u * 2 + f + 3)
                        c, si, cm, sm = (YB[:, n, :] for n in range(4))
                        pool.tensor_tensor(YF[:, f, 0, :], c, cm, ALU.add)
                        pool.tensor_tensor(YF[:, f, 1, :], si, sm, ALU.subtract)
                        pool.tensor_tensor(YF[:, f, 2, :], c, cm, ALU.subtract)
                        pool.tensor_tensor(YF[:, f, 3, :], si, sm, ALU.add).then_inc(y_y, 1)

            hyena_units(pool, lambda: filter_in(0, 0), hyena_pair)
            for gm in (hy_out, fc_in[1], fc_out[1]):
                pool_split(pool, gm)

        @block.tensor
        def _(pe):
            pe.sem_inc(acc_ready, 2)
            pe.sem_inc(vt_ready, 4)
            pe.sem_inc(ada_red, 4)
            pe.sem_inc(l2_sum, 2)
            pe.sem_inc(h_sum, 2)
            pe.sem_inc(sb_c, 1)
            pe.sem_inc(sb_o, 1)
            pe.sem_inc(a_t, 5)
            pe.sem_inc(a_o, 2)
            pe.sem_inc(y_inv, 1)
            pe.wait_ge(x_in, 32)
            pe.wait_ge(table_in, 16)
            for k in range(KD):
                if k >= 2:
                    pe.wait_ge(t_done, 2 * (k - 1))
                for n in range(NT):
                    mm = pe.transpose(ps[:, k % 2, n * P:(n + 1) * P], xt[:, n, k * P:(k + 1) * P], ident)
                mm.then_inc(t_ready, 1)
                pe.transpose(ps[:, 2 + k % 2, 0:META], mt[:, k * P:(k + 1) * P], ident[0:META, 0:META])\
                    .then_inc(t_ready, 1)
            pe.wait_ge(small_in, 16 * SMALL)
            for n in range(PT):
                mm = pe.transpose(ps[:, 4 + n // 4, n % 4 * P:(n % 4 + 1) * P], prow[:, n, :], ident)
            mm.then_inc(t_ready, 1)
            norm_pe(pe, 0, T)
            pe.wait_ge(n_out, KD)
            pe.wait_ge(wab_split, 1)
            pe.wait_ge(t_done, 2 * KD + 1)
            for n in range(NT + 1):
                m, c0 = (P, META + n * P) if n < NT else (META, 0)
                for k in range(KD):
                    products(pe, ps[0:m, 4, n * 16:(n + 1) * 16], [y[:, k, c0:c0 + m] for y in (HNH, HNL)],
                             [y[:, k, :] for y in (wabh, wabl)], k == 0, k == KD - 1)
            pe.matmul(ps[:, 5, 0:16], ones[0:1, :], abrow[:, :], start=True, stop=True).then_inc(ab_ready, 1)
            x_all = lambda k: (HNH[:, k, :], HNL[:, k, :])
            x_meta = lambda k: (HNH[:, k, META:T], HNL[:, k, META:T])
            x_hn = lambda k: (HNH[:, k, 0:SEQ], HNL[:, k, 0:SEQ])
            for i, slabs in groups(pe, dn_qk):
                for r in slabs:
                    for m in range(2):
                        pe_tile(pe, dn_qk, i, r, m, x_all, True)

            def v_turn(i, t):
                n = i * (2 * R) + t
                src = cv[:, t % 2, :]
                pe.wait_ge(silu_done, n + 2 + 16 + 1)
                pe.wait_ge(vt_done, n * 2 + 2)
                for c in range(NT):
                    mm = pe.transpose(ps[:, 6, c * P:(c + 1) * P], src[:, META + c * P:META + (c + 1) * P], ident)
                mm.then_inc(vt_ready, 1)
                pe.transpose(ps[0:META, 7, 0:P], src[:, 0:META], ident).then_inc(vt_ready, 1)

            pe.wait_ge(ab_x, 1)
            for i, slabs in groups(pe, dn_v):
                for r in slabs:
                    for m in range(2):
                        t = 2 * r + m
                        n = i * (2 * R) + t
                        pe_tile(pe, dn_v, i, r, m, x_all, True)
                        pe.wait_ge(l2_sq, n + 1)
                        pe.wait_ge(l2_rs, n + 1)
                        for h in range(2):
                            mm = pe.matmul(ps[:, 4 + h, 0:TH], ones[:, :], NSQ[:, t % 2, h * TH:(h + 1) * TH],
                                           start=True, stop=True)
                        mm.then_inc(l2_sum, 1)
                        if t:
                            v_turn(i, t - 1)
                v_turn(i, 2 * R - 1)

            m = META
            pe.wait_ge(l2_done, 1 + 16)
            pe.wait_ge(vt_done, 2 + 32)
            pe.wait_ge(m_dve, 1)
            for h in range(HEADS):
                pe.matmul(ps[0:m, 0, h * m:(h + 1) * m], gmb[:, h, :], triu[0:m, 0:m], start=True, stop=True)
            pe.matmul(ps[0:m, 1, 0:HEADS], triu[0:m, 0:m], gmb[:, :, 0], start=True, stop=True)
            for h in range(HEADS):
                kh = KC[:, h, 0:m]
                pe.matmul(ps[0:m, 2, h * m:(h + 1) * m], kh, kh, start=True, stop=True)
            for h in range(HEADS):
                mm = pe.transpose(ps[0:m, 3 + h // 4, h % 4 * P:(h % 4 + 1) * P], KC[:, h, 0:m], ident)
            mm.then_inc(m_pe, 1)
            for l in range(4):
                pe.wait_ge(m_dve, 4 + 3 * l)
                for h in range(HEADS):
                    mm = pe.matmul(ps[0:m, 0, h * m:(h + 1) * m], mlm[:, h, :], my[:, h, :] if l else ident[0:m, 0:m],
                                   start=True, stop=True)
                mm.then_inc(m_pe, 1)
                if l:
                    pe.wait_ge(m_dve, 5 + 3 * l)
                    for h in range(HEADS):
                        mm = pe.matmul(ps[0:m, 1, h * m:(h + 1) * m], mx[:, h, :], mp[:, h, :], start=True, stop=True)
                    for h in range(HEADS):
                        mm = pe.matmul(ps[0:m, 2, h * m:(h + 1) * m], mp[:, h, :], mx[:, h, :], start=True, stop=True)
                    mm.then_inc(m_pe, 1)
            pe.wait_ge(m_dve, 16)
            for h in range(HEADS):
                mm = pe.matmul(ps[0:m, 4 + h // 2, h % 2 * DV:(h % 2 + 1) * DV], my[:, h, :], vmb[:, h, :],
                               start=True, stop=True)
            mm.then_inc(m_pe, 1)
            pe.wait_ge(m_dve, 17)
            for h in range(HEADS):
                mm = pe.matmul(ps[:, h // 2, h % 2 * DV:(h % 2 + 1) * DV], km[:, h, :], vm[:, h, :], start=True, stop=True)
            mm.then_inc(m_pe, 1)

            pe.wait_ge(m_dve, 18)
            with pe.Fori(0, NT) as c:
                for g in range(2):
                    G, E, b = group[g], chunk[g], 4 * g
                    pe.wait_ge(E["staged"], c + 1)
                    pe.wait_ge(E["oc"], c + 1)
                    for h in range(G4):
                        pe.matmul(ps[:, b, h * P:(h + 1) * P], G["gb"][:, h, :], triu, start=True, stop=True)
                    pe.matmul(ps[:, b + 1, 0:G4], triu, G["gb"][:, :, 0], start=True, stop=True)
                    for h in range(G4):
                        pe.matmul(ps[:, b + 2, h * P:(h + 1) * P], G["k"][:, h, :], G["k"][:, h, :], start=True, stop=True)
                    for h in range(G4):
                        mm = pe.matmul(ps[:, b + 3, h * P:(h + 1) * P], G["k"][:, h, :], G["q"][:, h, :],
                                       start=True, stop=True)
                    mm.then_inc(E["gates"], 1)
                for l in range(LEVELS):
                    for g in range(2):
                        G, E, b = group[g], chunk[g], 4 * g
                        pe.wait_ge(E["masked"], c * LEVELS + l + 1)
                        if l:
                            pe.wait_ge(E["inv"], c * LEVELS + l)
                        for h in range(G4):
                            mm = pe.matmul(ps[:, b, h * P:(h + 1) * P], G["lm"][:, l % 2, h, :],
                                           G["y"][:, h, :] if l else ident, start=True, stop=True)
                        mm.then_inc(E["prod"], 1)
                        if l == 0:
                            for h in range(G4):
                                mm = pe.transpose(ps[:, b + 1, h * P:(h + 1) * P], G["k"][:, h, :], ident)
                            mm.then_inc(E["ktok"], 1)
                    for g in range(2):
                        G, E, b = group[g], chunk[g], 4 * g
                        if l:
                            pe.wait_ge(E["pcopy"], c * (LEVELS - 1) + l)
                            for h in range(G4):
                                mm = pe.matmul(ps[:, b + 2, h * P:(h + 1) * P], G["x"][:, h, :], G["lp"][:, 1, h, :],
                                               start=True, stop=True)
                            if l < LEVELS - 1:
                                for h in range(G4):
                                    mm = pe.matmul(ps[:, b + 3, h * P:(h + 1) * P], G["lp"][:, 1, h, :], G["x"][:, h, :],
                                                   start=True, stop=True)
                            mm.then_inc(E["delta"], 1)
                for g in range(2):
                    G, E, b = group[g], chunk[g], 4 * g
                    pe.wait_ge(E["inv"], c * LEVELS + LEVELS)
                    pe.wait_ge(E["kbg"], c + 1)
                    for h in range(G4):
                        mm = pe.matmul(ps[:, b, h * P:(h + 1) * P], G["gb"][:, h, :], G["y"][:, h, :], start=True, stop=True)
                    mm.then_inc(E["wt"], 1)
                for g in range(2):
                    G, E, b = group[g], chunk[g], 4 * g
                    pe.wait_ge(E["vb"], c + 1)
                    pe.wait_ge(E["nw"], c + 1)
                    pe.wait_ge(E["state"], c + 1)
                    for h in range(G4):
                        dst = ps[:, b + 2 + h // 2, h % 2 * DV:(h % 2 + 1) * DV]
                        vb = G["lm"][:, h // 2, h % 2 * 2:h % 2 * 2 + 2, :].rearrange("p a n -> p (a n)")
                        pe.matmul(dst, G["y"][:, h, :], vb, start=True, stop=False)
                        mm = pe.matmul(dst, G["x"][:, h, :], S[:, g * G4 + h, :], start=False, stop=True)
                    mm.then_inc(E["vn"], 1)
                for g in range(2):
                    G, E, b = group[g], chunk[g], 4 * g
                    pe.wait_ge(E["vnc"], c + 1)
                    for h in range(G4):
                        for e in range(2):
                            dst = ps[:, b + h // 2, (h % 2 * 2 + e) * P:(h % 2 * 2 + e + 1) * P]
                            pe.matmul(dst, S[:, g * G4 + h, e * P:(e + 1) * P], G["q"][:, h, :], start=True, stop=False)
                            mm = pe.matmul(dst, G["lp"][:, h // 2, h % 2 * 2 + e, :], G["dt"][:, h, :], start=False, stop=True)
                    mm.then_inc(E["o"], 1)
                    for h in range(G4):
                        dst = ps[:, b + 2 + h // 2, h % 2 * DV:(h % 2 + 1) * DV]
                        vn = G["lp"][:, h // 2, h % 2 * 2:h % 2 * 2 + 2, :].rearrange("p a n -> p (a n)")
                        mm = pe.matmul(dst, G["k"][:, h, :], vn, start=True, stop=True)
                    mm.then_inc(E["sd"], 1)

            for g in range(2):
                pe.wait_ge(chunk[g]["oc"], 1 + NT)
                pe.wait_ge(chunk[g]["state"], 1 + NT)
            for i, slabs in groups(pe, dn_z):
                for r in slabs:
                    for m in range(2):
                        pe_tile(pe, dn_z, i, r, m, x_meta)
                    n = i * R + r
                    pe.wait_ge(o_sq, n + 1)
                    pe.wait_ge(o_rs, n + 1)
                    for e in range(2):
                        mm = pe.matmul(ps[:, 6, :], ones[:, :], NSQ[:, e, 0:SEQ], start=e == 0, stop=e == 1)
                    mm.then_inc(o_sum, 1)
            pe.wait_ge(z_done, 2 + 2 * HEADS)
            for i, slabs in groups(pe, sb_qk):
                for r in slabs:
                    for m in range(2):
                        t = 2 * r + m
                        pe_tile(pe, sb_qk, i, r, m, x_all, True)
                        if t:
                            head_pe(pe, sb_qk, i, t - 1, i * (2 * R) + (t - 1))
                head_pe(pe, sb_qk, i, 2 * R - 1, i * (2 * R) + (2 * R - 1))
            for t in range(2 * sb_v.nslab):
                b = sb_v.buf(t)
                pe.wait_ge(split_ready, sb_v.u0 + t + 1)
                pe.wait_ge(acc_free[b], sb_v.free(t))
                for n in range(NT + 1):
                    m, c0 = (P, META + n * P) if n < NT else (META, 0)
                    dst = ps[0:m, 2 * b + n // NT, n % NT * P:(n % NT + 1) * P]
                    for k in range(KD):
                        mm = products(pe, dst, [y[:, k, c0:c0 + m] for y in (HNH, HNL)], halves_of(sb_v, t, k), k == 0, k == KD - 1)
                mm.then_inc(acc_ready, 1)
            taken(pe, sb_v, 0, 2 * sb_v.nslab - 1)
            taken(pe, sb_v, 0, 2 * sb_v.nslab - 2)
            pe.wait_ge(h_done, 1 + 2 * HEADS)

            def sb_turn(i, par, more):
                n = i * 2 + par
                zs = sbz[:, par, :]
                if more:
                    sb_logits(pe, i, par + 1)
                pe.wait_ge(sb_n, n + 1)
                pe.wait_ge(sb_lw, n + 1)
                later = {0: (1, 3, 2), 4: (0, 1, 3, 2), 1: (3, 2), 3: (2,), 2: ()}
                for t, after in later.items():
                    c, q0, k0, m = SB[t]
                    dst = sb_bank(4, t)
                    mm = pe.matmul(dst, tril[0:m, 0:m], sb_keys(sbn, t), start=True, stop=not after)
                    for a in after:
                        qa = SB[a][1]
                        mm = pe.matmul(dst[:, qa - q0:], ones[:, 0:m], sb_keys(sbn, a), start=False, stop=a == after[-1])
                mm.then_inc(sb_c, 1)
                pe.wait_ge(sb_w, n + 1)
                pe.wait_ge(sb_v_in, n * 2 + 2)
                if more:
                    pe.wait_ge(sb_zs, n + 4)
                for a, t in enumerate((0, 4, 1, 3, 2)):
                    c, q0, k0, m = SB[t]
                    mm = pe.matmul(ps[:, 0, q0:SEQ], sbv[0:m, SB_V[t], :], sb_keys(zs, t), start=a == 0, stop=a == 4)
                mm.then_inc(sb_o, 1)

            sb_logits(pe, 0, 0)
            with pe.Fori(0, HEADS // 2 - 1) as i:
                sb_turn(i, 0, True)
                sb_turn(i, 1, True)
            sb_turn(HEADS // 2 - 1, 0, True)
            sb_turn(HEADS // 2 - 1, 1, False)
            pe.wait_ge(sb_oc, 2 + HEADS)
            pe_gemm(pe, gate_dn, x_meta)
            pe.wait_ge(split_x, NT)
            pe_gemm_pair(pe, branch_dn, lambda k: [y[:, :, k // 2, k % 2 * P:(k % 2 + 1) * P] for y in (VOH, VOL)])
            ada_after = lambda gm: lambda r: [ada_pe(pe, 0, c) for c in ada_units(gm, r)]
            pe_gemm(pe, gate_sb, x_meta, after=ada_after(gate_sb))
            pe.wait_ge(split_x, NT + KD)
            pe_gemm(pe, branch_sb, lambda k: (OSH[:, k, :], OSL[:, k, 0:SEQ]), after=ada_after(branch_sb))
            pe_gemm(pe, mix_out, lambda k: (MGH[:, k, :], MGL[:, k, :]), lambda k: (merged, k + 1), ada_after(mix_out),
                    norm_after(pe, 1))
            norm_pe(pe, 1, SEQ, [KD - 1])
            for i, slabs in groups(pe, ffn_in):
                for r in slabs:
                    for m in range(2):
                        pe_tile(pe, ffn_in, i, r, m, x_hn, ready=lambda k: (n_out, KD + k + 1))
                    for c in ada_units(ffn_in, r):
                        ada_pe(pe, i, c)
            x_act = lambda k: (AFH[:, k, :], AFL[:, k, :])

            def ffn_after(t):
                ada_after(ffn_out)(t)
                norm_after(pe, 2)(t)

            pe_gemm_pair(pe, ffn_out, x_act, lambda q: (f_split, KF // (2 - q)), ffn_after)

            norm_pe(pe, 2, SEQ, [KD - 1])
            pe.wait_ge(mod_done, 1)

            def qk_sum(t):
                pe.wait_ge(h_sq, 2 * HEADS + t + 1)
                pe.wait_ge(h_rs, 2 * HEADS + t + 1)
                pe.matmul(ps[:, 6, :], pair_ones, NSQ[:, t % 2, 0:SEQ], start=True, stop=True).then_inc(h_sum, 1)

            def qk_rot(t):
                pe.wait_ge(a_nrm, t + 1)
                if t:
                    pe.wait_ge(a_done, t)
                pe.matmul(ps[:, 7, :], rot, QG[:, t, :], start=True, stop=True).then_inc(a_rot, 1)

            for t in range(10):
                pe_tile(pe, gq_qk, t // (2 * R), t // 2 % R, t % 2, x_hn, ready=lambda k: (n_out, 2 * KD + k + 1))
                if t >= 1:
                    qk_sum(t - 1)
                if t >= 2:
                    qk_rot(t - 2)
            qk_sum(9)
            qk_rot(8)
            for t in range(2):
                b = gq_v.buf(t)
                pe.wait_ge(split_ready, gq_v.u0 + t + 1)
                pe.wait_ge(acc_free[b], gq_v.free(t))
                for n in range(NT):
                    for k in range(KD):
                        mm = products(pe, ps[:, 2 * b, n * P:(n + 1) * P], [y[:, k, n * P:(n + 1) * P] for y in (HNH, HNL)],
                                      halves_of(gq_v, t, k), k == 0, k == KD - 1)
                mm.then_inc(acc_ready, 1)
            qk_rot(9)
            for g in range(KVH):
                pe.wait_ge(a_done, 9 + g // 2)
                if g >= 2:
                    pe.wait_ge(a_dupc, g - 1)
                pe.matmul(ps[:, 4 + g % 2, :], (dup0, dup1)[g % 2], QG[:, 8 + g // 2, :], start=True, stop=True).then_inc(a_dup, 1)
            pe.wait_ge(a_dupc, KVH)
            taken(pe, gq_v, 0, 1)
            taken(pe, gq_v, 0, 0)

            def scores(g, j):
                n = g * 4 + j
                pe.wait_ge(a_qk, g * 2 + 2)
                pe.wait_ge(a_e, n + 1)
                x = slice(j % 2 * HD, (j % 2 + 1) * HD)
                for q in range(NT):
                    mm = pe.matmul(ps[:, q, :], qst[x, j // 2, q * P:(q + 1) * P], kst[x, :], start=True, stop=True)
                mm.then_inc(a_s, 1)

            def gq_turn(g, more):
                for j in range(4):
                    n = g * 4 + j
                    if j < 3:
                        scores(g, j + 1)
                    elif more:
                        scores(g + 1, 0)
                    pe.wait_ge(a_p, n + 1)
                    for q in range(NT):
                        pe.wait_ge(a_tc, n * NT + q + 1)
                        for kt in range(NT):
                            mm = pe.transpose(ps[:, 4 + q % 2, kt * P:(kt + 1) * P], PB[:, j % 2, q, kt * P:(kt + 1) * P], ident)
                        mm.then_inc(a_t, 1)
                    pe.wait_ge(a_tc, n * NT + NT + 2)
                    pe.wait_ge(a_v, g + 1)
                    pe.wait_ge(a_oc, g * 2 + j // 2 + 1)
                    x = slice(j % 2 * HD, (j % 2 + 1) * HD)
                    for kt in range(NT):
                        mm = pe.matmul(ps[x, 6 + j // 2, :], vst[:, kt, :], PTB[:, j % 2, kt, :], start=kt == 0, stop=kt == NT - 1)
                    mm.then_inc(a_o, 1)

            scores(0, 0)
            with pe.Fori(0, KVH - 1) as g:
                gq_turn(g, True)
            gq_turn(KVH - 1, False)
            pe.wait_ge(a_e, 1 + QH)
            pe.wait_ge(a_oc, 2 + QH // 2)
            pe_gemm(pe, gq_out, lambda k: (OGH[:, k, :], OGL[:, k, :]), lambda k: (split_x, NT + KD + k + 1), tile_after=norm_after(pe, 3))

            def pe_conv_ffn(l, u):
                norm_pe(pe, u, SEQ, [KD - 1])
                pe_gemm(pe, fc_in[l], x_hn, lambda k: (n_out, u * KD + k + 1))
                pe_gemm_pair(pe, fc_out[l], x_act, lambda q: (f_split, (l + 1) * KF + KF // (2 - q)), norm_after(pe, u + 1))

            pe_conv_ffn(0, 3)
            norm_pe(pe, 4, SEQ, [KD - 1])
            pe_gemm(pe, hy_in, x_hn, lambda k: (n_out, 4 * KD + k + 1))
            pe.wait_ge(y_in, 48)
            pe.matmul(ps[0:FW, 6, :], W1[:, :], POS[:, :], start=True, stop=True).then_inc(y_mlp, 1)
            pe.wait_ge(y_sin, 1)
            pe.matmul(ps[0:FW, 7, :], W2[:, :], A1[:, 0, :], start=True, stop=True).then_inc(y_mlp, 1)
            pe.wait_ge(y_sin, 2)
            taken(pe, hy_in, 2, 2 * R - 1)
            taken(pe, hy_in, 2, 2 * R - 2)
            even_odd = lambda x, n: x.rearrange("p (h i e) -> p e h i", e=2, h=2)[:, n // 2, n % 2, :]

            def filters(u, dh):
                pe.wait_ge(y_w, u * 32 + 32)
                if not isinstance(u, int) or u:
                    pe.wait_ge(y_kc, u * 2)

                def sums(t):
                    if t == 0 and (not isinstance(u, int) or u):
                        pe.wait_ge(y_zc, u * 2)
                    pe.wait_ge(y_ab, u * NT + t + 1)
                    for c in range(NT):
                        for s in range(2):
                            mm = pe.matmul(ps[:, 4, c:c + 1], AB[:, s, c * P:(c + 1) * P], ones[:, 0:1],
                                           start=t + c + s == 0, stop=t == NT - 1 and c == NT - 1 and s == 1,
                                           skip_group_check=True)
                    mm.then_inc(y_n, 1)

                for t in range(NT):
                    if t >= 2:
                        pe.wait_ge(y_pm, u * NT + t + 1)
                    for s in range(2):
                        mm = pe.matmul(ps[:, t % 2 * 2 + s, :], even_odd(A1[:, 1, :], t), W3[:, s, :], start=True, stop=True)
                    mm.then_inc(y_f, 1)
                    if t:
                        sums(t - 1)
                sums(NT - 1)

            def hyena_pair(o, more):
                for dh in range(2):
                    u = o * 2 + dh
                    pe.wait_ge(y_z, u * NT + 1)
                    pe.wait_ge(y_rn, u + 1)
                    for t in range(NT):
                        if t >= 2:
                            pe.wait_ge(y_tc, u * NT + t - 1)
                        for c in range(NT):
                            mm = pe.transpose(ps[:, 4 + t % 2, c * P:(c + 1) * P], even_odd(U[:, dh * NT + c, :], t), ident)
                        mm.then_inc(y_t, 1)
                    pe.wait_ge(y_pm, u * NT + NT + 2)
                    for f in range(2):
                        fs = slice(f * P, (f + 1) * P)
                        if f:
                            pe.wait_ge(y_kc, u * 2 + f)
                        for s in range(2):
                            for t in range(NT):
                                mm = pe.matmul(ps[:, s * 2 + t // 2, :], t_fwd[:, s, t, fs], PM[:, s, t, :],
                                               start=t % 2 == 0, stop=t % 2 == 1)
                        mm.then_inc(y_k, 1)
                        pe.wait_ge(y_tc, u * NT + NT)
                        pe.wait_ge(y_z, u * NT + 5)
                        if f:
                            pe.wait_ge(y_zc, u * 2 + f)
                            pe.wait_ge(y_x, u * 2 + f + 1)
                        for s in range(2):
                            for t in range(NT):
                                mm = pe.matmul(ps[:, 4 + s * 2 + t // 2, :], t_fwd[:, s, t, fs], ZK[:, t, :],
                                               start=t % 2 == 0, stop=t % 2 == 1)
                        mm.then_inc(y_dft, 1)
                    if dh == 0 or more:
                        filters(u + 1, 1 - dh)
                    pe.wait_ge(y_y, u * 2 + 3)
                    for c in range(NT):
                        if c >= 2:
                            pe.wait_ge(y_z, u * NT + c + 4)
                        for e in range(2):
                            ts = slice(e * SEQ // 2, (e + 1) * SEQ // 2)
                            for f in range(2):
                                for s in range(2):
                                    mm = pe.matmul(ps[:, 6 + c % 2, ts], YF[:, f, e * 2 + s, c * P:(c + 1) * P], t_inv[:, s, f, ts],
                                                   start=f + s == 0, stop=f + s == 2)
                        mm.then_inc(y_inv, 1)

            pe.wait_ge(y_conv, 3 * KD)
            pe.wait_ge(table_full, 32)
            hyena_units(pe, lambda: filters(0, 0), hyena_pair)
            pe_gemm(pe, hy_out, lambda k: (ZH[:, k, :], ZL[:, k, :]), lambda k: (split_x, NT + 2 * KD + k + 1), tile_after=norm_after(pe, 5))
            pe_conv_ffn(1, 5)
            norm_pe(pe, 6, SEQ, [KD - 1])
            for n in range(NT):
                for h in range(2):
                    pe.wait_ge(n_out, 6 * KD + (KD if n else 4 * (h + 1)))
                    if n >= 1:
                        pe.wait_ge(f_out, 2 * n + h - 1)
                    for k in range(4):
                        mm = pe.transpose(ps[:, 4 + h, k * P:(k + 1) * P], HN[:, 4 * h + k, n * P:(n + 1) * P], ident)
                    mm.then_inc(f_t, 1)

        @block.scalar
        def _(act):
            act.sem_inc(silu_done, 2)
            act.sem_inc(l2_rs, 1)
            act.sem_inc(o_rs, 1)
            act.sem_inc(h_rs, 1)
            act.sem_inc(sb_zs, 2)
            act.sem_inc(sb_oc, 2)
            act.sem_inc(a_e, 1)
            act.sem_inc(a_tc, 2)
            act.sem_inc(a_oc, 2)
            for g in range(2):
                act.sem_inc(chunk[g]["oc"], 1)
            act.wait_ge(t_done, 2 * KD + 1)
            act.wait_ge(cleared, 1)
            norm_act(act, 0, lambda k: H[:, k, :], T)
            act.wait_ge(ab_x, 1)
            act.activation(soft[:, 1, :, 0:8], soft[:, 1, :, 0:8], ACT.Exp, bias=zero, scale=-1.0)
            act.drain()
            act.activation(soft[:, 1, :, 0:8], soft[:, 1, :, 0:8], ACT.Ln, bias=ones[:, 0:1], scale=1.0)
            act.activation(ab[:, 0:8], ab[:, 0:8], ACT.Exp, bias=zero, scale=1.0)
            act.activation(b_tok[:, :, :], soft[:, 0, :, 8:16], ACT.Sigmoid, bias=zero, scale=1.0).then_inc(ab_l, 1)

            def conv_in(gm, i, t):
                b = acc_in(act, gm, i, t)
                act.activation(split(xpad[:, t % 2, 3:3 + T]), half(2 * b), ACT.Copy).then_inc(acc_free[b], 1)

            for i, slabs in groups(act, dn_qk):
                for t in range(2 * R):
                    conv_in(dn_qk, i, t)
                    act.wait_ge(conv_done, i * (2 * R) + t + 1)
                    act.activation(QK[:, ds(i * (2 * R) + t, 1), :], cv[:, t % 2:t % 2 + 1, :], ACT.Silu)\
                        .then_inc(silu_done, 1)
            for i, slabs in groups(act, dn_v):
                for t in range(2 * R):
                    n = i * (2 * R) + t
                    act.wait_ge(silu_done, 2 + 16)
                    act.wait_ge(l2_sum, n + 1)
                    act.activation(NSQ[:, t % 2:t % 2 + 1, :], QK[:, ds(n, 1), :], ACT.Square).then_inc(l2_sq, 1)
                    conv_in(dn_v, i, t)
                    act.preload_act_table_set(SILU)
                    act.wait_ge(conv_done, n + 17)
                    act.activation(cv[:, t % 2, :], cv[:, t % 2, :], ACT.Silu).then_inc(silu_done, 1)
                    act.preload_act_table_set(LN_EXP)
                    act.wait_ge(l2_sum, n + 3)
                    act.wait_ge(l2_done, n + 1)
                    act.activation(split(RSB[:, :]), half(4), ACT.Ln, bias=eps, scale=1.0)
                    act.drain()
                    act.activation(RSB[:, :], RSB[:, :], ACT.Exp, bias=zero, scale=-0.5).then_inc(l2_rs, 1)

            act.wait_ge(m_dve, 3)
            act.activation(ml[:, :, :], ml[:, :, :], ACT.Exp, bias=zero[0:META], scale=1.0)
            act.activation(msm[:, 1, :], msm[:, 1, :], ACT.Exp, bias=zero[0:META], scale=1.0).then_inc(m_act, 1)
            with act.Fori(0, NT) as c:
                for g in range(2):
                    G, E, b = group[g], chunk[g], 4 * g
                    act.wait_ge(E["expin"], c + 1)
                    act.activation(G["dt"][:, :, :], G["dt"][:, :, :], ACT.Exp, bias=zero, scale=1.0)
                    act.activation(G["lp"][:, 0, :, :], G["lp"][:, 0, :, :], ACT.Exp, bias=zero, scale=1.0)
                    act.activation(G["x"][:, :, :], ps[:, b, :].rearrange("p (h n) -> p h n", h=G4), ACT.Exp, bias=zero, scale=1.0)
                    act.activation(G["sm"][:, 2:4, :], G["sm"][:, 0:2, :], ACT.Exp, bias=zero, scale=1.0).then_inc(E["expd"], 1)
                for l in range(1, LEVELS):
                    for g in range(2):
                        G, E, b = group[g], chunk[g], 4 * g
                        act.wait_ge(E["prod"], c * LEVELS + l + 1)
                        act.activation(G["lp"][:, 1, :, :], ps[:, b, :].rearrange("p (h n) -> p h n", h=G4), ACT.Copy)\
                            .then_inc(E["pcopy"], 1)
                for g in range(2):
                    G, E, b = group[g], chunk[g], 4 * g
                    act.wait_ge(E["wt"], c + 1)
                    act.activation(G["x"][:, :, :], ps[:, b, :].rearrange("p (h n) -> p h n", h=G4), ACT.Copy, scale=-1.0)\
                        .then_inc(E["nw"], 1)
                for g in range(2):
                    G, E, b = group[g], chunk[g], 4 * g
                    act.wait_ge(E["vn"], c + 1)
                    act.activation(G["lp"][:, :, :, :].rearrange("p a h n -> p a (h n)"), ps[:, b + 2:b + 4, :], ACT.Copy)\
                        .then_inc(E["vnc"], 1)
                for g in range(2):
                    G, E, b = group[g], chunk[g], 4 * g
                    act.wait_ge(E["o"], c + 1)
                    act.activation(VO[:, ds(c, 1), g * G4:(g + 1) * G4, :].rearrange("p c h n -> p (c h n)"),
                                   ps[:, b:b + 2, :].rearrange("p a n -> p (a n)"), ACT.Copy).then_inc(E["oc"], 1)

            act.drain()
            for i, slabs in groups(act, dn_z):
                for t in range(2 * R):
                    n = i * R + t // 2
                    if t % 2 == 0:
                        if t:
                            act.wait_ge(o_sum, n)
                        act.activation(NSQ[:, :, 0:SEQ].rearrange("p e (c n) -> p e c n", n=P),
                                       VO[:, :, ds(n, 1), :].rearrange("p c a (e n) -> p e (c a) n", e=2), ACT.Square)\
                            .then_inc(o_sq, 1)
                    act.wait_ge(z_done, i * (2 * R) + t + 1)
                    b = acc_in(act, dn_z, i, t)
                    act.activation(ZT[:, t % 2, :], ps[:, 2 * b, :], ACT.Silu).then_inc(acc_free[b], 1)
                    if t % 2 == 0:
                        act.preload_act_table_set(LN_EXP)
                        act.wait_ge(o_sum, n + 1)
                        act.wait_ge(z_done, n * 2 + 2)
                        act.activation(NRS[:, 0:SEQ], ps[:, 6, :], ACT.Ln, bias=eps, scale=1.0 / DV)
                        act.drain()
                        act.activation(NRS[:, 0:SEQ], NRS[:, 0:SEQ], ACT.Exp, bias=zero, scale=-0.5).then_inc(o_rs, 1)

            def head_rs(i, t, scale):
                n = i * (2 * R) + t
                act.wait_ge(h_sum, n + 3)
                act.wait_ge(h_done, n + 1)
                act.activation(split(NRS[:, :]), half(6), ACT.Ln, bias=eps, scale=scale)
                act.drain()
                act.activation(NRS[:, :], NRS[:, :], ACT.Exp, bias=zero, scale=-0.5).then_inc(h_rs, 1)

            act.preload_act_table_set(LN_EXP)
            act.wait_ge(z_done, 2 + 2 * HEADS)
            for i, slabs in groups(act, sb_qk):
                for t in range(2 * R):
                    n = i * (2 * R) + t
                    act.wait_ge(h_sum, n + 1)
                    b = acc_in(act, sb_qk, i, t)
                    act.activation(split(NSQ[:, t % 2, :]), half(2 * b), ACT.Square).then_inc(h_sq, 1)
                    act.activation(split(QSK[:, ds(n, 1), :].rearrange("p a n -> p (a n)")), half(2 * b), ACT.Copy)\
                        .then_inc(acc_free[b], 1)
                    if t:
                        head_rs(i, t - 1, 1.0 / P)
                head_rs(i, 2 * R - 1, 1.0 / P)

            def sb_evac(n, par):
                act.wait_ge(sb_z, n + 1)
                if not isinstance(n, int) or n:
                    act.wait_ge(sb_o, n)
                s = float(P) ** -0.5
                act.activation(sbz[:, par, 0:8 * P].rearrange("p (a n) -> p a n", a=2), ps[:, 0:2, :], ACT.Copy, scale=s)
                act.activation(sbz[:, par, 8 * P:SBX], ps[:, 2, 0:2 * P], ACT.Copy, scale=s)
                act.activation(sbz[0:META, par, SBX:SBW], ps[0:META, 3, :], ACT.Copy, scale=s).then_inc(sb_zs, 1)

            def sb_log(n):
                act.wait_ge(sb_abs, n + 1)
                act.activation(sbe[:, :], sbe[:, :], ACT.Exp, bias=zero, scale=-1.0)
                act.drain()
                act.activation(sbe[:, :], sbe[:, :], ACT.Ln, bias=ones[:, 0:1], scale=1.0).then_inc(sb_ln, 1)

            def sb_turn(i, par, more):
                n = i * 2 + par
                if more:
                    sb_evac(n + 1, 1 - par)
                    sb_log(n + 1)
                act.wait_ge(sb_lw, n + 2)
                act.activation(sbz[:, par, 0:SBX], sbz[:, par, 0:SBX], ACT.Exp, bias=zero, scale=1.0)
                act.activation(sbz[0:META, par, SBX:SBW], sbz[0:META, par, SBX:SBW], ACT.Exp, bias=zero[0:META], scale=1.0)\
                    .then_inc(sb_w, 1)
                act.wait_ge(sb_o, n + 2)
                act.activation(QSK[:, ds(n, 1), 0:SEQ].rearrange("p a n -> p (a n)"), ps[:, 0, :], ACT.Copy).then_inc(sb_oc, 1)

            act.wait_ge(sv_done, 4 * (NT + 1) + 1)
            sb_evac(0, 0)
            sb_log(0)
            with act.Fori(0, HEADS // 2 - 1) as i:
                sb_turn(i, 0, True)
                sb_turn(i, 1, True)
            sb_turn(HEADS // 2 - 1, 0, True)
            sb_turn(HEADS // 2 - 1, 1, False)
            act.activation(csil[:, :], cols("c", 0, KD), ACT.Silu).then_inc(silu_c, 1)
            for t in range(KD):
                b = acc_in(act, gate_dn, 0, t)
                act.activation(MG[:, t, :], ps[:, 2 * b, :], ACT.Sigmoid).then_inc(acc_free[b], 1)
            for t in range(KD):
                taken(act, branch_dn, t // R, t % R)
                b = acc_in(act, gate_sb, 0, t)
                act.activation(GT[:, t, :], ps[:, 2 * b, :], ACT.Sigmoid).then_inc(acc_free[b], 1)
            norm_act(act, 1, lambda k: H[:, k, META:T], SEQ, tile=lambda k: taken(act, mix_out, 0, k))
            for i, slabs in groups(act, ffn_in):
                for r in slabs:
                    taken(act, ffn_in, i, 2 * r - 3)
                    b = acc_in(act, ffn_in, i, 2 * r)
                    act.activation(SG[:, r % 2, :], ps[:, 2 * b, :], ACT.Silu).then_inc(acc_free[b], 1)

            def residual(gm):
                return lambda k: taken(act, gm, 0, k)

            norm_act(act, 2, lambda k: H[:, k, META:T], SEQ, shift_of(0, 0), tile=residual(ffn_out))

            def qk_rs(t):
                act.wait_ge(h_sum, 2 + 2 * HEADS + t + 1)
                act.wait_ge(h_done, 1 + 2 * HEADS + t)
                act.activation(NRS[:, 0:SEQ], ps[:, 6, :], ACT.Ln, bias=eps, scale=1.0 / HD)
                act.drain()
                act.activation(NRS[:, 0:SEQ], NRS[:, 0:SEQ], ACT.Exp, bias=zero, scale=-0.5).then_inc(h_rs, 1)

            act.wait_ge(n_out, 3 * KD)
            for t in range(10):
                i, tt = t // (2 * R), t % (2 * R)
                act.wait_ge(h_sum, 2 * HEADS + t + 1)
                b = acc_in(act, gq_qk, i, tt)
                act.activation(NSQ[:, t % 2, 0:SEQ], ps[:, 2 * b, :], ACT.Square).then_inc(h_sq, 1)
                act.activation(QG[:, t, :], ps[:, 2 * b, :], ACT.Copy).then_inc(acc_free[b], 1)
                if t:
                    qk_rs(t - 1)
            qk_rs(9)
            for g in range(KVH):
                act.wait_ge(a_dup, g + 1)
                act.activation(KDUP[:, g, :], ps[:, 4 + g % 2, :], ACT.Copy).then_inc(a_dupc, 1)

            def exps(g, j):
                n = g * 4 + j
                act.wait_ge(a_mx, n + 1)
                act.wait_ge(a_t, n * NT + 1)
                for q in range(NT):
                    ins = act.activation(PB[:, j % 2, q, :], ps[:, q, :], ACT.Exp, bias=asm[:, j % 2, 1, q:q + 1],
                                         scale=float(HD) ** -0.5, accum_out=asm[:, j % 2, 2, q:q + 1])
                ins.then_inc(a_e, 1)

            def gq_turn(g, more):
                for j in range(4):
                    n = g * 4 + j
                    act.wait_ge(a_o, n + 1)
                    for q in range(NT):
                        act.wait_ge(a_t, n * NT + q + 6)
                        act.activation(PTB[:, j % 2, :, q * P:(q + 1) * P], ps[:, 4 + q % 2, :].rearrange("p (k n) -> p k n", k=NT),
                                       ACT.Copy).then_inc(a_tc, 1)
                    if j < 3:
                        exps(g, j + 1)
                    elif more:
                        exps(g + 1, 0)
                    if j % 2:
                        act.wait_ge(a_o, n + 3)
                        o = lambda x: x[:, ds(g * 2 + j // 2, 1), :].rearrange("p a n -> p (a n)")
                        act.activation(o(OG), ps[:, 6 + j // 2, :], ACT.Copy)
                        act.activation(o(OGH), ps[:, 6 + j // 2, :], ACT.Copy).then_inc(a_oc, 1)

            exps(0, 0)
            with act.Fori(0, KVH - 1) as g:
                gq_turn(g, True)
            gq_turn(KVH - 1, False)

            def act_conv_ffn(l, u):
                norm_act(act, u, lambda k: H[:, k, META:T], SEQ, shift_of(l, 1), tile=residual((gq_out, hy_out)[l]))
                act.wait_ge(n_out, (u + 1) * KD)
                for i, slabs in groups(act, fc_in[l]):
                    for r in slabs:
                        b = acc_in(act, fc_in[l], i, 2 * r)
                        act.activation(GP[:, r % 2, 1:SEQ + 1], ps[:, 2 * b, :], ACT.Copy).then_inc(acc_free[b], 1)
                        act.wait_ge(fc_conv, i * R + (l * KF + r + 1))
                        act.activation(SG[:, r % 2, :], SG[:, r % 2, :], ACT.Silu).then_inc(fc_silu, 1)

            act_conv_ffn(0, 3)
            norm_act(act, 4, lambda k: H[:, k, META:T], SEQ, shift_of(1, 0), tile=residual(fc_out[0]))
            act.wait_ge(n_out, 5 * KD)
            for i, slabs in groups(act, hy_in):
                for t in range(2 * R):
                    if t >= 2:
                        act.wait_ge(y_conv, i * (2 * R) + (t - 1))
                    b = acc_in(act, hy_in, i, t)
                    act.activation(UP[:, t % 2, 1:SEQ + 1], ps[:, 2 * b, :], ACT.Copy).then_inc(acc_free[b], 1)
                act.wait_ge(y_conv, i * (2 * R) + 2 * R)
            for n in range(2):
                act.wait_ge(y_arg, n + 1)
                act.activation(A1[:, n, :], A1[:, n, :], ACT.Sin, bias=zero[0:FW], scale=1.0).then_inc(y_sin, 1)

            def filters(u):
                for t in range(NT):
                    act.wait_ge(y_fb, u * NT + t + 1)
                    if t:
                        act.wait_ge(y_n, u * NT + t)
                    act.activation(AB[:, :, :], FB[:, :, :], ACT.Abs).then_inc(y_ab, 1)

            def hyena_pair(o, more):
                for dh in range(2):
                    u = o * 2 + dh
                    for t in range(NT):
                        act.wait_ge(y_t, u * NT + t + 1)
                        act.activation(ZK[:, t, :], ps[:, 4 + t % 2, :], ACT.Copy).then_inc(y_tc, 1)
                    for f in range(2):
                        act.wait_ge(y_k, u * 2 + f + 1)
                        act.wait_ge(y_kp, u * 2 + f + 1)
                        act.activation(KS[:, :, :], ps[:, 0:4, :], ACT.Copy).then_inc(y_kc, 1)
                        act.wait_ge(y_dft, u * 2 + f + 1)
                        act.wait_ge(y_x, u * 2 + f + 1)
                        act.activation(ZS[:, :, :], ps[:, 4:8:2, :], ACT.Copy).then_inc(y_zc, 1)
                    if dh == 0 or more:
                        filters(u + 1)

            hyena_units(act, lambda: filters(0), hyena_pair)
            act_conv_ffn(1, 5)
            norm_act(act, 6, lambda k: H[:, k, META:T], SEQ, hi=False, tile=residual(fc_out[1]))
            for n in range(NT):
                act.wait_ge(f_out, 2 * n + 2)
                act.dma_start(out[n * P:(n + 1) * P, :], OUT[:, n, :]).then_inc(stored, 16)
            act.wait_ge(stored, 16 * NT)

        @block.vector
        def _(dve):
            for b in range(2):
                dve.sem_inc(acc_free[b], 1)
            dve.sem_inc(vt_done, 2)
            dve.sem_inc(l2_done, 1)
            dve.sem_inc(z_done, 2)
            dve.sem_inc(h_done, 1)
            dve.sem_inc(sb_lw, 1)
            dve.sem_inc(y_pm, 2)
            dve.sem_inc(y_z, 1 + NT)
            dve.sem_inc(y_x, 1)
            dve.sem_inc(y_cb, 2)
            for k in range(KD):
                dve.wait_ge(t_ready, 2 * k + 1)
                dve.tensor_copy(H[:, k, META:T], ps[:, k % 2, :]).then_inc(t_done, 1)
                dve.wait_ge(t_ready, 2 * k + 2)
                dve.tensor_copy(H[:, k, 0:META], ps[:, 2 + k % 2, 0:META]).then_inc(t_done, 1)
            dve.wait_ge(t_ready, 2 * KD + 1)
            dve.tensor_copy(pcol[:, :, :].rearrange("p a b -> p (a b)"),
                            ps[:, 4:6, :].rearrange("p a b -> p (a b)")[:, 0:PT * P]).then_inc(t_done, 1)
            dve.memset(soft[:, :, :, :], 0.0)
            dve.drain()
            norm_dve(dve, 0, lambda k: H[:, k, :], lambda k: col("norm_mix", k), T)
            dve.wait_ge(ab_ready, 1)
            dve.tensor_copy(soft[:, 0, 0:NT, :], ps[:, 4, 0:NT * 16].rearrange("p (n c) -> p n c", c=16))
            dve.tensor_copy(soft[0:META, 0, NT, :], ps[0:META, 4, NT * 16:(NT + 1) * 16])
            dve.tensor_copy(ab[:, :], ps[:, 5, 0:16])
            dve.drain()
            dve.tensor_tensor(soft[:, 0, :, 0:8], soft[:, 0, :, 0:8], heads_of(ab[:, 8:16], NT + 1), ALU.add)
            dve.drain()
            dve.scalar_tensor_tensor(soft[:, 1, :, 0:8], soft[:, 0, :, 0:8], -1.0, soft[:, 0, :, 0:8], ALU.mult, ALU.max)\
                .then_inc(ab_x, 1)
            dve.wait_ge(ab_l, 1)
            dve.scalar_tensor_tensor(soft[:, 0, :, 0:8], soft[:, 0, :, 0:8], 0.0, soft[:, 1, :, 0:8], ALU.max, ALU.add)
            dve.drain()
            dve.scalar_tensor_tensor(g_tok[:, :, :], soft[:, 0, :, 0:8], -1.0, heads_of(ab[:, 0:8], NT + 1), ALU.mult, ALU.mult)

            def conv(gm, i, t, taps):
                taken(dve, gm, i, t)
                x, y = xpad[:, t % 2, :], cv[:, t % 2, :]
                dve.tensor_scalar(y, x[:, 0:T], taps(0), None, ALU.mult)
                for j in range(1, 4):
                    dve.drain()
                    ins = dve.scalar_tensor_tensor(y, x[:, j:j + T], taps(j), y, ALU.mult, ALU.add)
                ins.then_inc(conv_done, 1)

            for i, slabs in groups(dve, dn_qk):
                for t in range(2 * R):
                    dve.wait_ge(silu_done, i * (2 * R) + t + 1)
                    conv(dn_qk, i, t, lambda j: dcol("conv_q", i * 32 + (j * 8 + t)))

            def v_out(i, t):
                n = i * (2 * R) + t
                dve.wait_ge(vt_ready, n * 2 + 4 + 1)
                dve.tensor_copy(VO[:, :, :, :].rearrange("p c h (e n) -> p c (h e) n", e=2)[:, :, ds(n, 1), :],
                                ps[:, 6, :].rearrange("p (c a n) -> p c a n", c=NT, a=1)).then_inc(vt_done, 1)
                dve.wait_ge(vt_ready, n * 2 + 4 + 2)
                dve.tensor_copy(vm[:, :, :].rearrange("p h (e n) -> p (h e) n", e=2)[:, ds(n, 1), :],
                                ps[0:META, 7, 0:P].unsqueeze(1)).then_inc(vt_done, 1)

            for i, slabs in groups(dve, dn_v):
                for t in range(2 * R):
                    n = i * (2 * R) + t
                    dve.wait_ge(silu_done, n + 16 + 1)
                    dve.wait_ge(vt_ready, n * 2 + 2)
                    conv(dn_v, i, t, lambda j: dcol("conv_v", i * 8 + (j * 16 + t)))
                    dve.wait_ge(l2_rs, n + 2)
                    dve.tensor_tensor(QK[:, ds(n, 1), :], QK[:, ds(n, 1), :], RSB[:, :].unsqueeze(1), ALU.mult)\
                        .then_inc(l2_done, 1)
                    if t:
                        v_out(i, t - 1)
                v_out(i, 2 * R - 1)

            m = META
            dve.drain()
            dve.tensor_copy(gmb[:, :, :], wide(g_tok[0:m, NT, :], m)).then_inc(m_dve, 1)
            dve.wait_ge(m_pe, 1)
            dve.wait_ge(mask_in, 16)
            dve.tensor_copy(msm[:, 0, :], ps[0:m, 1, 0:HEADS])
            dve.drain()
            h16 = lambda b: ps[0:m, b, 0:HEADS * m].rearrange("p (h n) -> p h n", h=HEADS)
            dve.tensor_tensor(ml[:, :, :], wide(msm[:, 0, :], m), h16(0), ALU.subtract)
            dve.tensor_tensor(msm[:, 1, :], h16(0)[:, :, m - 1], msm[:, 0, :], ALU.subtract).then_inc(m_dve, 1)
            dve.drain()
            dve.tensor_tensor(ml[:, :, :], ml[:, :, :], heads_of(masks[0:m, 1, 0:m], HEADS), ALU.add).then_inc(m_dve, 1)
            dve.wait_ge(m_act, 1)
            dve.tensor_tensor(ml[:, :, :], ml[:, :, :], wide(b_tok[0:m, NT, :], m), ALU.mult)
            dve.drain()
            dve.tensor_tensor(ml[:, :, :], ml[:, :, :], h16(2), ALU.mult)
            dve.drain()
            for l in range(4):
                dve.tensor_tensor(mlm[:, :, :], ml[:, :, :], heads_of(masks[0:m, 2 + l, 0:m], HEADS), ALU.mult)\
                    .then_inc(m_dve, 1)
                dve.wait_ge(m_pe, 2 * l + 2 - (1 if l else 0))
                if l == 0:
                    idn = heads_of(ident[0:m, 0:m], HEADS)
                    dve.tensor_tensor(mx[:, :, :], idn, mlm[:, :, :], ALU.subtract).then_inc(m_dve, 1)
                    dve.tensor_tensor(my[:, :, :], idn, h16(0), ALU.subtract).then_inc(m_dve, 1)
                else:
                    dve.tensor_copy(mp[:, :, :], h16(0)).then_inc(m_dve, 1)
                    dve.wait_ge(m_pe, 2 * l + 2)
                    dve.tensor_tensor(my[:, :, :], my[:, :, :], h16(1), ALU.subtract)
                    dve.tensor_tensor(mx[:, :, :], mx[:, :, :], h16(2), ALU.subtract).then_inc(m_dve, 1)
                dve.drain()
            kt = lambda: ps[0:m, 3:5, :].rearrange("p a (h n) -> p (a h) n", n=P)
            dve.tensor_tensor(km[:, :, :], kt(), wide(msm[:, 1, :]), ALU.mult)
            dve.tensor_tensor(vmb[:, :, :], vm[:, :, :], wide(b_tok[0:m, NT, :], DV), ALU.mult).then_inc(m_dve, 1)
            dve.wait_ge(m_pe, 9)
            dve.tensor_copy(vm[:, :, :], ps[0:m, 4:8, :].rearrange("p a (h n) -> p (a h) n", n=DV)).then_inc(m_dve, 1)
            dve.wait_ge(m_pe, 10)
            dve.tensor_copy(S[:, :, :], ps[:, 0:4, :].rearrange("p a (h n) -> p (a h) n", n=DV)).then_inc(m_dve, 1)
            dve.drain()
            for g in range(2):
                dve.sem_inc(chunk[g]["state"], 1)
            with dve.Fori(0, NT) as c:
                for g in range(2):
                    G, E, b = group[g], chunk[g], 4 * g
                    hs = slice(g * G4, (g + 1) * G4)
                    dve.tensor_copy(G["k"][:, :, :], KC[:, hs, ds(c * P + META, P)])
                    dve.tensor_scalar(G["q"][:, :, :], QC[:, hs, ds(c * P + META, P)], float(P) ** -0.5, None, ALU.mult)
                    dve.tensor_copy(G["sm"][:, 6, :], b_tok[:, ds(c, 1), hs].rearrange("p c h -> p (c h)"))
                    dve.tensor_copy(G["sm"][:, 7, :], g_tok[:, ds(c, 1), hs].rearrange("p c h -> p (c h)"))
                    dve.drain()
                    dve.tensor_copy(G["gb"][:, :, :], wide(G["sm"][:, 7, :])).then_inc(E["staged"], 1)
                for g in range(2):
                    G, E, b = group[g], chunk[g], 4 * g
                    h4 = lambda bb: ps[:, bb, :].rearrange("p (h n) -> p h n", h=G4)
                    dve.wait_ge(E["gates"], c + 1)
                    dve.tensor_copy(G["sm"][:, 0, :], ps[:, b + 1, 0:G4])
                    dve.drain()
                    dve.tensor_tensor(G["dt"][:, :, :], h4(b), wide(G["sm"][:, 0, :]), ALU.subtract)
                    dve.tensor_tensor(G["sm"][:, 1, :], h4(b)[:, :, P - 1], G["sm"][:, 0, :], ALU.subtract)
                    dve.drain()
                    dve.tensor_tensor(G["lp"][:, 0, :, :], heads_of(masks[:, 1, :], G4), G["dt"][:, :, :], ALU.subtract)
                    dve.tensor_tensor(G["dt"][:, :, :], G["dt"][:, :, :], heads_of(masks[:, 0, :], G4), ALU.add)\
                        .then_inc(E["expin"], 1)
                for g in range(2):
                    G, E, b = group[g], chunk[g], 4 * g
                    h4 = lambda bb: ps[:, bb, :].rearrange("p (h n) -> p h n", h=G4)
                    dve.wait_ge(E["expd"], c + 1)
                    dve.tensor_tensor(G["lp"][:, 0, :, :], G["lp"][:, 0, :, :], wide(G["sm"][:, 6, :]), ALU.mult)
                    dve.tensor_tensor(G["dt"][:, :, :], G["dt"][:, :, :], h4(b + 3), ALU.mult)
                    dve.tensor_tensor(G["sm"][:, 4, :], G["sm"][:, 6, :], G["sm"][:, 2, :], ALU.mult)
                    dve.tensor_tensor(G["q"][:, :, :], G["q"][:, :, :], G["x"][:, :, :], ALU.mult)
                    dve.tensor_copy(G["sm"][:, 5, :], G["x"][:, :, P - 1])
                    dve.drain()
                    dve.tensor_tensor(G["lp"][:, 0, :, :], G["lp"][:, 0, :, :], h4(b + 2), ALU.mult).then_inc(E["lower"], 1)
                for l in range(LEVELS):
                    for g in range(2):
                        G, E, b = group[g], chunk[g], 4 * g
                        h4 = lambda bb: ps[:, bb, :].rearrange("p (h n) -> p h n", h=G4)
                        if l == 0:
                            dve.wait_ge(E["prod"], c * LEVELS + 1)
                            idn = heads_of(ident, G4)
                            dve.tensor_tensor(G["x"][:, :, :], idn, G["lm"][:, 0, :, :], ALU.subtract)
                            dve.tensor_tensor(G["y"][:, :, :], idn, h4(b), ALU.subtract).then_inc(E["inv"], 1)
                            dve.wait_ge(E["ktok"], c + 1)
                            dve.tensor_tensor(G["gb"][:, :, :], h4(b + 1), wide(G["sm"][:, 4, :]), ALU.mult)
                            dve.tensor_tensor(G["k"][:, :, :], h4(b + 1), wide(G["sm"][:, 3, :]), ALU.mult)\
                                .then_inc(E["kbg"], 1)
                        else:
                            dve.wait_ge(E["delta"], c * (LEVELS - 1) + l)
                            if l < LEVELS - 1:
                                dve.tensor_tensor(G["x"][:, :, :], G["x"][:, :, :], h4(b + 3), ALU.subtract)
                            dve.tensor_tensor(G["y"][:, :, :], G["y"][:, :, :], h4(b + 2), ALU.subtract).then_inc(E["inv"], 1)
                        if l == LEVELS - 1:
                            vb = G["lm"][:, :, :, :].rearrange("p a h n -> p (a h n)").rearrange("p (h n) -> p h n", h=G4)
                            vsrc = VO[:, ds(c, 1), g * G4:(g + 1) * G4, :].rearrange("p c h n -> p (c h) n")
                            dve.tensor_tensor(vb, vsrc, wide(G["sm"][:, 6, :], DV), ALU.mult).then_inc(E["vb"], 1)
                for g in range(2):
                    G, E, b = group[g], chunk[g], 4 * g
                    dve.wait_ge(E["sd"], c + 1)
                    for h in range(G4):
                        Sh = S[:, g * G4 + h, :]
                        ins = dve.scalar_tensor_tensor(Sh, Sh, G["sm"][:, 5, h:h + 1],
                                                       ps[:, b + 2 + h // 2, h % 2 * DV:(h % 2 + 1) * DV], ALU.mult, ALU.add)
                    ins.then_inc(E["state"], 1)

            for i, slabs in groups(dve, dn_z):
                for t in range(2 * R):
                    n = i * R + t // 2
                    e = t % 2
                    if e == 0:
                        dve.wait_ge(o_rs, n + 2)
                    taken(dve, dn_z, i, t)
                    dve.scalar_tensor_tensor(ZT[:, e, :], ZT[:, e, :], col("dn_gain", e), NRS[:, 0:SEQ], ALU.mult, ALU.mult)
                    dve.drain()
                    o = VO[:, :, ds(n, 1), e * P:(e + 1) * P].rearrange("p c a n -> p c (a n)")
                    dve.tensor_tensor(o, o, ZT[:, e, :].rearrange("p (c n) -> p c n", c=NT), ALU.mult).then_inc(z_done, 1)
            for i, slabs in groups(dve, sb_qk):
                for t in range(2 * R):
                    n = i * (2 * R) + t
                    dve.wait_ge(h_rs, n + 2)
                    qk = QSK[:, ds(n, 1), :]
                    dve.scalar_tensor_tensor(qk, qk, dcol("sbq", i) if not isinstance(i, int) else col("sbq", i),
                                             NRS[:, :].unsqueeze(1), ALU.mult, ALU.mult).then_inc(h_done, 1)
            for t in range(2 * sb_v.nslab):
                b = acc_in(dve, sb_v, 0, t)
                dve.tensor_copy(SV[:, 0:NT, t * P:(t + 1) * P], ps[:, 2 * b, :].rearrange("p (n c) -> p n c", n=NT))
                dve.tensor_copy(SV[0:META, NT, t * P:(t + 1) * P], ps[0:META, 2 * b + 1, 0:P]).then_inc(acc_free[b], 1)
            dve.drain().then_inc(sv_done, 4 * (NT + 1))
            dve.memset(sbz[:, :, SBX:SBW], 0.0).then_inc(sv_done, 1)

            def sb_abs_of(n, par):
                dve.wait_ge(sb_zs, n + 3)
                z = sbz[:, par, :]
                dve.scalar_tensor_tensor(sbe[:, :], z, -1.0, z, ALU.mult, ALU.max).then_inc(sb_abs, 1)

            def sb_turn(i, par, more):
                n = i * 2 + par
                z = sbz[:, par, :]
                dve.wait_ge(sb_ln, n + 1)
                dve.wait_ge(sb_c, n + 1)
                dve.scalar_tensor_tensor(sbn[:, :], z, 0.0, sbe[:, :], ALU.max, ALU.add)
                dve.drain()
                for c in (0, 4, 7, 8):
                    d = sbn[:, c * P:(c + 1) * P]
                    ins = dve.tensor_tensor(d, d, vis, ALU.mult)
                ins.then_inc(sb_n, 1)
                if more:
                    sb_abs_of(n + 1, 1 - par)
                dve.wait_ge(sb_c, n + 2)
                two = lambda x: x.rearrange("p (a n) -> p a n", a=2)
                dve.tensor_tensor(two(z[:, 0:8 * P]), two(z[:, 0:8 * P]), ps[:, 4:6, :], ALU.subtract)
                dve.tensor_tensor(z[:, 8 * P:SBX], z[:, 8 * P:SBX], ps[:, 6, 0:2 * P], ALU.subtract)
                dve.tensor_tensor(z[0:META, SBX:SBW], z[0:META, SBX:SBW], ps[0:META, 7, :], ALU.subtract)
                dve.drain()
                for c in (0, 4, 7, 8):
                    d = z[:, c * P:(c + 1) * P]
                    ins = dve.tensor_tensor(d, d, vis_neg, ALU.add)
                ins.then_inc(sb_lw, 1)

            sb_abs_of(0, 0)
            with dve.Fori(0, HEADS // 2 - 1) as i:
                sb_turn(i, 0, True)
                sb_turn(i, 1, True)
            sb_turn(HEADS // 2 - 1, 0, True)
            sb_turn(HEADS // 2 - 1, 1, False)

            def with_ada(gm, r):
                for c in ada_units(gm, r):
                    ada_dve(dve, 0, c)

            dve.wait_ge(sb_oc, 2 + HEADS)
            for c in range(NT):
                split_tile(dve, VO[:, c, :, :], VOH[:, c, :, :], VOL[:, c, :, :]).then_inc(split_x, 1)
            for i, slabs in groups(dve, branch_dn):
                for t in slabs:
                    b = acc_in(dve, branch_dn, i, t)
                    if isinstance(i, int):
                        taken(dve, gate_dn, 0, t)
                    else:
                        taken(dve, gate_dn, 0, KD - 2)
                        taken(dve, gate_dn, 0, KD - 1)
                    n = ds(i * R + t, 1)
                    dve.tensor_tensor(MG[:, n, :], ps[:, 2 * b:2 * b + 1, :], MG[:, n, :], ALU.mult).then_inc(acc_free[b], 1)
            dve.wait_ge(silu_c, 1)
            for r in range(R):
                with_ada(gate_sb, r)
            for k in range(KD):
                split_tile(dve, QSK[:, k, 0:SEQ], OSH[:, k, :], OSL[:, k, 0:SEQ]).then_inc(split_x, 1)
            for t in range(KD):
                if t % 2 == 0:
                    with_ada(branch_sb, t // 2)
                b = acc_in(dve, branch_sb, 0, t)
                taken(dve, gate_sb, 0, t)
                dve.tensor_tensor(GT[:, t, :], ps[:, 2 * b, :], GT[:, t, :], ALU.mult).then_inc(acc_free[b], 1)
                dve.drain()
                dve.tensor_tensor(MG[:, t, :], MG[:, t, :], GT[:, t, :], ALU.add)
                dve.drain()
                split_tile(dve, MG[:, t, :], MGH[:, t, :], MGL[:, t, :]).then_inc(merged, 1)

            def add_residual(gm, gate=None, before=None):
                for t in range(KD):
                    if before:
                        before(t)
                    b = acc_in(dve, gm, 0, t)
                    x = H[:, t, META:T]
                    if gate is None:
                        dve.tensor_tensor(x, x, ps[:, 2 * b, :], ALU.add).then_inc(acc_free[b], 1)
                    else:
                        dve.scalar_tensor_tensor(x, ps[:, 2 * b, :], gate(t), x, ALU.mult, ALU.add).then_inc(acc_free[b], 1)

            add_residual(mix_out, before=lambda t: t % 2 or with_ada(mix_out, t // 2))
            norm_dve(dve, 1, lambda k: H[:, k, META:T], lambda k: col("norm_ffn", k), SEQ)

            def split_act(j):
                n = ds(j, 1)
                dve.drain()
                split_tile(dve, ACTF[:, n, :], AFH[:, n, :], AFL[:, n, :]).then_inc(f_split, 1)

            for i, slabs in groups(dve, ffn_in):
                for r in slabs:
                    for c in ada_units(ffn_in, r):
                        ada_dve(dve, i, c)
                    taken(dve, ffn_in, i, 2 * r)
                    b = acc_in(dve, ffn_in, i, 2 * r + 1)
                    dve.tensor_tensor(ACTF[:, ds(i * R + r, 1), :], SG[:, r % 2, :].unsqueeze(1), ps[:, 2 * b:2 * b + 1, :], ALU.mult)\
                        .then_inc(acc_free[b], 1)
                    split_act(i * R + r)

            add_residual(ffn_out, before=lambda t: with_ada(ffn_out, t))

            dve.wait_ge(ada_red, 4 + ADA)
            dve.tensor_tensor(mod[:, :, :].rearrange("p l n -> p (l n)"), ps[:, 4, 0:ADA], cols("ada_b", 0, ADA), ALU.add)
            dve.drain()
            for l in range(2):
                for n, name in enumerate(("norm1", "norm2")):
                    c = (n * 3 + 1) * KD
                    ins = dve.scalar_tensor_tensor(gsc[:, l, n, :], mod[:, l, c:c + KD], 1.0, cols(name, l * KD, KD), ALU.add, ALU.mult)
            ins.then_inc(mod_done, 1)
            dve.drain()

            shift_dve(dve, 2, 0, 0)
            dve.wait_ge(a_in, 16)

            def rope(t):
                dve.wait_ge(a_rot, t + 1)
                dve.tensor_tensor(rtmp[:, :], ps[:, 7, :], ropes[:, 1, :], ALU.mult)
                dve.tensor_tensor(QG[:, t, :], QG[:, t, :], ropes[:, 0, :], ALU.mult)
                dve.drain()
                dve.tensor_tensor(QG[:, t, :], QG[:, t, :], rtmp[:, :], ALU.add).then_inc(a_done, 1)

            for t in range(10):
                dve.wait_ge(h_rs, 1 + 2 * HEADS + t + 1)
                dve.scalar_tensor_tensor(QG[:, t, :], QG[:, t, :], col("gq" if t < 8 else "gk"), NRS[:, 0:SEQ], ALU.mult, ALU.mult)\
                    .then_inc(h_done, 1)
                dve.drain().then_inc(a_nrm, 1)
                if t:
                    rope(t - 1)
            for t in range(2):
                b = acc_in(dve, gq_v, 0, t)
                dve.tensor_copy(VG[:, :, t * P:(t + 1) * P], ps[:, 2 * b, :].rearrange("p (n c) -> p n c", n=NT)).then_inc(acc_free[b], 1)
            rope(9)

            def maxima(g, j):
                n = g * 4 + j
                dve.wait_ge(a_s, n + 1)
                for q in range(NT):
                    dve.tensor_reduce(asm[:, j % 2, 0, q:q + 1], ps[:, q, :], AX.X, ALU.max)
                dve.drain()
                dve.tensor_scalar(asm[:, j % 2, 1, :], asm[:, j % 2, 0, :], -float(HD) ** -0.5, None, ALU.mult).then_inc(a_mx, 1)

            def gq_turn(g, more):
                for j in range(4):
                    n = g * 4 + j
                    dve.wait_ge(a_e, n + 2)
                    dve.reciprocal(asm[:, j % 2, 3, :], asm[:, j % 2, 2, :])
                    dve.drain()
                    for q in range(NT):
                        ins = dve.tensor_scalar(PB[:, j % 2, q, :], PB[:, j % 2, q, :], asm[:, j % 2, 3, q:q + 1], None, ALU.mult)
                    ins.then_inc(a_p, 1)
                    if j < 3:
                        maxima(g, j + 1)
                    elif more:
                        maxima(g + 1, 0)

            maxima(0, 0)
            with dve.Fori(0, KVH - 1) as g:
                gq_turn(g, True)
            gq_turn(KVH - 1, False)
            for k in range(KD):
                dve.wait_ge(a_oc, k + 3)
                dve.tensor_tensor(OGL[:, k, :], OG[:, k, :], OGH[:, k, :], ALU.subtract).then_inc(split_x, 1)
            add_residual(gq_out, lambda t: mod[:, 0, 2 * KD + t:2 * KD + t + 1])

            def dve_conv_ffn(l, u):
                shift_dve(dve, u, l, 1)
                dve.memset(GP[:, :, 0:1], 0.0)
                dve.memset(GP[:, :, SEQ + 1:SEQ + 2], 0.0)
                dve.drain()
                for i, slabs in groups(dve, fc_in[l]):
                    for r in slabs:
                        j = i * R + r
                        taken(dve, fc_in[l], i, 2 * r)
                        x, y = GP[:, r % 2, :], SG[:, r % 2, :]
                        dve.tensor_scalar(y, x[:, 0:SEQ], dcol(f"fc_w{l}", j), dcol(f"fc_b{l}", j), ALU.mult, ALU.add)
                        dve.drain()
                        dve.scalar_tensor_tensor(y, x[:, 1:SEQ + 1], dcol(f"fc_w{l}", j + KF), y, ALU.mult, ALU.add)
                        dve.drain()
                        dve.scalar_tensor_tensor(y, x[:, 2:SEQ + 2], dcol(f"fc_w{l}", j + 2 * KF), y, ALU.mult, ALU.add)\
                            .then_inc(fc_conv, 1)
                        b = acc_in(dve, fc_in[l], i, 2 * r + 1)
                        dve.wait_ge(fc_silu, i * R + (l * KF + r + 1))
                        dve.tensor_tensor(ACTF[:, ds(j, 1), :], y.unsqueeze(1), ps[:, 2 * b:2 * b + 1, :], ALU.mult)\
                            .then_inc(acc_free[b], 1)
                        split_act(j)
                add_residual(fc_out[l], lambda t: mod[:, l, 5 * KD + t:5 * KD + t + 1])

            dve_conv_ffn(0, 3)
            dve.memset(UP[:, :, 0:1], 0.0)
            dve.memset(UP[:, :, SEQ + 1:SEQ + 2], 0.0)
            dve.memset(later_t[:, :], 1.0)
            dve.drain()
            dve.memset(later_t[0:1, :], 0.0)
            shift_dve(dve, 4, 1, 0)
            for i, slabs in groups(dve, hy_in):
                for t in range(2 * R):
                    n = i * (2 * R) + t
                    taken(dve, hy_in, i, t)
                    x, y = UP[:, t % 2, :], U[:, ds(n, 1), :].rearrange("p a n -> p (a n)")
                    dve.tensor_scalar(y, x[:, 0:SEQ], dcol("hy_w", n), dcol("hy_b", n), ALU.mult, ALU.add)
                    dve.drain()
                    dve.scalar_tensor_tensor(y, x[:, 1:SEQ + 1], dcol("hy_w", n + 3 * KD), y, ALU.mult, ALU.add)
                    dve.drain()
                    dve.scalar_tensor_tensor(y, x[:, 2:SEQ + 2], dcol("hy_w", n + 6 * KD), y, ALU.mult, ALU.add).then_inc(y_conv, 1)
            two_pi_hi = 6.28125
            two_pi_lo = 2.0 * np.pi - two_pi_hi
            rounder = 1.5 * 2.0 ** 23
            for n in range(2):
                x, k = A1[:, n, :], A1[:, 2, :]
                dve.wait_ge(y_mlp, n + 1)
                dve.tensor_scalar(x, ps[0:FW, 6 + n, :], col(("b1", "b2")[n])[0:FW], col("freq")[0:FW], ALU.add, ALU.mult)
                dve.drain()
                dve.tensor_scalar(k, x, 1.0 / (2.0 * np.pi), rounder, ALU.mult, ALU.add)
                dve.drain()
                dve.tensor_scalar(k, k, rounder, None, ALU.subtract)
                dve.drain()
                dve.scalar_tensor_tensor(x, k, -two_pi_hi, x, ALU.mult, ALU.add)
                dve.drain()
                dve.scalar_tensor_tensor(x, k, -two_pi_lo, x, ALU.mult, ALU.add)
                dve.drain()
                dve.tensor_scalar(x, x, 3.1415925, -3.1415925, ALU.min, ALU.max).then_inc(y_arg, 1)

            def filters(u, dh):
                for t in range(NT):
                    b = t % 2 * 2
                    dve.drain()
                    if t == 0:
                        dve.wait_ge(y_w, u * 32 + 32)
                    dve.wait_ge(y_f, u * NT + t + 1)
                    if t:
                        dve.wait_ge(y_ab, u * NT + t)
                    dve.tensor_tensor(FB[:, 0, :], ps[:, b, :], DEC[:, t, :], ALU.mult)
                    if t == 0:
                        dve.scalar_tensor_tensor(FB[:, 1, :], ps[:, b + 1, :], later_t[:, 0:1], DEC[:, t, :], ALU.mult, ALU.mult)\
                            .then_inc(y_fb, 1)
                    else:
                        dve.tensor_tensor(FB[:, 1, :], ps[:, b + 1, :], DEC[:, t, :], ALU.mult).then_inc(y_fb, 1)
                    dve.drain()
                    dve.tensor_tensor(PM[:, 0, t, :], FB[:, 0, :], FB[:, 1, :], ALU.add)
                    dve.tensor_tensor(PM[:, 1, t, :], FB[:, 0, :], FB[:, 1, :], ALU.subtract).then_inc(y_pm, 1)
                dve.wait_ge(y_n, u * NT + NT)
                dve.reciprocal(rn[:, dh, :], ps[:, 4, 0:NT]).then_inc(y_rn, 1)

            def hyena_pair(o, more):
                for dh in range(2):
                    u = o * 2 + dh
                    for f in range(2):
                        dve.drain()
                        dve.wait_ge(y_zc, u * 2 + f + 1)
                        dve.tensor_tensor(XZ[:, 0, :], ZS[:, 0, :], ps[:, 5, :], ALU.add)
                        dve.tensor_tensor(XZ[:, 1, :], ZS[:, 1, :], ps[:, 7, :], ALU.add)
                        dve.tensor_tensor(XZ[:, 2, :], ZS[:, 0, :], ps[:, 5, :], ALU.subtract)
                        dve.tensor_tensor(XZ[:, 3, :], ps[:, 7, :], ZS[:, 1, :], ALU.subtract).then_inc(y_x, 1)
                        dve.drain()
                        dve.wait_ge(y_kp, u * 2 + f + 2)
                        dve.wait_ge(y_y, u * 2 + f + 1)
                        for n in (0, 2):
                            zc, zs, kc, ks = XZ[:, n, :], XZ[:, n + 1, :], KP[:, f, n, :], KP[:, f, n + 1, :]
                            dve.tensor_tensor(YB[:, n, :], zc, kc, ALU.mult)
                            dve.tensor_tensor(YT[:, 0, :], zs, ks, ALU.mult)
                            dve.tensor_tensor(YB[:, n + 1, :], zc, ks, ALU.mult)
                            dve.tensor_tensor(YT[:, 1, :], zs, kc, ALU.mult)
                            dve.drain()
                            dve.tensor_tensor(YB[:, n, :], YB[:, n, :], YT[:, 0, :], ALU.subtract)
                            ins = dve.tensor_tensor(YB[:, n + 1, :], YB[:, n + 1, :], YT[:, 1, :], ALU.add)
                            if n == 0:
                                dve.drain()
                        ins.then_inc(y_cb, 1)
                    if dh == 0 or more:
                        filters(u + 1, 1 - dh)
                    pairs = lambda x: x.rearrange("p (t e) -> p t e", e=2)
                    for c in range(NT):
                        n = dh * NT + c
                        z, y = U[:, n, :], ytmp[:, c % 2, :]
                        dve.tensor_scalar(y, z, dcol("skip", o * KD + n), None, ALU.mult)
                        dve.drain()
                        dve.wait_ge(y_inv, u * NT + c + 2)
                        dve.scalar_tensor_tensor(pairs(y), ps[:, 6 + c % 2, :].rearrange("p (e t) -> p t e", e=2), rn[:, dh, c:c + 1],
                                                 pairs(y), ALU.mult, ALU.add)
                        dve.drain()
                        dve.tensor_tensor(z.unsqueeze(1), ytmp[:, c % 2:c % 2 + 1, :], U[:, ds(o * KD + (KD + n), 1), :], ALU.mult)\
                            .then_inc(y_z, 1)
                        if not more:
                            dve.drain()
                            split_tile(dve, z, ZH[:, n, :], ZL[:, n, :]).then_inc(split_x, 1)

            hyena_units(dve, lambda: filters(0, 0), hyena_pair)
            add_residual(hy_out, lambda t: mod[:, 1, 2 * KD + t:2 * KD + t + 1])
            dve_conv_ffn(1, 5)
            dve.wait_ge(n_rs, 7)
            for k in range(KD):
                dve.scalar_tensor_tensor(HN[:, k, 0:SEQ], H[:, k, META:T], col("final", k), NRS[:, 0:SEQ], ALU.mult, ALU.mult)\
                    .then_inc(n_out, 1)
            for n in range(NT):
                for h in range(2):
                    dve.wait_ge(f_t, 2 * n + h + 1)
                    dve.tensor_copy(OUT[:, n, h * 4 * P:(h + 1) * 4 * P], ps[:, 4 + h, :]).then_inc(f_out, 1)


_TABLES = ("t_square", "t_delta", "t_rope", "t_fwd", "t_inv", "t_pos", "t_decay")
_SKIP = ("s5_",)


def kernel(**inputs):
    import concourse.bacc as bacc
    from concourse.bass_utils import run_bass_kernel_spmd

    nc = bacc.Bacc("TRN2", target_bir_lowering=False, num_devices=1)
    arrays, args = {}, {}
    given = {n: np.ascontiguousarray(a) for n, a in inputs.items() if not n.startswith(_SKIP)}
    for name, a in {**given, **tables()}.items():
        arrays[f"in_{name}"] = a
        args[name] = nc.dram_tensor(f"in_{name}", a.shape, F32, kind="ExternalInput").ap()
    out = nc.dram_tensor("out", (1, SEQ, D), F32, kind="ExternalOutput").ap()
    build(nc, args, out[0])
    r = run_bass_kernel_spmd(nc, [arrays], core_ids=[0])
    return r.results[0]["out"]
```

```python
from contextlib import ExitStack

import numpy as np

import concourse.bass as bass
from concourse import mybir

F32 = mybir.dt.float32
F32R = mybir.dt.float32r
ALU = mybir.AluOpType
ACT = mybir.ActivationFunctionType
AX = mybir.AxisListType
ds = bass.ds

P = 128
D = 1024
KD = D // P
SEQ = 512
META = 16
T = META + SEQ
TH = T // 2
NT = SEQ // P
HEADS = 8
DV = 256
DFF = 2816
KF = DFF // P
EPS = 1e-6
R = 4
SLOT = 11 * 256
NEG = -1e30
LEVELS = 7
QH, KVH, HD = 16, 4, 64
ORDERS = 2
EMB, FW = 33, 64

C_DQ, C_DK, C_DV, C_DZ = 0, 1024, 2048, 4096
C_AB, C_SQ, C_SK, C_SV = 6144, 6160, 7184, 8208
C_GD, C_GS = 9232, 10256

ROWS = {}


def _rows():
    tiles = [
        [("conv_q", 32), ("conv_k", 32), ("conv_v", 64)],
        [("norm_mix", 8), ("dn_gain", 2), ("sbq", 1), ("sbk", 1), ("norm_ffn", 8), ("norm1", 16),
         ("norm2", 16), ("final", 8), ("gq", 1), ("gk", 1), ("freq", 1), ("b1", 1), ("b2", 1),
         ("c", 8), ("skip", 16)],
        [("hy_w", 72), ("hy_b", 24)],
        [("ada_b", 96)],
        [("fc_w0", 66), ("fc_b0", 22)],
        [("fc_w1", 66), ("fc_b1", 22)],
    ]
    for n, tile in enumerate(tiles):
        at = n * P
        for name, rows in tile:
            ROWS[name] = (at, rows)
            at += rows
    return len(tiles)


PT = _rows()


def tables():
    i = np.arange(P)
    square = [
        np.eye(P),
        (i[:, None] <= i[None, :]),
        (i[:, None] >= i[None, :]),
        (i[:, None] // HD == i[None, :] // HD),
        np.where(i[:, None] < i[None, :], 0.0, NEG),
        (i[:, None] == i[None, :] % HD),
        (i[:, None] == HD + i[None, :] % HD),
    ]
    rot = np.zeros((P, P))
    rot[i[1::2], i[0::2]] = -1.0
    rot[i[0::2], i[1::2]] = 1.0
    square.append(rot)
    delta = [
        np.where(i[None, :] >= i[:, None], 0.0, NEG),
        np.where(i[None, :] < i[:, None], 0.0, NEG),
    ]
    for s in range(LEVELS):
        b = i >> s
        delta.append((b[:, None] % 2 == 1) & (b[None, :] == b[:, None] - 1))
    flat = lambda a: np.ascontiguousarray(np.concatenate([np.asarray(x, np.float32) for x in a], axis=1))
    n_freq = HD // 4
    inv = (1.0 / (np.float32(10000.0) ** (np.arange(n_freq, dtype=np.float32) / np.float32(n_freq)))).astype(np.float32)
    t = np.arange(SEQ)
    ang = np.concatenate([(t // 64)[:, None].astype(np.float32) * inv, (t % 64)[:, None].astype(np.float32) * inv], 1)
    ang = np.repeat(ang.astype(np.float64), 2, axis=1).T
    rope = flat([np.tile(np.cos(ang), (2, 1)), np.tile(np.sin(ang), (2, 1))])
    f = np.arange(SEQ // 2)
    w = np.pi * ((2 * f[:, None] + 1) * t[None, :] % (4 * SEQ)) / (2 * SEQ)
    by_parity = np.concatenate([t[0::2], t[1::2]])
    rows = lambda a: flat([a[n * P:(n + 1) * P] for n in range(len(a) // P)])
    fwd = flat([rows(np.cos(w).T[by_parity]), rows(np.sin(w).T[by_parity])])
    inv_dft = flat([rows(np.cos(w)[:, by_parity] / SEQ), rows(np.sin(w)[:, by_parity] / SEQ)])
    lin = np.linspace(0.0, 1.0, SEQ, dtype=np.float32)[:, None]
    bands = (EMB - 1) // 2
    wl = (np.float32(2.0 * np.pi) * np.arange(SEQ, dtype=np.float32) / np.float32(SEQ))
    freq = np.linspace(1e-4, bands - 1, bands, dtype=np.float32)
    a = (wl[:, None] * freq[None, :]).astype(np.float32)
    pos = np.concatenate([lin, np.cos(a), -np.sin(a)], axis=1).astype(np.float32).T
    deltas = np.abs(np.linspace(np.log(1e-2) / 1.5, np.log(1e-2) / 0.3, D, dtype=np.float32))
    decay = np.exp(-lin * deltas[None, :]).astype(np.float32)[by_parity]
    return {"t_square": flat(square), "t_delta": flat(delta), "t_rope": rope, "t_fwd": fwd,
            "t_inv": inv_dft, "t_pos": np.ascontiguousarray(pos), "t_decay": decay}


def build(nc, A, out, stop=None):
    ctx = ExitStack()
    with ctx:
        top = [(nc.sbuf_base + 31) // 32 * 32]

        def at(name, shape, offset, parts=P, dtype=F32):
            return nc.alloc_sbuf_tensor_at(name, [parts, *shape], dtype, offset=top[0] + 4 * offset)

        here = [0]

        def fresh(name, *shape, parts=P, dtype=F32):
            n = int(np.prod(shape))
            t = at(name, shape, here[0], parts, dtype)
            here[0] += (n + 7) // 8 * 8
            return t

        def sem(name):
            return ctx.enter_context(nc.semaphore(name))

        raw = fresh("raw", 2, SLOT)
        spl_at = here[0]
        spl = fresh("spl", 2, 2, SLOT // 2, dtype=F32R)
        H = fresh("H", KD, T)
        hn_at = here[0]
        HNH = fresh("HNH", KD, T, dtype=F32R)
        lo_at = here[0]
        HNL = fresh("HNL", KD, T, dtype=F32R)
        HN = at("HN", [KD, T], lo_at)
        pcol = fresh("pcol", PT, P)
        square = fresh("square", 8, P)
        ident, triu, tril, pair_ones, vis_neg, dup0, dup1, rot = (square[:, n, :] for n in range(8))
        ones = fresh("ones", P)
        tiny = fresh("tiny", 8)
        eps, zero = tiny[:, 0:1], tiny[:, 1:2]
        mod = fresh("mod", 2, 6 * KD)
        gsc = fresh("gsc", 2, 2, KD)
        csil = fresh("csil", KD)
        top_words = (nc.sbuf_usable_end - top[0]) // 4

        def col(name, n=0):
            c = ROWS[name][0] + n
            return pcol[:, c // P, c % P:c % P + 1]

        def cols(name, n, count):
            c = ROWS[name][0] + n
            return pcol[:, c // P, c % P:c % P + count]

        def dcol(name, n):
            c = ROWS[name][0]
            return pcol[:, c // P, ds(n + c % P, 1)]

        norm_at = here[0]
        NSQ = fresh("NSQ", 2, T)
        NRS = fresh("NRS", T)
        work = here[0]

        QK = fresh("QK", 2 * HEADS, T)
        QC, KC = QK[:, 0:HEADS, :], QK[:, HEADS:2 * HEADS, :]
        vo_at = here[0]
        VO = fresh("VO", NT, HEADS, DV)
        xt = at("xt", [NT, D], work)
        mt = at("mt", [D], work + NT * D, META)
        prow = at("prow", [PT, P], work + NT * D + D)
        gates_at = here[0]
        g_tok = fresh("g_tok", NT + 1, HEADS)
        b_tok = fresh("b_tok", NT + 1, HEADS)
        ab = fresh("ab", 16)
        wab = fresh("wab", KD, 16)
        wabh = fresh("wabh", KD, 16, dtype=F32R)
        wabl = fresh("wabl", KD, 16, dtype=F32R)
        abrow = fresh("abrow", 16, parts=1)
        soft = fresh("soft", 2, NT + 1, 16)
        scratch = here[0]
        xpad = fresh("xpad", 2, 536)
        cv = fresh("cv", 2, T)
        RSB = fresh("RSB", T)
        vm = fresh("vm", HEADS, DV, parts=META)
        abT = at("abT", [T], here[0], 16)
        km = fresh("km", HEADS, P, parts=META)
        gmb = fresh("gmb", HEADS, META, parts=META)
        ml = fresh("ml", HEADS, META, parts=META)
        mlm = fresh("mlm", HEADS, META, parts=META)
        mx = fresh("mx", HEADS, META, parts=META)
        my = fresh("my", HEADS, META, parts=META)
        mp = fresh("mp", HEADS, META, parts=META)
        msm = fresh("msm", 5, HEADS, parts=META)
        peak = [here[0]]
        here[0] = spl_at
        S = fresh("S", HEADS, DV)
        masks = fresh("masks", 2 + LEVELS, P)
        G4 = HEADS // 2
        lm = [fresh(f"lm{g}", 2, G4, P) for g in range(2)]
        vmb = at("vmb", [HEADS, DV], here[0] - 4 * G4 * P, META)
        assert here[0] <= spl_at + 2 * SLOT
        here[0] = scratch
        group = []
        for g in range(2):
            group.append(dict(
                k=fresh(f"k{g}", G4, P),
                q=fresh(f"q{g}", G4, P),
                gb=fresh(f"gb{g}", G4, P),
                dt=fresh(f"dt{g}", G4, P),
                lp=fresh(f"lp{g}", 2, G4, P),
                x=fresh(f"x{g}", G4, P),
                y=at(f"y{g}", [G4, P], norm_at + g * G4 * P),
                lm=lm[g],
                sm=fresh(f"sm{g}", 8, G4)))
        peak.append(here[0])
        assert max(peak) <= top_words, (peak, top_words)

        QSK = at("QSK", [2 * HEADS, T], work)
        OSL = at("OSL", [2 * HEADS, T], work, dtype=F32R)
        here[0] = scratch
        SV = fresh("SV", NT + 1, D)
        SBW = 14 * P
        SBX = 10 * P
        sbn = fresh("sbn", SBW)
        peak.append(here[0])
        here[0] = spl_at
        sbz = fresh("sbz", 2, SBW)
        sbe = fresh("sbe", SBW)
        assert here[0] <= spl_at + 2 * SLOT
        here[0] = norm_at
        sbk = fresh("sbk", T)
        sbv = fresh("sbv", NT + 1, P)
        assert here[0] <= work
        ZT = at("ZT", [2, SEQ], scratch)
        VOL = at("VOL", [NT, HEADS, DV], vo_at, dtype=F32R)
        VOH = at("VOH", [NT, HEADS, DV], gates_at, dtype=F32R)
        peak.append(gates_at + NT * HEADS * DV)
        mg_at = work + HEADS * T
        MG = at("MG", [KD, SEQ], mg_at)
        MGL = at("MGL", [KD, SEQ], mg_at, dtype=F32R)
        GT = at("GT", [KD, SEQ], vo_at)
        MGH = at("MGH", [KD, SEQ], vo_at + KD * SEQ, dtype=F32R)
        OSH = at("OSH", [KD, SEQ], gates_at, dtype=F32R)
        assert max(peak) <= top_words, (peak, top_words)
        here[0] = work
        AFH = fresh("AFH", KF, SEQ, dtype=F32R)
        af_at = here[0]
        AFL = fresh("AFL", KF, SEQ, dtype=F32R)
        ACTF = at("ACTF", [KF, SEQ], af_at)
        SG = at("SG", [2, SEQ], norm_at)
        ada_at = here[0]
        adw = fresh("adw", 2, KD, P)
        ads = fresh("ads", 4, P)
        assert here[0] <= top_words
        here[0] = ada_at
        GP = fresh("GP", 2, SEQ + 2)
        here[0] = work
        QG = fresh("QG", 10, SEQ)
        KDUP = fresh("KDUP", KVH, SEQ)
        VG = fresh("VG", NT, KVH * HD)
        ropes = fresh("ropes", 2, SEQ)
        rtmp = fresh("rtmp", SEQ)
        PB = fresh("PB", 2, NT, SEQ)
        PTB = fresh("PTB", 2, NT, SEQ)
        qst = fresh("qst", 2, SEQ)
        kst = fresh("kst", SEQ)
        vst = fresh("vst", NT, HD)
        asm = fresh("asm", 2, 4, NT)
        assert here[0] <= top_words
        OG = at("OG", [KD, SEQ], lo_at)
        OGH = at("OGH", [KD, SEQ], hn_at, dtype=F32R)
        OGL = at("OGL", [KD, SEQ], lo_at, dtype=F32R)
        here[0] = work
        U = fresh("U", 3 * KD, SEQ)
        ZL = at("ZL", [KD, SEQ], work, dtype=F32R)
        ZH = at("ZH", [KD, SEQ], work + KD * SEQ, dtype=F32R)
        UP_AT = here[0]
        UP = fresh("UP", 2, SEQ + 2)
        PM = fresh("PM", 2, NT, SEQ)
        fb_at = here[0]
        FB = fresh("FB", 2, SEQ)
        AB = fresh("AB", 2, SEQ)
        AS = fresh("AS", SEQ)
        YT = at("YT", [2, SEQ], UP_AT)
        XZ = at("XZ", [4, SEQ], fb_at)
        DEC = fresh("DEC", NT, SEQ)
        W3 = fresh("W3", 2, SEQ, parts=FW)
        A1 = fresh("A1", 3, SEQ, parts=FW)
        POS = fresh("POS", SEQ, parts=EMB)
        W1 = fresh("W1", FW, parts=EMB)
        W2 = fresh("W2", FW, parts=FW)
        later_t = fresh("later_t", 1)
        rn = fresh("rn", 2, NT)
        assert here[0] <= top_words, here[0]
        ytmp = at("ytmp", [2, SEQ], norm_at)
        here[0] = hn_at
        YF = fresh("YF", 2, 4, SEQ)
        ZK = fresh("ZK", NT, SEQ)
        KS = fresh("KS", 4, SEQ)
        assert here[0] <= hn_at + 2 * KD * T
        here[0] = 0
        t_fwd = fresh("t_fwd", 2, NT, SEQ // 2)
        t_inv = fresh("t_inv", 2, 2, SEQ)
        KP = fresh("KP", 2, 4, SEQ)
        YB = fresh("YB", 4, SEQ)
        ZS = fresh("ZS", 2, SEQ)
        assert here[0] <= hn_at - KD * T
        OUT = at("OUT", [NT, D], work)

        ps = ctx.enter_context(nc.psum_tensor("ps", [P, 8, 512], F32))

        def half(b, m=P):
            return ps[0:m, b:b + 2, 0:TH]

        def split(ap):
            return ap.rearrange("p (h n) -> p h n", h=2)

        slot_full = [sem(f"slot_full{r}") for r in range(2)]
        split_ready = sem("split_ready")
        acc_ready = sem("acc_ready")
        split_x = sem("split_x")
        ada_in = [sem(f"ada_in{r}") for r in range(2)]
        ada_sum, ada_red = sem("ada_sum"), sem("ada_red")
        wab_split, n_y, n_hi = sem("wab_split"), sem("n_y"), sem("n_hi")
        table_full = sem("table_full")
        acc_free = [sem(f"acc_free{b}") for b in range(2)]
        x_in, small_in, act_small_in, table_in = sem("x_in"), sem("small_in"), sem("act_small_in"), sem("table_in")
        mask_in = sem("mask_in")
        cleared = sem("cleared")
        t_ready, t_done = sem("t_ready"), sem("t_done")
        n_sq, n_sum, n_rs, n_out = sem("n_sq"), sem("n_sum"), sem("n_rs"), sem("n_out")
        ab_ready = sem("ab_ready")
        conv_done, silu_done = sem("conv_done"), sem("silu_done")
        l2_sq, l2_sum, l2_rs, l2_done = sem("l2_sq"), sem("l2_sum"), sem("l2_rs"), sem("l2_done")
        vt_ready, vt_done = sem("vt_ready"), sem("vt_done")
        ab_x, ab_l = sem("ab_x"), sem("ab_l")
        m_pe, m_dve, m_act = sem("m_pe"), sem("m_dve"), sem("m_act")
        steps = ("staged", "gates", "expin", "expd", "lower", "masked", "prod", "inv", "pcopy", "delta", "ktok",
                 "kbg", "wt", "nw", "vb", "vn", "vnc", "o", "oc", "sd", "state")
        chunk = [{name: sem(f"{name}{g}") for name in steps} for g in range(2)]
        o_sq, o_sum, o_rs, z_done = sem("o_sq"), sem("o_sum"), sem("o_rs"), sem("z_done")
        h_sq, h_sum, h_rs, h_done = sem("h_sq"), sem("h_sum"), sem("h_rs"), sem("h_done")
        sv_t, sv_done = sem("sv_t"), sem("sv_done")
        sb_k, sb_v_in, sb_z, sb_zs, sb_abs, sb_ln = sem("sb_k"), sem("sb_v_in"), sem("sb_z"), sem("sb_zs"), sem("sb_abs"), sem("sb_ln")
        sb_n, sb_c, sb_lw, sb_w, sb_o, sb_oc = sem("sb_n"), sem("sb_c"), sem("sb_lw"), sem("sb_w"), sem("sb_o"), sem("sb_oc")
        merged = sem("merged")
        mod_done, silu_c, fc_conv, fc_silu = sem("mod_done"), sem("silu_c"), sem("fc_conv"), sem("fc_silu")
        a_in, a_nrm, a_rot, a_done, a_dup, a_dupc = sem("a_in"), sem("a_nrm"), sem("a_rot"), sem("a_done"), sem("a_dup"), sem("a_dupc")
        a_qk, a_v, a_s, a_mx, a_e, a_p = sem("a_qk"), sem("a_v"), sem("a_s"), sem("a_mx"), sem("a_e"), sem("a_p")
        a_t, a_tc, a_o, a_oc = sem("a_t"), sem("a_tc"), sem("a_o"), sem("a_oc")
        y_in, y_w, y_mlp, y_arg, y_sin = sem("y_in"), sem("y_w"), sem("y_mlp"), sem("y_arg"), sem("y_sin")
        y_conv, y_f, y_fb, y_ab, y_pm, y_n, y_rn = sem("y_conv"), sem("y_f"), sem("y_fb"), sem("y_ab"), sem("y_pm"), sem("y_n"), sem("y_rn")
        y_t, y_tc, y_k, y_kc, y_kp = sem("y_t"), sem("y_tc"), sem("y_k"), sem("y_kc"), sem("y_kp")
        y_dft, y_zc, y_x, y_cb, y_y, y_inv, y_z = sem("y_dft"), sem("y_zc"), sem("y_x"), sem("y_cb"), sem("y_y"), sem("y_inv"), sem("y_z")
        f_split = sem("f_split")
        f_t, f_out, stored = sem("f_t"), sem("f_out"), sem("stored")

        class Gemm:
            slabs = evacs = 0
            landed = [0, 0]

            def __init__(self, src, nslab, kt, width=256, pair=False, parts=1):
                self.src, self.nslab, self.kt, self.width, self.pair = src, nslab, kt, width, pair
                self.s0, self.u0, self.f0 = Gemm.slabs, 2 + 2 * Gemm.slabs, Gemm.evacs
                self.turn = R if pair else 2 * R
                Gemm.slabs += nslab
                Gemm.evacs += nslab if pair else 2 * nslab
                self.parts, self.base = parts, list(Gemm.landed)
                for r in range(nslab):
                    Gemm.landed[self.slot(r)] += 16 * parts
                plan.append(self)

            def slot(self, r):
                return (self.s0 + r) % 2

            def view(self, r):
                return raw[:, self.slot(r), 0:self.kt * self.width].rearrange("p (k n) -> p k n", k=self.kt)

            def half(self, u, part):
                return spl[:, u % 2, part, 0:self.kt * P].rearrange("p (k n) -> p k n", k=self.kt)

            def full(self, r):
                return self.base[self.slot(r)] + 16 * self.parts * (r // 2 + 1)

            def units(self, n):
                if self.pair:
                    return [(4 * j + 2 * m + q, 2 * j + q, m) for j in range(n // 2) for m in range(2) for q in range(2)]
                return [(2 * r + m, r, m) for r in range(n) for m in range(2)]

            def last(self, r):
                return self.u0 + (4 * (r // 2) + 2 + r % 2 if self.pair else 2 * r + 1) + 1

            def ready(self, t):
                return self.u0 + (t + 1) * (2 if self.pair else 1)

            def free(self, t):
                return (self.f0 + t) // 2 + 1

            def freed(self, t):
                return self.free(t) + 1

            def buf(self, t):
                return (self.f0 + t) % 2

        plan = []

        def w_cols(w, c0, width=256):
            v = w.rearrange("(k p) n -> p k n", p=P)
            return lambda i, r, h: v[:, :, ds(i * (R * width) + (r * width + c0), width)]

        def w_gate_up(w):
            v = w.rearrange("(k p) (h n) -> h p k n", p=P, h=2)
            return lambda i, r, h: v[h, :, :, ds(i * (R * P) + r * P, P)]

        def w_half_rows(w):
            v = w.rearrange("(q k p) n -> q p k n", p=P, q=2)
            return lambda i, r, h: v[r % 2, :, :, ds(i * (R // 2 * 256) + r // 2 * 256, 256)]

        w_in = A["w_in"][0]
        dn_qk = Gemm(w_cols(w_in, C_DQ), 8, KD)
        dn_v = Gemm(w_cols(w_in, C_DV), 8, KD)
        dn_z = Gemm(w_cols(w_in, C_DZ), 8, KD)
        sb_qk = Gemm(w_cols(w_in, C_SQ), 8, KD)
        sb_v = Gemm(w_cols(w_in, C_SV), 4, KD)
        gate_dn = Gemm(w_cols(w_in, C_GD), 4, KD)
        branch_dn = Gemm(w_half_rows(A["w_branch_dn"][0]), 8, KD, pair=True)
        gate_sb = Gemm(w_cols(w_in, C_GS), 4, KD)
        branch_sb = Gemm(w_cols(A["w_branch_sb"][0], 0), 4, KD)
        mix_out = Gemm(w_cols(A["w_out"][0], 0), 4, KD)
        ffn_in = Gemm(w_gate_up(A["w_ffn_in"][0]), KF, KD, parts=2)
        ffn_out = Gemm(w_half_rows(A["w_ffn_out"][0]), 8, KF // 2, pair=True)

        def groups(eng, gm):
            n = gm.nslab // R
            if n > 1:
                with eng.Fori(0, n) as i:
                    yield i, range(R)
            elif n:
                yield 0, range(R)
            if gm.nslab % R:
                yield n, range(gm.nslab % R)

        def products(pe, dst, w, x, first=True, final=True):
            pe.matmul(dst, w[0], x[0], start=first, stop=False)
            pe.matmul(dst, w[0], x[1], start=False, stop=False)
            return pe.matmul(dst, w[1], x[0], start=False, stop=final)

        def halves_of(gm, u, k):
            return gm.half(u, 0)[:, k, :], gm.half(u, 1)[:, k, :]

        def pe_tile(pe, gm, i, r, m, x, wide_t=False, ready=None):
            t = 2 * r + m
            b = gm.buf(t)
            pe.wait_ge(split_ready, i * (2 * R) + (gm.u0 + t + 1))
            pe.wait_ge(acc_free[b], i * (gm.turn // 2) + gm.free(t))
            for k in range(gm.kt):
                if ready and t == 0:
                    pe.wait_ge(*ready(k))
                w, tok = halves_of(gm, t, k), x(k)
                if wide_t:
                    for h in range(2):
                        mm = products(pe, ps[:, 2 * b + h, 0:TH], w, [y[:, h * TH:(h + 1) * TH] for y in tok],
                                      k == 0, k == gm.kt - 1)
                else:
                    mm = products(pe, ps[:, 2 * b, :], w, tok, k == 0, k == gm.kt - 1)
            mm.then_inc(acc_ready, 1)

        def wide(ap, n=P):
            return ap.unsqueeze(2).broadcast_to([ap.shape[0], ap.shape[1], n])

        def heads_of(ap, n):
            return ap.unsqueeze(1).broadcast_to([ap.shape[0], n, ap.shape[1]])

        gq_k = Gemm(w_cols(A["attn_w_qkv_2"][0], QH * HD), 1, KD)
        gq_q = Gemm(w_cols(A["attn_w_qkv_2"][0], 0), 4, KD)
        GQ_TILES = [(gq_k, t, KD + t) for t in range(2)] + [(gq_q, t, t) for t in range(KD)]
        gq_v = Gemm(w_cols(A["attn_w_qkv_2"][0], (QH + KVH) * HD), 1, KD)
        gq_out = Gemm(w_cols(A["attn_w_o_2"][0], 0), 4, KD)
        fc_in, fc_out = [None, None], [None, None]

        def conv_ffn(l):
            fc_in[l] = Gemm(w_gate_up(A["ffn_w_up_2"][l]), KF, KD, parts=2)
            fc_out[l] = Gemm(w_half_rows(A["ffn_w_down_2"][l]), 8, KF // 2, pair=True)

        conv_ffn(0)
        hy_in = Gemm(w_cols(A["hy_w_in_2"][0], 0), 12, KD)
        hy_out = Gemm(w_cols(A["hy_w_out_2"][0], 0), 4, KD)
        conv_ffn(1)

        def taken(eng, gm, i, t):
            eng.wait_ge(acc_free[gm.buf(t)], i * (gm.turn // 2) + gm.freed(t))

        def acc_in(eng, gm, i, t):
            eng.wait_ge(acc_ready, i * (2 * R) + gm.ready(t))
            return gm.buf(t)

        LN_EXP, SILU = "natural_log_exp_and_others", "silu_and_others"

        def norm_act(act, u, x, n, shift=None, hi=True, tile=None):
            act.preload_act_table_set(LN_EXP)
            for k in range(KD):
                if tile:
                    tile(k)
                if k >= 2:
                    act.wait_ge(n_sum, KD * u + k - 1)
                act.activation(NSQ[:, k % 2, 0:n], x(k), ACT.Square).then_inc(n_sq, 1)
            act.wait_ge(n_sum, KD * (u + 1))
            src = half(6) if n == T else ps[:, 6, 0:n]
            dst = split(NRS[:, 0:n]) if n == T else NRS[:, 0:n]
            if u:
                act.wait_ge(n_out, KD * u)
            act.activation(dst, src, ACT.Ln, bias=eps, scale=1.0 / D)
            act.drain()
            act.activation(NRS[:, 0:n], NRS[:, 0:n], ACT.Exp, bias=zero, scale=-0.5).then_inc(n_rs, 1)
            for k in range(KD if hi else 0):
                act.wait_ge(n_y, KD * u + k + 1)
                act.activation(HNH[:, k, 0:n], HN[:, k, 0:n], ACT.Identity, bias=shift(k) if shift else zero, scale=1.0)\
                    .then_inc(n_hi, 1)

        def norm_pe(pe, u, n, tiles=range(KD)):
            for k in tiles:
                pe.wait_ge(n_sq, KD * u + k + 1)
                if n == T:
                    for h in range(2):
                        mm = pe.matmul(ps[:, 6 + h, 0:TH], ones[:, :], NSQ[:, k % 2, h * TH:(h + 1) * TH],
                                       start=k == 0, stop=k == KD - 1)
                else:
                    mm = pe.matmul(ps[:, 6, 0:n], ones[:, :], NSQ[:, k % 2, 0:n], start=k == 0, stop=k == KD - 1)
                mm.then_inc(n_sum, 1)

        def norm_after(pe, u):
            return lambda t: norm_pe(pe, u, SEQ, range(t - 1, t)) if t else None

        def norm_dve(dve, u, x, gain, n, shift=None):
            def lo(k):
                dve.wait_ge(n_hi, KD * u + k + 1)
                y = HN[:, k, 0:n]
                if shift:
                    ins = dve.scalar_tensor_tensor(HNL[:, k, 0:n], y, shift(k), HNH[:, k, 0:n], ALU.add, ALU.subtract)
                else:
                    ins = dve.tensor_tensor(HNL[:, k, 0:n], y, HNH[:, k, 0:n], ALU.subtract)
                ins.then_inc(n_out, 1)

            dve.wait_ge(n_rs, u + 1)
            for k in range(KD):
                dve.scalar_tensor_tensor(HN[:, k, 0:n], x(k), gain(k), NRS[:, 0:n], ALU.mult, ALU.mult).then_inc(n_y, 1)
                if k:
                    lo(k - 1)
            lo(KD - 1)

        def shift_of(l, n):
            return lambda k: mod[:, l, n * 3 * KD + k:n * 3 * KD + k + 1]

        def shift_dve(dve, u, l, n):
            norm_dve(dve, u, lambda k: H[:, k, META:T], lambda k: gsc[:, l, n, k:k + 1], SEQ, shift_of(l, n))

        def head_pe(pe, gm, i, t, n):
            pe.wait_ge(h_sq, n + 1)
            pe.wait_ge(h_rs, n + 1)
            for h in range(2):
                mm = pe.matmul(ps[:, 6 + h, 0:TH], ones[:, :], NSQ[:, t % 2, h * TH:(h + 1) * TH], start=True, stop=True)
            mm.then_inc(h_sum, 1)

        def pe_gemm(pe, gm, x, ready=None, after=None, tile_after=None):
            for i, slabs in groups(pe, gm):
                for r in slabs:
                    for m in range(2):
                        pe_tile(pe, gm, i, r, m, x, False, ready)
                        if tile_after:
                            tile_after(2 * r + m)
                    if after:
                        after(r)

        def pe_gemm_pair(pe, gm, x, ready=None, after=None):
            if after:
                turns = [(i, range(R)) for i in range(gm.nslab // R)]
            else:
                turns = groups(pe, gm)
            for i, slabs in turns:
                for u, r, m in gm.units(len(slabs)):
                    t, q = u // 2, u % 2
                    b = gm.buf(t)
                    if ready and u < 2:
                        pe.wait_ge(*ready(q))
                    pe.wait_ge(split_ready, i * (2 * R) + (gm.u0 + u + 1))
                    if q == 0:
                        pe.wait_ge(acc_free[b], i * (gm.turn // 2) + gm.free(t))
                    for k in range(gm.kt):
                        mm = products(pe, ps[:, 2 * b, :], halves_of(gm, u, k), x(q * gm.kt + k),
                                      q + k == 0, q == 1 and k == gm.kt - 1)
                    mm.then_inc(acc_ready, 1)
                    if after and q:
                        after(i * R + t)

        def pool_split(pool, gm):
            for i, slabs in groups(pool, gm):
                seen = set()
                for u, r, m in gm.units(len(slabs)):
                    if r not in seen:
                        pool.wait_ge(slot_full[gm.slot(r)], i * (16 * gm.parts * R // 2) + gm.full(r))
                        seen.add(r)
                    pool.wait_ge(acc_ready, i * (2 * R) + (gm.u0 + u - 1))
                    w, hi, lo = gm.view(r)[:, :, m * P:(m + 1) * P], gm.half(u, 0), gm.half(u, 1)
                    pool.tensor_tensor(hi, w, heads_of(ones[:, :], gm.kt), ALU.mult)
                    pool.drain()
                    pool.tensor_tensor(lo, w, hi, ALU.subtract).then_inc(split_ready, 1)

        def split_tile(eng, x, hi, lo):
            eng.tensor_copy(hi, x)
            eng.drain()
            return eng.tensor_tensor(lo, x, hi, ALU.subtract)

        SB = [(0, 0, META, P), (4 * P, P, META + P, P), (7 * P, 3 * P, META + 3 * P, P), (8 * P, 2 * P, META + 2 * P, P),
              (10 * P, 0, 0, META)]
        SB_V = [0, 1, 3, 2, NT]

        def sb_bank(b, n):
            c, q0, _, m = SB[n]
            c = c if n < 4 else 12 * P
            return ps[0:m, b + c // 512, c % 512:c % 512 + SEQ - q0]

        def sb_keys(x, n):
            c, q0, _, m = SB[n]
            return x[0:m, c:c + SEQ - q0]

        def sb_logits(pe, i, par):
            n = i * 2 + par
            pe.wait_ge(sb_k, n + 1)
            pe.wait_ge(sb_zs, n + 2)
            pe.wait_ge(sb_oc, n + 1)
            for t in (1, 2, 3, 4, 0):
                c, q0, k0, m = SB[t]
                mm = pe.matmul(sb_bank(0, t), sbk[:, k0:k0 + m],
                               QSK[:, ds(n, 1), META + q0:T].rearrange("p a n -> p (a n)"), start=True, stop=True)
            mm.then_inc(sb_z, 1)

        def hyena_units(eng, start, pair):
            start()
            with eng.Fori(0, ORDERS - 1) as o:
                pair(o, True)
            pair(ORDERS - 1, False)

        def y_step(c, l, x=0):
            return c * (2 * LEVELS - 2) + ((2 * l if l else 1) + x)

        tile = lambda ap: ap.rearrange("j (k p) -> (j k) p", p=P)
        one = lambda ap: ap.rearrange("(j k) -> j k", j=1)

        POOL_SMALL, ACT_SMALL = 14, 16

        def load_rows(eng, done, name, src):
            r, n = ROWS[name]
            eng.dma_start(prow[r % P:r % P + n, r // P, 0:src.shape[-1]], src).then_inc(done, 16)

        block = ctx.enter_context(nc.Block())

        ADA = 2 * 6 * KD
        ADA_WITH = {gate_sb: 2, branch_sb: 2, mix_out: 3, ffn_in: 2, ffn_out: 3}
        ada_base, n_ada = {}, 0
        for gm, n in ADA_WITH.items():
            ada_base[gm] = n_ada
            n_ada += n * gm.nslab
        assert n_ada == ADA
        ADA_TURN = R * ADA_WITH[ffn_in]
        ada_w = A["ada_w_2"].rearrange("l (k p) n -> l p k n", p=P)

        def ada_units(gm, r):
            n = ADA_WITH[gm]
            return range(ada_base[gm] + r * n, ada_base[gm] + (r + 1) * n)

        def ada_load(sp, i, c):
            if c >= 2:
                sp.wait_ge(ada_sum, i * ADA_TURN + (c - 1))
            sp.dma_start(adw[:, c % 2, :, :], ada_w[c % 2][:, :, ds((i * (ADA_TURN // 2) + c // 2) * P, P)]).then_inc(ada_in[c % 2], 16)

        def ada_dve(dve, i, c):
            dve.wait_ge(ada_in[c % 2], i * (16 * ADA_TURN // 2) + 16 * (c // 2 + 1))
            dve.wait_ge(ada_red, i * ADA_TURN + (c + 1))
            w = adw[:, c % 2, :, :]
            dve.tensor_tensor(w, w, wide(csil[:, :]), ALU.mult)
            for n in (4, 2):
                dve.drain()
                dve.tensor_tensor(w[:, 0:n, :], w[:, 0:n, :], w[:, n:2 * n, :], ALU.add)
            dve.drain()
            dve.tensor_tensor(ads[:, c % 4, :], w[:, 0, :], w[:, 1, :], ALU.add).then_inc(ada_sum, 1)

        def ada_pe(pe, i, c):
            pe.wait_ge(ada_sum, i * ADA_TURN + (c + 1))
            n = i * (ADA_TURN // 2) + (c % 2 * 6 * KD + c // 2)
            pe.matmul(ps[:, 4, ds(n, 1)], ads[:, c % 4, :], ones[:, 0:1], start=True, stop=True).then_inc(ada_red, 1)

        @block.sync
        def _(sp):
            x_rows = A["x"][0].rearrange("(n p) d -> p n d", p=P)
            for n in range(0, NT, 2):
                sp.dma_start(xt[:, n:n + 2, :], x_rows[:, n:n + 2, :]).then_inc(x_in, 16)
            done = []
            for gm in plan:
                def load(i, r):
                    n = gm.width // gm.parts
                    for h in range(gm.parts):
                        sp.dma_start(gm.view(r)[:, :, h * n:(h + 1) * n], gm.src(i, r, h))\
                            .then_inc(slot_full[gm.slot(r)], 16)
                    if gm in ada_base:
                        if r or not isinstance(i, int) or i:
                            for c in ada_units(gm, r - 1):
                                if c == 0:
                                    sp.wait_ge(acc_ready, gate_sb.u0)
                                ada_load(sp, i, c)
                        elif gm is not gate_sb:
                            before = list(ada_base)[list(ada_base).index(gm) - 1]
                            for c in ada_units(before, before.nslab - 1):
                                ada_load(sp, 0, c)

                def reread(i, r):
                    sp.wait_ge(split_ready, i * (2 * R) + (gm.last(r - 2) if r >= 2 else gm.last(r + 2) - 2 * R))

                if gm is hy_out:
                    sp.wait_ge(acc_ready, hy_out.u0)
                    for buf, src in ((t_fwd, A["t_fwd"]), (t_inv, A["t_inv"])):
                        sp.dma_start(buf[:, :, :, :].rearrange("p s k n -> p (s k n)"), src).then_inc(table_full, 16)
                    sp.wait_ge(y_inv, 1 + 2 * ORDERS * NT)
                done += [gm.last(r) for r in range(gm.nslab)]
                turns, rest = gm.nslab // R, gm.nslab % R
                for r in range(min(R, gm.nslab)):
                    if gm.s0 + r >= 2:
                        sp.wait_ge(split_ready, done[gm.s0 + r - 2])
                    load(0, r)
                if gm is ffn_out:
                    for r in range(R, 2 * R):
                        sp.wait_ge(split_ready, gm.last(r - 2))
                        load(0, r)
                    for c in ada_units(gm, 2 * R - 1):
                        ada_load(sp, 0, c)
                elif turns > 1:
                    with sp.Fori(1, turns) as i:
                        for r in range(R):
                            reread(i, r)
                            load(i, r)
                for r in range(rest if turns else 0):
                    reread(turns, r)
                    load(turns, r)

        @block.gpsimd
        def _(pool):
            pool.sem_inc(split_ready, 2)
            pool.sem_inc(y_kp, 1)
            pool.sem_inc(y_n, 1)
            pool.sem_inc(y_y, 1)
            pool.memset(ones[:, :], 1.0)
            pool.memset(tiny[:, 0:1], EPS)
            pool.memset(tiny[:, 1:2], 0.0)
            pool.memset(prow[:, :, :], 0.0)
            pool.memset(xpad[:, :, 0:3], 0.0).then_inc(cleared, 1)
            pool.wait_ge(cleared, 1)
            load_rows(pool, small_in, "norm_mix", tile(A["norm_mix_gain"]))
            load_rows(pool, small_in, "dn_gain", tile(A["dn_out_norm_gain"]))
            load_rows(pool, small_in, "sbq", A["sb_q_norm_gain"])
            load_rows(pool, small_in, "sbk", A["sb_k_norm_gain"])
            load_rows(pool, small_in, "norm_ffn", tile(A["norm_ffn_gain"]))
            load_rows(pool, small_in, "norm1", tile(A["norm1_g_2"]))
            load_rows(pool, small_in, "norm2", tile(A["norm2_g_2"]))
            load_rows(pool, small_in, "final", tile(one(A["final_g_2"])))
            load_rows(pool, small_in, "freq", A["hy_f_freq_2"])
            load_rows(pool, small_in, "b1", A["hy_f_b1_2"])
            load_rows(pool, small_in, "b2", A["hy_f_b2_2"])
            pool.dma_start(wab[:, :, :], w_cols(w_in, C_AB, 16)(0, 0, 0)).then_inc(small_in, 16)
            pool.dma_start(abrow[:, 0:8], A["dn_a_log"]).then_inc(small_in, 16)
            pool.dma_start(abrow[:, 8:16], A["dn_dt_bias"]).then_inc(small_in, 16)
            pool_split(pool, dn_qk)
            pool.wait_ge(small_in, 16 * POOL_SMALL)
            pool.tensor_tensor(wabh[:, :, :], wab[:, :, :], heads_of(ones[:, 0:16], KD), ALU.mult)
            pool.drain()
            pool.tensor_tensor(wabl[:, :, :], wab[:, :, :], wabh[:, :, :], ALU.subtract).then_inc(wab_split, 1)
            pool_split(pool, dn_v)
            pool.wait_ge(l2_done, 1 + 16)
            pool.wait_ge(vt_done, 2 + 32)
            pool.dma_start(masks[:, :, :].rearrange("p a b -> p (a b)"), A["t_delta"]).then_inc(mask_in, 16)
            pool.wait_ge(mask_in, 16)
            with pool.Fori(0, NT) as c:
                for l in range(LEVELS):
                    for g in range(2):
                        G, E = group[g], chunk[g]
                        if l == 0:
                            pool.wait_ge(E["lower"], c + 1)
                        if l == 2:
                            pool.wait_ge(E["inv"], y_step(c, 0))
                        if l >= 2:
                            pool.wait_ge(E["prod"], c * LEVELS + l - 1)
                        pool.tensor_tensor(G["lm"][:, l % 2, :, :], G["lp"][:, 0, :, :],
                                           heads_of(masks[:, 2 + l, :], G4), ALU.mult).then_inc(E["masked"], 1)
            for g in range(2):
                pool.wait_ge(chunk[g]["state"], 1 + NT)
                pool.wait_ge(chunk[g]["oc"], 1 + NT)
            pool_split(pool, dn_z)
            pool_split(pool, sb_qk)
            pool_split(pool, sb_v)
            pool.wait_ge(h_done, 1 + 2 * HEADS)
            pool.wait_ge(sv_done, KD)

            def stage_head(n):
                pool.tensor_copy(sbk[:, :].unsqueeze(1), QSK[:, ds(n + HEADS, 1), :]).then_inc(sb_k, 1)

            def stage_v(n):
                pool.tensor_copy(sbv[:, 0:NT, :], SV[:, 0:NT, ds(n * P, P)]).then_inc(sb_v_in, 1)
                pool.tensor_copy(sbv[0:META, NT, :], SV[0:META, NT, ds(n * P, P)]).then_inc(sb_v_in, 1)

            stage_head(0)
            stage_v(0)
            pool.wait_ge(sb_z, 1)
            stage_head(1)
            with pool.Fori(1, HEADS - 1) as n:
                pool.wait_ge(sb_z, n + 1)
                stage_head(n + 1)
                pool.wait_ge(sb_o, n + 1)
                stage_v(n)
            pool.wait_ge(sb_o, HEADS)
            stage_v(HEADS - 1)

            pool.wait_ge(sb_oc, 2 + HEADS)
            for gm in (gate_dn, branch_dn, gate_sb, branch_sb, mix_out, ffn_in, ffn_out):
                pool_split(pool, gm)
            taken(pool, ffn_out, 1, 2 * R - 1 - R)
            taken(pool, ffn_out, 1, 2 * R - 2 - R)
            pool.dma_start(ropes[:, :, :].rearrange("p a n -> p (a n)"), A["t_rope"]).then_inc(a_in, 16)
            pool_split(pool, gq_k)
            pool_split(pool, gq_q)
            pool_split(pool, gq_v)
            pool.wait_ge(a_done, 10)
            pool.wait_ge(a_dupc, KVH)

            def stage_qk(g):
                pool.tensor_copy(qst[:, :, :], QG[:, ds(g * 2, 2), :]).then_inc(a_qk, 1)
                pool.tensor_copy(kst[:, :].unsqueeze(1), KDUP[:, ds(g, 1), :]).then_inc(a_qk, 1)

            def stage_vg(g):
                pool.tensor_copy(vst[:, :, :], VG[:, :, ds(g * HD, HD)]).then_inc(a_v, 1)

            stage_qk(0)
            pool.wait_ge(sv_done, KD + 1 + 2)
            stage_vg(0)
            with pool.Fori(1, KVH) as g:
                pool.wait_ge(a_s, g * (4 * NT))
                stage_qk(g)
                pool.wait_ge(a_o, g * 4 + 2)
                stage_vg(g)

            for gm in (gq_out, fc_in[0], fc_out[0]):
                pool_split(pool, gm)
            taken(pool, fc_out[0], 1, R - 1)
            taken(pool, fc_out[0], 1, R - 2)
            pool.dma_start(POS[:, :], A["t_pos"]).then_inc(y_in, 16)
            pool.dma_start(W1[:, :], A["hy_f_w1_2"][0]).then_inc(y_in, 16)
            pool.dma_start(W2[:, :], A["hy_f_w2_2"][0]).then_inc(y_in, 16)
            pool_split(pool, hy_in)
            w3 = A["hy_f_w3_2"][0].rearrange("p (o s d) -> o p s d", o=ORDERS, s=2)
            dec = A["t_decay"].rearrange("(n p) d -> p n d", p=P)

            def filter_in(o, dh):
                half_d = slice(dh * SEQ, (dh + 1) * SEQ)
                pool.dma_start(W3[:, :, :], w3[ds(o, 1), :, :, half_d].rearrange("o p s d -> (o p) s d")).then_inc(y_w, 16)
                pool.dma_start(DEC[:, :, :], dec[:, :, half_d]).then_inc(y_w, 16)

            def hyena_pair(o, more):
                for dh in range(2):
                    u = o * 2 + dh
                    for f in range(2):
                        pool.wait_ge(y_cb, u * 4 + (f * 2 + 2))
                        pool.wait_ge(y_kc, u * 2 + f + 1)
                        ce, co, se, so = (KS[:, n, :] for n in range(4))
                        pool.tensor_tensor(KP[:, f, 0, :], ce, co, ALU.add)
                        pool.tensor_tensor(KP[:, f, 1, :], se, so, ALU.add)
                        pool.tensor_tensor(KP[:, f, 2, :], ce, co, ALU.subtract)
                        pool.tensor_tensor(KP[:, f, 3, :], so, se, ALU.subtract).then_inc(y_kp, 1)
                        if f == 0 and (dh == 0 or more):
                            filter_in(o + dh, 1 - dh)
                    for f in range(2):
                        pool.wait_ge(y_inv, u * NT + 1)
                        c, si, cm, sm = (YB[:, n, :] for n in range(4))
                        pool.wait_ge(y_cb, u * 4 + (f * 2 + 5))
                        pool.tensor_tensor(YF[:, f, 0, :], c, cm, ALU.add)
                        pool.tensor_tensor(YF[:, f, 2, :], c, cm, ALU.subtract)
                        pool.wait_ge(y_cb, u * 4 + (f * 2 + 6))
                        pool.tensor_tensor(YF[:, f, 1, :], si, sm, ALU.subtract)
                        pool.tensor_tensor(YF[:, f, 3, :], si, sm, ALU.add).then_inc(y_y, 1)
                    if dh == 0 or more:
                        pool.wait_ge(y_f, (u + 1) * (NT + 1))
                        filter_sums(u + 1)

            def filter_sums(u):
                for t in range(NT):
                    pool.wait_ge(y_ab, u * NT + t + 1)
                    if t == 0:
                        pool.tensor_tensor(AS[:, :], AB[:, 0, :], AB[:, 1, :], ALU.add).then_inc(y_n, 1)
                    else:
                        pool.tensor_tensor(AB[:, 0, :], AB[:, 0, :], AB[:, 1, :], ALU.add)
                        pool.drain()
                        pool.tensor_tensor(AS[:, :], AS[:, :], AB[:, 0, :], ALU.add).then_inc(y_n, 1)

            def filters_start():
                filter_in(0, 0)
                filter_sums(0)

            hyena_units(pool, filters_start, hyena_pair)
            for gm in (hy_out, fc_in[1], fc_out[1]):
                pool_split(pool, gm)

        @block.tensor
        def _(pe):
            pe.sem_inc(acc_ready, 2)
            pe.sem_inc(vt_ready, 4)
            pe.sem_inc(ada_red, 4)
            pe.sem_inc(l2_sum, 2)
            pe.sem_inc(h_sum, 2)
            pe.sem_inc(sb_c, 1)
            pe.sem_inc(sb_o, 1)
            pe.sem_inc(a_t, 5)
            pe.sem_inc(a_o, 2)
            pe.sem_inc(y_inv, 1)
            pe.wait_ge(x_in, 48)
            pe.wait_ge(table_in, 16)
            for k in range(KD):
                if k >= 2:
                    pe.wait_ge(t_done, 2 * (k - 1))
                for n in range(NT):
                    mm = pe.transpose(ps[:, k % 2, n * P:(n + 1) * P], xt[:, n, k * P:(k + 1) * P], ident)
                mm.then_inc(t_ready, 1)
                pe.transpose(ps[:, 2 + k % 2, 0:META], mt[:, k * P:(k + 1) * P], ident[0:META, 0:META])\
                    .then_inc(t_ready, 1)
            norm_pe(pe, 0, T)
            pe.wait_ge(small_in, 16 * POOL_SMALL)
            pe.wait_ge(act_small_in, 16 * ACT_SMALL)
            for n in range(PT):
                mm = pe.transpose(ps[:, 4 + n // 4, n % 4 * P:(n % 4 + 1) * P], prow[:, n, :], ident)
            mm.then_inc(t_ready, 1)
            x_all = lambda k: (HNH[:, k, :], HNL[:, k, :])
            x_meta = lambda k: (HNH[:, k, META:T], HNL[:, k, META:T])
            x_hn = lambda k: (HNH[:, k, 0:SEQ], HNL[:, k, 0:SEQ])
            for i, slabs in groups(pe, dn_qk):
                for r in slabs:
                    for m in range(2):
                        pe_tile(pe, dn_qk, i, r, m, x_all, True, lambda k: (n_out, k + 1))

            pe.wait_ge(wab_split, 1)
            for h in range(2):
                for k in range(KD):
                    mm = products(pe, ps[0:16, 4 + h, 0:TH], [y[:, k, :] for y in (wabh, wabl)],
                                  [y[:, k, h * TH:(h + 1) * TH] for y in (HNH, HNL)], k == 0, k == KD - 1)
            mm.then_inc(ab_ready, 1)
            pe.wait_ge(ab_l, 1)
            for n in range(NT + 1):
                m, c0 = (P, META + n * P) if n < NT else (META, 0)
                pe.transpose(ps[0:m, 6, n * 16:(n + 1) * 16], abT[:, c0:c0 + m], ident[0:16, 0:16])
            pe.matmul(ps[:, 7, 0:16], ones[0:1, :], abrow[:, :], start=True, stop=True).then_inc(ab_ready, 1)

            def v_turn(i, t):
                n = i * (2 * R) + t
                src = cv[:, t % 2, :]
                pe.wait_ge(silu_done, n + 2 + 16 + 1)
                pe.wait_ge(vt_done, n * 2 + 2)
                for c in range(NT):
                    mm = pe.transpose(ps[:, 6, c * P:(c + 1) * P], src[:, META + c * P:META + (c + 1) * P], ident)
                mm.then_inc(vt_ready, 1)
                pe.transpose(ps[0:META, 7, 0:P], src[:, 0:META], ident).then_inc(vt_ready, 1)

            for i, slabs in groups(pe, dn_v):
                for r in slabs:
                    for m in range(2):
                        t = 2 * r + m
                        n = i * (2 * R) + t
                        pe_tile(pe, dn_v, i, r, m, x_all, True)
                        pe.wait_ge(l2_sq, n + 1)
                        pe.wait_ge(l2_rs, n + 1)
                        for h in range(2):
                            mm = pe.matmul(ps[:, 4 + h, 0:TH], ones[:, :], NSQ[:, t % 2, h * TH:(h + 1) * TH],
                                           start=True, stop=True)
                        mm.then_inc(l2_sum, 1)
                        if t:
                            v_turn(i, t - 1)
                v_turn(i, 2 * R - 1)

            m = META
            pe.wait_ge(l2_done, 1 + 16)
            pe.wait_ge(vt_done, 2 + 32)
            pe.wait_ge(m_dve, 1)
            for h in range(HEADS):
                pe.matmul(ps[0:m, 0, h * m:(h + 1) * m], gmb[:, h, :], triu[0:m, 0:m], start=True, stop=True)
            pe.matmul(ps[0:m, 1, 0:HEADS], triu[0:m, 0:m], gmb[:, :, 0], start=True, stop=True)
            for h in range(HEADS):
                kh = KC[:, h, 0:m]
                pe.matmul(ps[0:m, 2, h * m:(h + 1) * m], kh, kh, start=True, stop=True)
            for h in range(HEADS):
                mm = pe.transpose(ps[0:m, 3 + h // 4, h % 4 * P:(h % 4 + 1) * P], KC[:, h, 0:m], ident)
            mm.then_inc(m_pe, 1)
            for l in range(4):
                pe.wait_ge(m_dve, 4 + 3 * l)
                for h in range(HEADS):
                    mm = pe.matmul(ps[0:m, 0, h * m:(h + 1) * m], mlm[:, h, :], my[:, h, :] if l else ident[0:m, 0:m],
                                   start=True, stop=True)
                mm.then_inc(m_pe, 1)
                if l:
                    pe.wait_ge(m_dve, 5 + 3 * l)
                    for h in range(HEADS):
                        mm = pe.matmul(ps[0:m, 1, h * m:(h + 1) * m], mx[:, h, :], mp[:, h, :], start=True, stop=True)
                    for h in range(HEADS):
                        mm = pe.matmul(ps[0:m, 2, h * m:(h + 1) * m], mp[:, h, :], mx[:, h, :], start=True, stop=True)
                    mm.then_inc(m_pe, 1)
            pe.wait_ge(m_dve, 16)
            for h in range(HEADS):
                mm = pe.matmul(ps[0:m, 4 + h // 2, h % 2 * DV:(h % 2 + 1) * DV], my[:, h, :], vmb[:, h, :],
                               start=True, stop=True)
            mm.then_inc(m_pe, 1)
            pe.wait_ge(m_dve, 17)
            for h in range(HEADS):
                mm = pe.matmul(ps[:, h // 2, h % 2 * DV:(h % 2 + 1) * DV], km[:, h, :], vm[:, h, :], start=True, stop=True)
            mm.then_inc(m_pe, 1)

            pe.wait_ge(m_dve, 18)
            with pe.Fori(0, NT) as c:
                for g in range(2):
                    G, E, b = group[g], chunk[g], 4 * g
                    pe.wait_ge(E["staged"], c * 2 + 1)
                    pe.wait_ge(E["oc"], c + 1)
                    for h in range(G4):
                        pe.matmul(ps[:, b, h * P:(h + 1) * P], G["gb"][:, h, :], triu, start=True, stop=True)
                    pe.matmul(ps[:, b + 1, 0:G4], triu, G["gb"][:, :, 0], start=True, stop=True).then_inc(E["gates"], 1)
                for g in range(2):
                    G, E, b = group[g], chunk[g], 4 * g
                    pe.wait_ge(E["staged"], c * 2 + 2)
                    pe.wait_ge(E["state"], c + 1)
                    for h in range(G4):
                        pe.matmul(ps[:, b + 2, h * P:(h + 1) * P], G["k"][:, h, :], G["k"][:, h, :], start=True, stop=True)
                    for h in range(G4):
                        mm = pe.matmul(ps[:, b + 3, h * P:(h + 1) * P], G["k"][:, h, :], QC[:, g * G4 + h, ds(c * P + META, P)],
                                       start=True, stop=True)
                    mm.then_inc(E["gates"], 1)
                for l in range(LEVELS):
                    for g in range(2):
                        G, E, b = group[g], chunk[g], 4 * g
                        pe.wait_ge(E["masked"], c * LEVELS + l + 1)
                        if l == 0:
                            pe.wait_ge(E["expd"], c * 3 + 2)
                        else:
                            pe.wait_ge(E["inv"], y_step(c, l - 1))
                        for h in range(G4):
                            mm = pe.matmul(ps[:, b, h * P:(h + 1) * P], G["lm"][:, l % 2, h, :],
                                           G["y"][:, h, :] if l else ident, start=True, stop=True)
                        mm.then_inc(E["prod"], 1)
                        if l == 0:
                            for h in range(G4):
                                mm = pe.transpose(ps[:, b + 1, h * P:(h + 1) * P], G["k"][:, h, :], ident)
                            mm.then_inc(E["ktok"], 1)
                    for g in range(2 if l else 0):
                        G, E, b = group[g], chunk[g], 4 * g
                        pe.wait_ge(E["pcopy"], c * (LEVELS - 1) + l)
                        if l >= 2:
                            pe.wait_ge(E["inv"], y_step(c, l - 1, 1))
                        for h in range(G4):
                            mm = pe.matmul(ps[:, b + 2, h * P:(h + 1) * P], G["x"][:, h, :], G["lp"][:, 1, h, :],
                                           start=True, stop=True)
                        mm.then_inc(E["delta"], 1)
                    for g in range(2 if 0 < l < LEVELS - 1 else 0):
                        G, E, b = group[g], chunk[g], 4 * g
                        for h in range(G4):
                            mm = pe.matmul(ps[:, b + 3, h * P:(h + 1) * P], G["lp"][:, 1, h, :], G["x"][:, h, :],
                                           start=True, stop=True)
                        mm.then_inc(E["delta"], 1)
                for g in range(2):
                    G, E, b = group[g], chunk[g], 4 * g
                    pe.wait_ge(E["inv"], y_step(c, LEVELS - 1))
                    pe.wait_ge(E["kbg"], c + 1)
                    for h in range(G4):
                        mm = pe.matmul(ps[:, b, h * P:(h + 1) * P], G["gb"][:, h, :], G["y"][:, h, :], start=True, stop=True)
                    mm.then_inc(E["wt"], 1)
                for g in range(2):
                    G, E, b = group[g], chunk[g], 4 * g
                    pe.wait_ge(E["vb"], c + 1)
                    pe.wait_ge(E["nw"], c + 1)
                    pe.wait_ge(E["state"], c + 1)
                    for h in range(G4):
                        dst = ps[:, b + 2 + h // 2, h % 2 * DV:(h % 2 + 1) * DV]
                        vb = G["lm"][:, h // 2, h % 2 * 2:h % 2 * 2 + 2, :].rearrange("p a n -> p (a n)")
                        pe.matmul(dst, G["y"][:, h, :], vb, start=True, stop=False)
                        mm = pe.matmul(dst, G["x"][:, h, :], S[:, g * G4 + h, :], start=False, stop=True)
                    mm.then_inc(E["vn"], 1)
                for g in range(2):
                    G, E, b = group[g], chunk[g], 4 * g
                    pe.wait_ge(E["vnc"], c + 1)
                    for h in range(G4):
                        for e in range(2):
                            dst = ps[:, b + h // 2, (h % 2 * 2 + e) * P:(h % 2 * 2 + e + 1) * P]
                            pe.matmul(dst, S[:, g * G4 + h, e * P:(e + 1) * P], G["q"][:, h, :], start=True, stop=False)
                            mm = pe.matmul(dst, G["lp"][:, h // 2, h % 2 * 2 + e, :], G["dt"][:, h, :], start=False, stop=True)
                    mm.then_inc(E["o"], 1)
                    for h in range(G4):
                        dst = ps[:, b + 2 + h // 2, h % 2 * DV:(h % 2 + 1) * DV]
                        vn = G["lp"][:, h // 2, h % 2 * 2:h % 2 * 2 + 2, :].rearrange("p a n -> p (a n)")
                        mm = pe.matmul(dst, G["k"][:, h, :], vn, start=True, stop=True)
                    mm.then_inc(E["sd"], 1)

            for g in range(2):
                pe.wait_ge(chunk[g]["oc"], 1 + NT)
                pe.wait_ge(chunk[g]["state"], 1 + NT)
            for i, slabs in groups(pe, dn_z):
                for r in slabs:
                    for m in range(2):
                        pe_tile(pe, dn_z, i, r, m, x_meta)
                    n = i * R + r
                    pe.wait_ge(o_sq, n + 1)
                    pe.wait_ge(o_rs, n + 1)
                    for e in range(2):
                        mm = pe.matmul(ps[:, 6, :], ones[:, :], NSQ[:, e, 0:SEQ], start=e == 0, stop=e == 1)
                    mm.then_inc(o_sum, 1)
            pe.wait_ge(z_done, 2 + 2 * HEADS)
            for i, slabs in groups(pe, sb_qk):
                for r in slabs:
                    for m in range(2):
                        t = 2 * r + m
                        pe_tile(pe, sb_qk, i, r, m, x_all, True)
                        if t:
                            head_pe(pe, sb_qk, i, t - 1, i * (2 * R) + (t - 1))
                head_pe(pe, sb_qk, i, 2 * R - 1, i * (2 * R) + (2 * R - 1))
            def sv_turn(t):
                taken(pe, sb_v, 0, t)
                pe.wait_ge(sv_done, t)
                for c in range(NT):
                    pe.transpose(ps[:, 6, c * P:(c + 1) * P], NSQ[:, t % 2, META + c * P:META + (c + 1) * P], ident)
                pe.transpose(ps[0:META, 7, 0:P], NSQ[:, t % 2, 0:META], ident).then_inc(sv_t, 1)

            pe.wait_ge(h_done, 1 + 2 * HEADS)
            for t in range(KD):
                pe_tile(pe, sb_v, 0, t // 2, t % 2, x_all, True)
                if t:
                    sv_turn(t - 1)
            sv_turn(KD - 1)
            taken(pe, sb_v, 0, 2 * sb_v.nslab - 1)
            taken(pe, sb_v, 0, 2 * sb_v.nslab - 2)

            def sb_turn(i, par, more):
                n = i * 2 + par
                zs = sbz[:, par, :]
                if more:
                    sb_logits(pe, i, par + 1)
                pe.wait_ge(sb_n, n + 1)
                pe.wait_ge(sb_lw, n * 2 + 2)
                later = {0: (1, 3, 2), 4: (0, 1, 3, 2), 1: (3, 2), 3: (2,), 2: ()}
                for t, after in later.items():
                    c, q0, k0, m = SB[t]
                    dst = sb_bank(4, t)
                    mm = pe.matmul(dst, tril[0:m, 0:m], sb_keys(sbn, t), start=True, stop=not after)
                    for a in after:
                        qa = SB[a][1]
                        mm = pe.matmul(dst[:, qa - q0:], ones[:, 0:m], sb_keys(sbn, a), start=False, stop=a == after[-1])
                mm.then_inc(sb_c, 1)
                pe.wait_ge(sb_w, n * 2 + 1)
                pe.wait_ge(sb_v_in, n * 2 + 2)
                if more:
                    pe.wait_ge(sb_zs, n + 4)
                for a, t in enumerate((0, 1, 3, 2, 4)):
                    c, q0, k0, m = SB[t]
                    if t == 4:
                        pe.wait_ge(sb_w, n * 2 + 2)
                    mm = pe.matmul(ps[:, 0, q0:SEQ], sbv[0:m, SB_V[t], :], sb_keys(zs, t), start=a == 0, stop=a == 4)
                mm.then_inc(sb_o, 1)

            sb_logits(pe, 0, 0)
            with pe.Fori(0, HEADS // 2 - 1) as i:
                sb_turn(i, 0, True)
                sb_turn(i, 1, True)
            sb_turn(HEADS // 2 - 1, 0, True)
            sb_turn(HEADS // 2 - 1, 1, False)
            pe.wait_ge(sb_oc, 2 + HEADS)
            pe_gemm(pe, gate_dn, x_meta)
            pe.wait_ge(split_x, NT)
            pe_gemm_pair(pe, branch_dn, lambda k: [y[:, :, k // 2, k % 2 * P:(k % 2 + 1) * P] for y in (VOH, VOL)])
            ada_after = lambda gm: lambda r: [ada_pe(pe, 0, c) for c in ada_units(gm, r)]
            pe_gemm(pe, gate_sb, x_meta, after=ada_after(gate_sb))
            pe.wait_ge(split_x, NT + KD)
            pe_gemm(pe, branch_sb, lambda k: (OSH[:, k, :], OSL[:, k, 0:SEQ]), after=ada_after(branch_sb))
            pe_gemm(pe, mix_out, lambda k: (MGH[:, k, :], MGL[:, k, :]), lambda k: (merged, k + 1), ada_after(mix_out),
                    norm_after(pe, 1))
            norm_pe(pe, 1, SEQ, [KD - 1])
            for i, slabs in groups(pe, ffn_in):
                for r in slabs:
                    for m in range(2):
                        pe_tile(pe, ffn_in, i, r, m, x_hn, ready=lambda k: (n_out, KD + k + 1))
                    for c in ada_units(ffn_in, r):
                        ada_pe(pe, i, c)
            x_act = lambda k: (AFH[:, k, :], AFL[:, k, :])

            def ffn_after(t):
                ada_after(ffn_out)(t)
                norm_after(pe, 2)(t)

            pe_gemm_pair(pe, ffn_out, x_act, lambda q: (f_split, KF // (2 - q)), ffn_after)

            norm_pe(pe, 2, SEQ, [KD - 1])
            pe.wait_ge(mod_done, 1)

            def qk_sum(t):
                pe.wait_ge(h_sq, 2 * HEADS + t + 1)
                pe.wait_ge(h_rs, 2 * HEADS + t + 1)
                pe.matmul(ps[:, 6, :], pair_ones, NSQ[:, t % 2, 0:SEQ], start=True, stop=True).then_inc(h_sum, 1)

            def qk_rot(t):
                pe.wait_ge(a_nrm, t + 1)
                if t:
                    pe.wait_ge(a_done, t)
                pe.matmul(ps[:, 7, :], rot, QG[:, GQ_TILES[t][2], :], start=True, stop=True).then_inc(a_rot, 1)

            def k_dup(g):
                pe.wait_ge(a_done, 1 + g // 2)
                if g >= 2:
                    pe.wait_ge(a_dupc, g - 1)
                pe.matmul(ps[:, 4 + g % 2, :], (dup0, dup1)[g % 2], QG[:, KD + g // 2, :], start=True, stop=True).then_inc(a_dup, 1)

            for n, (gm, t, _) in enumerate(GQ_TILES):
                pe_tile(pe, gm, 0, t // 2, t % 2, x_hn, ready=lambda k: (n_out, 2 * KD + k + 1))
                if n >= 1:
                    qk_sum(n - 1)
                if n >= 2:
                    qk_rot(n - 2)
                if n in (5, 7):
                    k_dup(n - 5)
                    k_dup(n - 4)
            qk_sum(9)
            qk_rot(8)
            for t in range(2):
                pe_tile(pe, gq_v, 0, 0, t, x_hn)
                if t == 0:
                    qk_rot(9)
            pe.wait_ge(a_dupc, KVH)
            for t in range(2):
                taken(pe, gq_v, 0, t)
                for c in range(NT):
                    mm = pe.transpose(ps[:, 4 + t, c * P:(c + 1) * P], NSQ[:, t, c * P:(c + 1) * P], ident)
                mm.then_inc(sv_t, 1)

            def scores(g, j):
                n = g * 4 + j
                pe.wait_ge(a_qk, g * 2 + 2)
                x = slice(j % 2 * HD, (j % 2 + 1) * HD)
                for q in range(NT):
                    pe.wait_ge(a_e, n * NT + q + 1)
                    pe.matmul(ps[:, q, :], qst[x, j // 2, q * P:(q + 1) * P], kst[x, :], start=True, stop=True).then_inc(a_s, 1)

            def gq_turn(g, more):
                for j in range(4):
                    n = g * 4 + j
                    if j < 3:
                        scores(g, j + 1)
                    elif more:
                        scores(g + 1, 0)
                    for q in range(NT):
                        pe.wait_ge(a_p, n * NT + q + 1)
                        pe.wait_ge(a_tc, n * NT + q + 1)
                        for kt in range(NT):
                            mm = pe.transpose(ps[:, 4 + q % 2, kt * P:(kt + 1) * P], PB[:, j % 2, q, kt * P:(kt + 1) * P], ident)
                        mm.then_inc(a_t, 1)
                    pe.wait_ge(a_tc, n * NT + NT + 2)
                    pe.wait_ge(a_v, g + 1)
                    pe.wait_ge(a_oc, g * 2 + j // 2 + 1)
                    x = slice(j % 2 * HD, (j % 2 + 1) * HD)
                    for kt in range(NT):
                        mm = pe.matmul(ps[x, 6 + j // 2, :], vst[:, kt, :], PTB[:, j % 2, kt, :], start=kt == 0, stop=kt == NT - 1)
                    mm.then_inc(a_o, 1)

            scores(0, 0)
            pe.wait_ge(sv_done, KD + 1 + 2)
            with pe.Fori(0, KVH - 1) as g:
                gq_turn(g, True)
            gq_turn(KVH - 1, False)
            pe.wait_ge(a_e, (1 + QH) * NT)
            pe.wait_ge(a_oc, 2 + QH // 2)
            pe_gemm(pe, gq_out, lambda k: (OGH[:, k, :], OGL[:, k, :]), lambda k: (split_x, NT + KD + k + 1), tile_after=norm_after(pe, 3))

            def pe_conv_ffn(l, u):
                norm_pe(pe, u, SEQ, [KD - 1])
                pe_gemm(pe, fc_in[l], x_hn, lambda k: (n_out, u * KD + k + 1))
                pe_gemm_pair(pe, fc_out[l], x_act, lambda q: (f_split, (l + 1) * KF + KF // (2 - q)), norm_after(pe, u + 1))

            pe_conv_ffn(0, 3)
            norm_pe(pe, 4, SEQ, [KD - 1])
            pe.wait_ge(y_in, 48)
            pe.matmul(ps[0:FW, 7, :], W1[:, :], POS[:, :], start=True, stop=True).then_inc(y_mlp, 1)
            pe_gemm(pe, hy_in, x_hn, lambda k: (n_out, 4 * KD + k + 1))
            pe.wait_ge(y_sin, 1)
            pe.matmul(ps[0:FW, 6, :], W2[:, :], A1[:, 0, :], start=True, stop=True).then_inc(y_mlp, 1)
            pe.wait_ge(y_sin, 2)
            taken(pe, hy_in, 2, 2 * R - 1)
            taken(pe, hy_in, 2, 2 * R - 2)
            even_odd = lambda x, n: x.rearrange("p (h i e) -> p e h i", e=2, h=2)[:, n // 2, n % 2, :]

            def filters(u, tiles):
                for t in tiles:
                    if t == 0:
                        pe.wait_ge(y_w, u * 32 + 32)
                        if not isinstance(u, int) or u:
                            pe.wait_ge(y_kc, u * 2)
                    if t >= 2:
                        pe.wait_ge(y_pm, u * NT + t + 1)
                    for s in range(2):
                        mm = pe.matmul(ps[:, t % 2 * 2 + s, :], even_odd(A1[:, 1, :], t), W3[:, s, :], start=True, stop=True)
                    mm.then_inc(y_f, 1)

            def filter_norm(u):
                pe.wait_ge(y_n, u * NT + NT + 1)
                pe.wait_ge(y_pm, u * NT + NT + 1)
                for c in range(NT):
                    mm = pe.matmul(ps[:, 0, c:c + 1], AS[:, c * P:(c + 1) * P], ones[:, 0:1], start=True, stop=True)
                mm.then_inc(y_f, 1)

            def filters_start():
                filters(0, range(NT))
                filter_norm(0)

            def hyena_pair(o, more):
                for dh in range(2):
                    u = o * 2 + dh
                    pe.wait_ge(y_z, u * NT + 1)
                    for t in range(NT):
                        if t >= 2:
                            pe.wait_ge(y_tc, u * NT + t - 1)
                        for c in range(NT):
                            mm = pe.transpose(ps[:, 4 + t % 2, c * P:(c + 1) * P], even_odd(U[:, dh * NT + c, :], t), ident)
                        mm.then_inc(y_t, 1)
                    pe.wait_ge(y_pm, u * NT + NT + 2)
                    pe.wait_ge(y_rn, u + 1)
                    for f in range(2):
                        fs = slice(f * P, (f + 1) * P)
                        if f:
                            pe.wait_ge(y_kc, u * 2 + f)
                        for s in range(2):
                            for t in range(NT):
                                mm = pe.matmul(ps[:, s * 2 + t // 2, :], t_fwd[:, s, t, fs], PM[:, s, t, :],
                                               start=t % 2 == 0, stop=t % 2 == 1)
                        mm.then_inc(y_k, 1)
                        pe.wait_ge(y_tc, u * NT + NT)
                        pe.wait_ge(y_z, u * NT + 5)
                        if f:
                            pe.wait_ge(y_zc, u * 2 + f)
                            pe.wait_ge(y_x, u * 2 + f + 1)
                        for s in range(2):
                            for t in range(NT):
                                mm = pe.matmul(ps[:, 4 + s * 2 + t // 2, :], t_fwd[:, s, t, fs], ZK[:, t, :],
                                               start=t % 2 == 0, stop=t % 2 == 1)
                        mm.then_inc(y_dft, 1)
                    following = dh == 0 or more
                    if following:
                        filters(u + 1, range(2))
                    pe.wait_ge(y_y, u * 2 + 3)
                    for c in range(NT):
                        if c == 2 and following:
                            filters(u + 1, range(2, NT))
                        if c >= 2:
                            pe.wait_ge(y_z, u * NT + c + 4)
                        for e in range(2):
                            ts = slice(e * SEQ // 2, (e + 1) * SEQ // 2)
                            for f in range(2):
                                for s in range(2):
                                    mm = pe.matmul(ps[:, 6 + c % 2, ts], YF[:, f, e * 2 + s, c * P:(c + 1) * P], t_inv[:, s, f, ts],
                                                   start=f + s == 0, stop=f + s == 2)
                        mm.then_inc(y_inv, 1)
                    if following:
                        filter_norm(u + 1)

            pe.wait_ge(y_conv, 3 * KD)
            pe.wait_ge(table_full, 32)
            hyena_units(pe, filters_start, hyena_pair)
            pe_gemm(pe, hy_out, lambda k: (ZH[:, k, :], ZL[:, k, :]), lambda k: (split_x, NT + 2 * KD + k + 1), tile_after=norm_after(pe, 5))
            pe_conv_ffn(1, 5)
            norm_pe(pe, 6, SEQ, [KD - 1])
            for n in range(NT):
                for h in range(2):
                    pe.wait_ge(n_out, 6 * KD + (KD if n else 4 * (h + 1)))
                    if n >= 1:
                        pe.wait_ge(f_out, 2 * n + h - 1)
                    for k in range(4):
                        mm = pe.transpose(ps[:, 4 + h, k * P:(k + 1) * P], HN[:, 4 * h + k, n * P:(n + 1) * P], ident)
                    mm.then_inc(f_t, 1)

        @block.scalar
        def _(act):
            act.sem_inc(silu_done, 2)
            act.sem_inc(l2_rs, 1)
            act.sem_inc(o_rs, 1)
            act.sem_inc(h_rs, 1)
            act.sem_inc(sb_zs, 2)
            act.sem_inc(sb_oc, 2)
            act.sem_inc(a_e, NT)
            act.sem_inc(a_tc, 2)
            act.sem_inc(a_oc, 2)
            for g in range(2):
                act.sem_inc(chunk[g]["oc"], 1)
            act.dma_start(mt[:, :], A["meta_tokens"]).then_inc(x_in, 16)
            act.dma_start(square[:, :, :].rearrange("p a b -> p (a b)"), A["t_square"]).then_inc(table_in, 16)
            act.wait_ge(cleared, 1)
            load_rows(act, act_small_in, "conv_q", tile(A["conv_q"][0]))
            load_rows(act, act_small_in, "conv_k", tile(A["conv_k"][0]))
            load_rows(act, act_small_in, "conv_v", tile(A["conv_v"][0]))
            for part in range(2):
                for name, src in (("gq", A["attn_q_gain_2"]), ("gk", A["attn_k_gain_2"])):
                    r = ROWS[name][0]
                    act.dma_start(prow[r % P:r % P + 1, r // P, part * HD:(part + 1) * HD], src).then_inc(act_small_in, 16)
            load_rows(act, act_small_in, "c", tile(A["c_2"]))
            load_rows(act, act_small_in, "skip", tile(A["hy_skip_2"][0]))
            load_rows(act, act_small_in, "hy_w", tile(A["hy_conv_w_2"][0]))
            load_rows(act, act_small_in, "hy_b", tile(A["hy_conv_b_2"]))
            load_rows(act, act_small_in, "ada_b", tile(A["ada_b_2"]))
            for l in range(2):
                load_rows(act, act_small_in, f"fc_w{l}", tile(A["ffn_conv_w_2"][l]))
                load_rows(act, act_small_in, f"fc_b{l}", tile(A["ffn_conv_b_2"][l:l + 1]))
            norm_act(act, 0, lambda k: H[:, k, :], T, tile=lambda k: act.wait_ge(t_done, 2 * (k + 1)))
            def conv_in(gm, i, t):
                b = acc_in(act, gm, i, t)
                act.activation(split(xpad[:, t % 2, 3:3 + T]), half(2 * b), ACT.Copy).then_inc(acc_free[b], 1)

            for i, slabs in groups(act, dn_qk):
                for t in range(2 * R):
                    conv_in(dn_qk, i, t)
                    act.wait_ge(conv_done, i * (2 * R) + t + 1)
                    act.activation(QK[:, ds(i * (2 * R) + t, 1), :], cv[:, t % 2:t % 2 + 1, :], ACT.Silu)\
                        .then_inc(silu_done, 1)
            act.wait_ge(ab_ready, 1)
            act.activation(split(abT[:, :]), half(4, 16), ACT.Copy).then_inc(ab_l, 1)
            act.preload_act_table_set(LN_EXP)
            act.wait_ge(ab_x, 1)
            act.activation(soft[:, 1, :, 0:8], soft[:, 1, :, 0:8], ACT.Exp, bias=zero, scale=-1.0)
            act.drain()
            act.activation(soft[:, 1, :, 0:8], soft[:, 1, :, 0:8], ACT.Ln, bias=ones[:, 0:1], scale=1.0)
            act.activation(ab[:, 0:8], ab[:, 0:8], ACT.Exp, bias=zero, scale=1.0)
            act.activation(b_tok[:, :, :], soft[:, 0, :, 8:16], ACT.Sigmoid, bias=zero, scale=1.0).then_inc(ab_l, 1)

            for i, slabs in groups(act, dn_v):
                for t in range(2 * R):
                    n = i * (2 * R) + t
                    act.wait_ge(silu_done, 2 + 16)
                    act.wait_ge(l2_sum, n + 1)
                    act.activation(NSQ[:, t % 2:t % 2 + 1, :], QK[:, ds(n, 1), :], ACT.Square).then_inc(l2_sq, 1)
                    conv_in(dn_v, i, t)
                    act.preload_act_table_set(LN_EXP)
                    act.wait_ge(l2_sum, n + 3)
                    act.wait_ge(l2_done, n + 1)
                    act.activation(split(RSB[:, :]), half(4), ACT.Ln, bias=eps, scale=1.0)
                    act.drain()
                    act.activation(RSB[:, :], RSB[:, :], ACT.Exp, bias=zero, scale=-0.5).then_inc(l2_rs, 1)
                    act.preload_act_table_set(SILU)
                    act.wait_ge(conv_done, n + 17)
                    act.activation(cv[:, t % 2, :], cv[:, t % 2, :], ACT.Silu).then_inc(silu_done, 1)

            act.wait_ge(m_dve, 3)
            act.activation(ml[:, :, :], ml[:, :, :], ACT.Exp, bias=zero[0:META], scale=1.0)
            act.activation(msm[:, 1, :], msm[:, 1, :], ACT.Exp, bias=zero[0:META], scale=1.0).then_inc(m_act, 1)
            with act.Fori(0, NT) as c:
                for g in range(2):
                    G, E, b = group[g], chunk[g], 4 * g
                    act.wait_ge(E["expin"], c + 1)
                    act.activation(G["lp"][:, 0, :, :], G["lp"][:, 0, :, :], ACT.Exp, bias=zero, scale=1.0).then_inc(E["expd"], 1)
                for g in range(2):
                    G, E, b = group[g], chunk[g], 4 * g
                    act.activation(G["x"][:, :, :], ps[:, b, :].rearrange("p (h n) -> p h n", h=G4), ACT.Exp, bias=zero, scale=1.0)\
                        .then_inc(E["expd"], 1)
                for g in range(2):
                    G, E, b = group[g], chunk[g], 4 * g
                    act.activation(G["dt"][:, :, :], G["dt"][:, :, :], ACT.Exp, bias=zero, scale=1.0)
                    act.activation(G["sm"][:, 2:4, :], G["sm"][:, 0:2, :], ACT.Exp, bias=zero, scale=1.0).then_inc(E["expd"], 1)
                for l in range(1, LEVELS):
                    for g in range(2):
                        G, E, b = group[g], chunk[g], 4 * g
                        act.wait_ge(E["prod"], c * LEVELS + l + 1)
                        act.activation(G["lp"][:, 1, :, :], ps[:, b, :].rearrange("p (h n) -> p h n", h=G4), ACT.Copy)\
                            .then_inc(E["pcopy"], 1)
                for g in range(2):
                    G, E, b = group[g], chunk[g], 4 * g
                    act.wait_ge(E["wt"], c + 1)
                    act.activation(G["x"][:, :, :], ps[:, b, :].rearrange("p (h n) -> p h n", h=G4), ACT.Copy, scale=-1.0)\
                        .then_inc(E["nw"], 1)
                for g in range(2):
                    G, E, b = group[g], chunk[g], 4 * g
                    act.wait_ge(E["vn"], c + 1)
                    act.activation(G["lp"][:, :, :, :].rearrange("p a h n -> p a (h n)"), ps[:, b + 2:b + 4, :], ACT.Copy)\
                        .then_inc(E["vnc"], 1)
                for g in range(2):
                    G, E, b = group[g], chunk[g], 4 * g
                    act.wait_ge(E["o"], c + 1)
                    act.activation(VO[:, ds(c, 1), g * G4:(g + 1) * G4, :].rearrange("p c h n -> p (c h n)"),
                                   ps[:, b:b + 2, :].rearrange("p a n -> p (a n)"), ACT.Copy).then_inc(E["oc"], 1)

            act.drain()
            for i, slabs in groups(act, dn_z):
                for t in range(2 * R):
                    n = i * R + t // 2
                    if t % 2 == 0:
                        if t:
                            act.wait_ge(o_sum, n)
                        act.activation(NSQ[:, :, 0:SEQ].rearrange("p e (c n) -> p e c n", n=P),
                                       VO[:, :, ds(n, 1), :].rearrange("p c a (e n) -> p e (c a) n", e=2), ACT.Square)\
                            .then_inc(o_sq, 1)
                    act.wait_ge(z_done, i * (2 * R) + t + 1)
                    b = acc_in(act, dn_z, i, t)
                    act.activation(ZT[:, t % 2, :], ps[:, 2 * b, :], ACT.Silu).then_inc(acc_free[b], 1)
                    if t % 2 == 0:
                        act.preload_act_table_set(LN_EXP)
                        act.wait_ge(o_sum, n + 1)
                        act.wait_ge(z_done, n * 2 + 2)
                        act.activation(NRS[:, 0:SEQ], ps[:, 6, :], ACT.Ln, bias=eps, scale=1.0 / DV)
                        act.drain()
                        act.activation(NRS[:, 0:SEQ], NRS[:, 0:SEQ], ACT.Exp, bias=zero, scale=-0.5).then_inc(o_rs, 1)

            def head_rs(i, t, scale):
                n = i * (2 * R) + t
                act.wait_ge(h_sum, n + 3)
                act.wait_ge(h_done, n + 1)
                act.activation(split(NRS[:, :]), half(6), ACT.Ln, bias=eps, scale=scale)
                act.drain()
                act.activation(NRS[:, :], NRS[:, :], ACT.Exp, bias=zero, scale=-0.5).then_inc(h_rs, 1)

            act.preload_act_table_set(LN_EXP)
            act.wait_ge(z_done, 2 + 2 * HEADS)
            for i, slabs in groups(act, sb_qk):
                for t in range(2 * R):
                    n = i * (2 * R) + t
                    act.wait_ge(h_sum, n + 1)
                    b = acc_in(act, sb_qk, i, t)
                    act.activation(split(NSQ[:, t % 2, :]), half(2 * b), ACT.Square).then_inc(h_sq, 1)
                    act.activation(split(QSK[:, ds(n, 1), :].rearrange("p a n -> p (a n)")), half(2 * b), ACT.Copy)\
                        .then_inc(acc_free[b], 1)
                    if t:
                        head_rs(i, t - 1, 1.0 / P)
                head_rs(i, 2 * R - 1, 1.0 / P)

            def sb_evac(n, par):
                act.wait_ge(sb_z, n + 1)
                if not isinstance(n, int) or n:
                    act.wait_ge(sb_o, n)
                s = float(P) ** -0.5
                act.activation(sbz[:, par, 0:8 * P].rearrange("p (a n) -> p a n", a=2), ps[:, 0:2, :], ACT.Copy, scale=s)
                act.activation(sbz[:, par, 8 * P:SBX], ps[:, 2, 0:2 * P], ACT.Copy, scale=s)
                act.activation(sbz[0:META, par, SBX:SBW], ps[0:META, 3, :], ACT.Copy, scale=s).then_inc(sb_zs, 1)

            def sb_log(n):
                act.wait_ge(sb_abs, n + 1)
                act.activation(sbe[:, :], sbe[:, :], ACT.Exp, bias=zero, scale=-1.0)
                act.drain()
                act.activation(sbe[:, :], sbe[:, :], ACT.Ln, bias=ones[:, 0:1], scale=1.0).then_inc(sb_ln, 1)

            def sb_turn(i, par, more):
                n = i * 2 + par
                if more:
                    sb_evac(n + 1, 1 - par)
                    sb_log(n + 1)
                act.wait_ge(sb_lw, n * 2 + 3)
                act.activation(sbz[:, par, 0:SBX], sbz[:, par, 0:SBX], ACT.Exp, bias=zero, scale=1.0).then_inc(sb_w, 1)
                act.wait_ge(sb_lw, n * 2 + 4)
                act.activation(sbz[0:META, par, SBX:SBW], sbz[0:META, par, SBX:SBW], ACT.Exp, bias=zero[0:META], scale=1.0)\
                    .then_inc(sb_w, 1)
                act.wait_ge(sb_o, n + 2)
                act.activation(QSK[:, ds(n, 1), 0:SEQ].rearrange("p a n -> p (a n)"), ps[:, 0, :], ACT.Copy).then_inc(sb_oc, 1)

            for t in range(KD):
                if t >= 2:
                    act.wait_ge(sv_t, t - 1)
                b = acc_in(act, sb_v, 0, t)
                act.activation(split(NSQ[:, t % 2, :]), half(2 * b), ACT.Copy).then_inc(acc_free[b], 1)
            act.wait_ge(sv_done, KD + 1)
            sb_evac(0, 0)
            sb_log(0)
            with act.Fori(0, HEADS // 2 - 1) as i:
                sb_turn(i, 0, True)
                sb_turn(i, 1, True)
            sb_turn(HEADS // 2 - 1, 0, True)
            sb_turn(HEADS // 2 - 1, 1, False)
            act.activation(csil[:, :], cols("c", 0, KD), ACT.Silu).then_inc(silu_c, 1)
            for t in range(KD):
                b = acc_in(act, gate_dn, 0, t)
                act.activation(MG[:, t, :], ps[:, 2 * b, :], ACT.Sigmoid).then_inc(acc_free[b], 1)
            for t in range(KD):
                taken(act, branch_dn, t // R, t % R)
                b = acc_in(act, gate_sb, 0, t)
                act.activation(GT[:, t, :], ps[:, 2 * b, :], ACT.Sigmoid).then_inc(acc_free[b], 1)
            norm_act(act, 1, lambda k: H[:, k, META:T], SEQ, tile=lambda k: taken(act, mix_out, 0, k))
            for i, slabs in groups(act, ffn_in):
                for r in slabs:
                    taken(act, ffn_in, i, 2 * r - 3)
                    b = acc_in(act, ffn_in, i, 2 * r)
                    act.activation(SG[:, r % 2, :], ps[:, 2 * b, :], ACT.Silu).then_inc(acc_free[b], 1)

            def residual(gm):
                return lambda k: taken(act, gm, 0, k)

            norm_act(act, 2, lambda k: H[:, k, META:T], SEQ, shift_of(0, 0), tile=residual(ffn_out))

            def qk_rs(t):
                act.wait_ge(h_sum, 2 + 2 * HEADS + t + 1)
                act.wait_ge(h_done, 1 + 2 * HEADS + t)
                act.activation(NRS[:, 0:SEQ], ps[:, 6, :], ACT.Ln, bias=eps, scale=1.0 / HD)
                act.drain()
                act.activation(NRS[:, 0:SEQ], NRS[:, 0:SEQ], ACT.Exp, bias=zero, scale=-0.5).then_inc(h_rs, 1)

            act.wait_ge(n_out, 3 * KD)
            def k_both(g):
                act.wait_ge(a_dup, g + 1)
                act.activation(KDUP[:, g, :], ps[:, 4 + g % 2, :], ACT.Copy).then_inc(a_dupc, 1)

            for n, (gm, t, place) in enumerate(GQ_TILES):
                act.wait_ge(h_sum, 2 * HEADS + n + 1)
                b = acc_in(act, gm, 0, t)
                act.activation(NSQ[:, n % 2, 0:SEQ], ps[:, 2 * b, :], ACT.Square).then_inc(h_sq, 1)
                act.activation(QG[:, place, :], ps[:, 2 * b, :], ACT.Copy).then_inc(acc_free[b], 1)
                if n:
                    qk_rs(n - 1)
                if n in (5, 7):
                    k_both(n - 5)
                    k_both(n - 4)
            qk_rs(9)
            for t in range(2):
                b = acc_in(act, gq_v, 0, t)
                act.activation(NSQ[:, t, 0:SEQ], ps[:, 2 * b, :], ACT.Copy).then_inc(acc_free[b], 1)

            def exps(g, j):
                n = g * 4 + j
                act.wait_ge(a_t, n * NT + 1)
                for q in range(NT):
                    act.wait_ge(a_mx, n * NT + q + 1)
                    act.activation(PB[:, j % 2, q, :], ps[:, q, :], ACT.Exp, bias=asm[:, j % 2, 1, q:q + 1],
                                   scale=float(HD) ** -0.5, accum_out=asm[:, j % 2, 2, q:q + 1]).then_inc(a_e, 1)

            def gq_turn(g, more):
                for j in range(4):
                    n = g * 4 + j
                    act.wait_ge(a_o, n + 1)
                    for q in range(NT):
                        act.wait_ge(a_t, n * NT + q + 6)
                        act.activation(PTB[:, j % 2, :, q * P:(q + 1) * P], ps[:, 4 + q % 2, :].rearrange("p (k n) -> p k n", k=NT),
                                       ACT.Copy).then_inc(a_tc, 1)
                    if j < 3:
                        exps(g, j + 1)
                    elif more:
                        exps(g + 1, 0)
                    if j % 2:
                        act.wait_ge(a_o, n + 3)
                        o = lambda x: x[:, ds(g * 2 + j // 2, 1), :].rearrange("p a n -> p (a n)")
                        act.activation(o(OG), ps[:, 6 + j // 2, :], ACT.Copy)
                        act.activation(o(OGH), ps[:, 6 + j // 2, :], ACT.Copy).then_inc(a_oc, 1)

            exps(0, 0)
            with act.Fori(0, KVH - 1) as g:
                gq_turn(g, True)
            gq_turn(KVH - 1, False)

            def act_conv_ffn(l, u):
                norm_act(act, u, lambda k: H[:, k, META:T], SEQ, shift_of(l, 1), tile=residual((gq_out, hy_out)[l]))
                act.wait_ge(n_out, (u + 1) * KD)
                for i, slabs in groups(act, fc_in[l]):
                    for r in slabs:
                        b = acc_in(act, fc_in[l], i, 2 * r)
                        act.activation(GP[:, r % 2, 1:SEQ + 1], ps[:, 2 * b, :], ACT.Copy).then_inc(acc_free[b], 1)
                        act.wait_ge(fc_conv, i * R + (l * KF + r + 1))
                        act.activation(SG[:, r % 2, :], SG[:, r % 2, :], ACT.Silu).then_inc(fc_silu, 1)

            act_conv_ffn(0, 3)
            def sin_of(n):
                act.wait_ge(y_arg, n + 1)
                act.activation(A1[:, n, :], A1[:, n, :], ACT.Sin, bias=zero[0:FW], scale=1.0).then_inc(y_sin, 1)

            norm_act(act, 4, lambda k: H[:, k, META:T], SEQ, shift_of(1, 0), tile=residual(fc_out[0]))
            act.wait_ge(n_out, 5 * KD)
            sin_of(0)
            for i, slabs in groups(act, hy_in):
                for t in range(2 * R):
                    if t >= 2:
                        act.wait_ge(y_conv, i * (2 * R) + (t - 1))
                    b = acc_in(act, hy_in, i, t)
                    act.activation(UP[:, t % 2, 1:SEQ + 1], ps[:, 2 * b, :], ACT.Copy).then_inc(acc_free[b], 1)
                act.wait_ge(y_conv, i * (2 * R) + 2 * R)
            sin_of(1)

            def filters(u):
                for t in range(NT):
                    act.wait_ge(y_fb, u * NT + t + 1)
                    act.wait_ge(y_n, u * NT + t + 1)
                    act.activation(AB[:, :, :], FB[:, :, :], ACT.Abs).then_inc(y_ab, 1)

            def hyena_pair(o, more):
                for dh in range(2):
                    u = o * 2 + dh
                    for t in range(NT):
                        act.wait_ge(y_t, u * NT + t + 1)
                        act.activation(ZK[:, t, :], ps[:, 4 + t % 2, :], ACT.Copy).then_inc(y_tc, 1)
                    for f in range(2):
                        act.wait_ge(y_k, u * 2 + f + 1)
                        act.wait_ge(y_kp, u * 2 + f + 1)
                        act.activation(KS[:, :, :], ps[:, 0:4, :], ACT.Copy).then_inc(y_kc, 1)
                        act.wait_ge(y_dft, u * 2 + f + 1)
                        act.wait_ge(y_x, u * 2 + f + 1)
                        act.activation(ZS[:, :, :], ps[:, 4:8:2, :], ACT.Copy).then_inc(y_zc, 1)
                    if dh == 0 or more:
                        filters(u + 1)

            hyena_units(act, lambda: filters(0), hyena_pair)
            act_conv_ffn(1, 5)
            norm_act(act, 6, lambda k: H[:, k, META:T], SEQ, hi=False, tile=residual(fc_out[1]))
            for n in range(NT):
                act.wait_ge(f_out, 2 * n + 2)
                act.dma_start(out[n * P:(n + 1) * P, :], OUT[:, n, :]).then_inc(stored, 16)
            act.wait_ge(stored, 16 * NT)

        @block.vector
        def _(dve):
            for b in range(2):
                dve.sem_inc(acc_free[b], 1)
            dve.sem_inc(vt_done, 2)
            dve.sem_inc(l2_done, 1)
            dve.sem_inc(z_done, 2)
            dve.sem_inc(h_done, 1)
            dve.sem_inc(sb_lw, 2)
            dve.sem_inc(y_pm, 2)
            dve.sem_inc(y_z, 1 + NT)
            dve.sem_inc(y_x, 1)
            dve.sem_inc(y_cb, 4)
            for k in range(KD):
                dve.wait_ge(t_ready, 2 * k + 1)
                dve.tensor_copy(H[:, k, META:T], ps[:, k % 2, :]).then_inc(t_done, 1)
                dve.wait_ge(t_ready, 2 * k + 2)
                dve.tensor_copy(H[:, k, 0:META], ps[:, 2 + k % 2, 0:META]).then_inc(t_done, 1)
            dve.wait_ge(t_ready, 2 * KD + 1)
            dve.tensor_copy(pcol[:, :, :].rearrange("p a b -> p (a b)"),
                            ps[:, 4:6, :].rearrange("p a b -> p (a b)")[:, 0:PT * P]).then_inc(t_done, 1)
            dve.memset(soft[:, :, :, :], 0.0)
            dve.drain()
            norm_dve(dve, 0, lambda k: H[:, k, :], lambda k: col("norm_mix", k), T)
            def conv(gm, i, t, taps):
                taken(dve, gm, i, t)
                x, y = xpad[:, t % 2, :], cv[:, t % 2, :]
                dve.tensor_scalar(y, x[:, 0:T], taps(0), None, ALU.mult)
                for j in range(1, 4):
                    dve.drain()
                    ins = dve.scalar_tensor_tensor(y, x[:, j:j + T], taps(j), y, ALU.mult, ALU.add)
                ins.then_inc(conv_done, 1)

            for i, slabs in groups(dve, dn_qk):
                for t in range(2 * R):
                    dve.wait_ge(silu_done, i * (2 * R) + t + 1)
                    conv(dn_qk, i, t, lambda j: dcol("conv_q", i * 32 + (j * 8 + t)))

            dve.wait_ge(ab_ready, 2)
            dve.tensor_copy(soft[:, 0, 0:NT, :], ps[:, 6, 0:NT * 16].rearrange("p (n c) -> p n c", c=16))
            dve.tensor_copy(soft[0:META, 0, NT, :], ps[0:META, 6, NT * 16:(NT + 1) * 16])
            dve.tensor_copy(ab[:, :], ps[:, 7, 0:16])
            dve.drain()
            dve.tensor_tensor(soft[:, 0, :, 0:8], soft[:, 0, :, 0:8], heads_of(ab[:, 8:16], NT + 1), ALU.add)
            dve.drain()
            dve.scalar_tensor_tensor(soft[:, 1, :, 0:8], soft[:, 0, :, 0:8], -1.0, soft[:, 0, :, 0:8], ALU.mult, ALU.max)\
                .then_inc(ab_x, 1)
            dve.wait_ge(ab_l, 2)
            dve.scalar_tensor_tensor(soft[:, 0, :, 0:8], soft[:, 0, :, 0:8], 0.0, soft[:, 1, :, 0:8], ALU.max, ALU.add)
            dve.drain()
            dve.scalar_tensor_tensor(g_tok[:, :, :], soft[:, 0, :, 0:8], -1.0, heads_of(ab[:, 0:8], NT + 1), ALU.mult, ALU.mult)

            def v_out(i, t):
                n = i * (2 * R) + t
                dve.wait_ge(vt_ready, n * 2 + 4 + 1)
                dve.tensor_copy(VO[:, :, :, :].rearrange("p c h (e n) -> p c (h e) n", e=2)[:, :, ds(n, 1), :],
                                ps[:, 6, :].rearrange("p (c a n) -> p c a n", c=NT, a=1)).then_inc(vt_done, 1)
                dve.wait_ge(vt_ready, n * 2 + 4 + 2)
                dve.tensor_copy(vm[:, :, :].rearrange("p h (e n) -> p (h e) n", e=2)[:, ds(n, 1), :],
                                ps[0:META, 7, 0:P].unsqueeze(1)).then_inc(vt_done, 1)

            for i, slabs in groups(dve, dn_v):
                for t in range(2 * R):
                    n = i * (2 * R) + t
                    dve.wait_ge(silu_done, n + 16 + 1)
                    dve.wait_ge(vt_ready, n * 2 + 2)
                    conv(dn_v, i, t, lambda j: dcol("conv_v", i * 8 + (j * 16 + t)))
                    dve.wait_ge(l2_rs, n + 2)
                    dve.tensor_tensor(QK[:, ds(n, 1), :], QK[:, ds(n, 1), :], RSB[:, :].unsqueeze(1), ALU.mult)\
                        .then_inc(l2_done, 1)
                    if t:
                        v_out(i, t - 1)
                v_out(i, 2 * R - 1)

            m = META
            dve.drain()
            dve.tensor_copy(gmb[:, :, :], wide(g_tok[0:m, NT, :], m)).then_inc(m_dve, 1)
            dve.wait_ge(m_pe, 1)
            dve.wait_ge(mask_in, 16)
            dve.tensor_copy(msm[:, 0, :], ps[0:m, 1, 0:HEADS])
            dve.drain()
            h16 = lambda b: ps[0:m, b, 0:HEADS * m].rearrange("p (h n) -> p h n", h=HEADS)
            dve.tensor_tensor(ml[:, :, :], wide(msm[:, 0, :], m), h16(0), ALU.subtract)
            dve.tensor_tensor(msm[:, 1, :], h16(0)[:, :, m - 1], msm[:, 0, :], ALU.subtract).then_inc(m_dve, 1)
            dve.drain()
            dve.tensor_tensor(ml[:, :, :], ml[:, :, :], heads_of(masks[0:m, 1, 0:m], HEADS), ALU.add).then_inc(m_dve, 1)
            dve.wait_ge(m_act, 1)
            dve.tensor_tensor(ml[:, :, :], ml[:, :, :], wide(b_tok[0:m, NT, :], m), ALU.mult)
            dve.drain()
            dve.tensor_tensor(ml[:, :, :], ml[:, :, :], h16(2), ALU.mult)
            dve.drain()
            for l in range(4):
                dve.tensor_tensor(mlm[:, :, :], ml[:, :, :], heads_of(masks[0:m, 2 + l, 0:m], HEADS), ALU.mult)\
                    .then_inc(m_dve, 1)
                dve.wait_ge(m_pe, 2 * l + 2 - (1 if l else 0))
                if l == 0:
                    idn = heads_of(ident[0:m, 0:m], HEADS)
                    dve.tensor_tensor(mx[:, :, :], idn, mlm[:, :, :], ALU.subtract).then_inc(m_dve, 1)
                    dve.tensor_tensor(my[:, :, :], idn, h16(0), ALU.subtract).then_inc(m_dve, 1)
                else:
                    dve.tensor_copy(mp[:, :, :], h16(0)).then_inc(m_dve, 1)
                    dve.wait_ge(m_pe, 2 * l + 2)
                    dve.tensor_tensor(my[:, :, :], my[:, :, :], h16(1), ALU.subtract)
                    dve.tensor_tensor(mx[:, :, :], mx[:, :, :], h16(2), ALU.subtract).then_inc(m_dve, 1)
                dve.drain()
            kt = lambda: ps[0:m, 3:5, :].rearrange("p a (h n) -> p (a h) n", n=P)
            dve.tensor_tensor(km[:, :, :], kt(), wide(msm[:, 1, :]), ALU.mult)
            dve.tensor_tensor(vmb[:, :, :], vm[:, :, :], wide(b_tok[0:m, NT, :], DV), ALU.mult).then_inc(m_dve, 1)
            dve.wait_ge(m_pe, 9)
            dve.tensor_copy(vm[:, :, :], ps[0:m, 4:8, :].rearrange("p a (h n) -> p (a h) n", n=DV)).then_inc(m_dve, 1)
            dve.wait_ge(m_pe, 10)
            dve.tensor_copy(S[:, :, :], ps[:, 0:4, :].rearrange("p a (h n) -> p (a h) n", n=DV)).then_inc(m_dve, 1)
            dve.drain()
            for g in range(2):
                dve.sem_inc(chunk[g]["state"], 1)
            heads4 = lambda bank: ps[:, bank, :].rearrange("p (h n) -> p h n", h=G4)

            def stage_decay(c, g):
                G, E, hs = group[g], chunk[g], slice(g * G4, (g + 1) * G4)
                dve.tensor_copy(G["sm"][:, 6, :], b_tok[:, ds(c, 1), hs].rearrange("p c h -> p (c h)"))
                dve.tensor_copy(G["sm"][:, 7, :], g_tok[:, ds(c, 1), hs].rearrange("p c h -> p (c h)"))
                dve.drain()
                dve.tensor_copy(G["gb"][:, :, :], wide(G["sm"][:, 7, :])).then_inc(E["staged"], 1)

            def stage_k(c, g):
                hs = slice(g * G4, (g + 1) * G4)
                dve.tensor_copy(group[g]["k"][:, :, :], KC[:, hs, ds(c * P + META, P)]).then_inc(chunk[g]["staged"], 1)

            def chunk_dve(c, more):
                for g in range(2):
                    G, E, b = group[g], chunk[g], 4 * g
                    dve.wait_ge(E["gates"], c * 2 + 1)
                    dve.tensor_copy(G["sm"][:, 0, :], ps[:, b + 1, 0:G4])
                    dve.drain()
                    dve.tensor_tensor(G["dt"][:, :, :], heads4(b), wide(G["sm"][:, 0, :]), ALU.subtract)
                    dve.tensor_tensor(G["sm"][:, 1, :], heads4(b)[:, :, P - 1], G["sm"][:, 0, :], ALU.subtract)
                    dve.drain()
                    dve.tensor_tensor(G["lp"][:, 0, :, :], heads_of(masks[:, 1, :], G4), G["dt"][:, :, :], ALU.subtract)
                    dve.tensor_tensor(G["dt"][:, :, :], G["dt"][:, :, :], heads_of(masks[:, 0, :], G4), ALU.add)\
                        .then_inc(E["expin"], 1)
                for g in range(2):
                    G, E, b = group[g], chunk[g], 4 * g
                    dve.wait_ge(E["expd"], c * 3 + 1)
                    dve.tensor_tensor(G["lp"][:, 0, :, :], G["lp"][:, 0, :, :], wide(G["sm"][:, 6, :]), ALU.mult)
                    dve.drain()
                    dve.wait_ge(E["gates"], c * 2 + 2)
                    dve.tensor_tensor(G["lp"][:, 0, :, :], G["lp"][:, 0, :, :], heads4(b + 2), ALU.mult).then_inc(E["lower"], 1)
                q_scale = float(P) ** -0.5
                for g in range(2):
                    G, E, b = group[g], chunk[g], 4 * g
                    hs = slice(g * G4, (g + 1) * G4)
                    dve.wait_ge(E["expd"], c * 3 + 3)
                    dve.scalar_tensor_tensor(G["dt"][:, :, :], heads4(b + 3), q_scale, G["dt"][:, :, :], ALU.mult, ALU.mult)
                    dve.tensor_tensor(G["sm"][:, 4, :], G["sm"][:, 6, :], G["sm"][:, 2, :], ALU.mult)
                    dve.scalar_tensor_tensor(G["q"][:, :, :], QC[:, hs, ds(c * P + META, P)], q_scale, G["x"][:, :, :], ALU.mult, ALU.mult)
                    dve.tensor_copy(G["sm"][:, 5, :], G["x"][:, :, P - 1])
                dve.drain()
                idn = heads_of(ident, G4)
                for g in range(2):
                    G, E, b = group[g], chunk[g], 4 * g
                    dve.wait_ge(E["masked"], c * LEVELS + 1)
                    dve.tensor_tensor(G["x"][:, :, :], idn, G["lm"][:, 0, :, :], ALU.subtract)
                    dve.wait_ge(E["prod"], c * LEVELS + 1)
                    dve.tensor_tensor(G["y"][:, :, :], idn, heads4(b), ALU.subtract).then_inc(E["inv"], 1)
                for g in range(2):
                    G, E, b = group[g], chunk[g], 4 * g
                    dve.wait_ge(E["ktok"], c + 1)
                    dve.tensor_tensor(G["gb"][:, :, :], heads4(b + 1), wide(G["sm"][:, 4, :]), ALU.mult)
                    dve.tensor_tensor(G["k"][:, :, :], heads4(b + 1), wide(G["sm"][:, 3, :]), ALU.mult).then_inc(E["kbg"], 1)
                for l in range(1, LEVELS):
                    for g in range(2):
                        G, E, b = group[g], chunk[g], 4 * g
                        dve.wait_ge(E["delta"], c * (2 * LEVELS - 3) + (2 * l - 1))
                        dve.tensor_tensor(G["y"][:, :, :], G["y"][:, :, :], heads4(b + 2), ALU.subtract).then_inc(E["inv"], 1)
                    for g in range(2 if l < LEVELS - 1 else 0):
                        G, E, b = group[g], chunk[g], 4 * g
                        dve.wait_ge(E["delta"], c * (2 * LEVELS - 3) + 2 * l)
                        dve.tensor_tensor(G["x"][:, :, :], G["x"][:, :, :], heads4(b + 3), ALU.subtract).then_inc(E["inv"], 1)
                for g in range(2):
                    G, E = group[g], chunk[g]
                    vb = G["lm"][:, :, :, :].rearrange("p a h n -> p (a h n)").rearrange("p (h n) -> p h n", h=G4)
                    vsrc = VO[:, ds(c, 1), g * G4:(g + 1) * G4, :].rearrange("p c h n -> p (c h) n")
                    dve.tensor_tensor(vb, vsrc, wide(G["sm"][:, 6, :], DV), ALU.mult).then_inc(E["vb"], 1)
                dve.drain()
                for g in range(2 if more else 0):
                    dve.wait_ge(chunk[g]["wt"], c + 1)
                    stage_decay(c + 1, g)
                for g in range(2):
                    G, E, b = group[g], chunk[g], 4 * g
                    dve.wait_ge(E["sd"], c + 1)
                    if more:
                        stage_k(c + 1, g)
                    for h in range(G4):
                        Sh = S[:, g * G4 + h, :]
                        ins = dve.scalar_tensor_tensor(Sh, Sh, G["sm"][:, 5, h:h + 1],
                                                       ps[:, b + 2 + h // 2, h % 2 * DV:(h % 2 + 1) * DV], ALU.mult, ALU.add)
                    ins.then_inc(E["state"], 1)

            for g in range(2):
                stage_decay(0, g)
                stage_k(0, g)
            with dve.Fori(0, NT - 1) as c:
                chunk_dve(c, True)
            chunk_dve(NT - 1, False)

            for i, slabs in groups(dve, dn_z):
                for t in range(2 * R):
                    n = i * R + t // 2
                    e = t % 2
                    if e == 0:
                        dve.wait_ge(o_rs, n + 2)
                    taken(dve, dn_z, i, t)
                    dve.scalar_tensor_tensor(ZT[:, e, :], ZT[:, e, :], col("dn_gain", e), NRS[:, 0:SEQ], ALU.mult, ALU.mult)
                    dve.drain()
                    o = VO[:, :, ds(n, 1), e * P:(e + 1) * P].rearrange("p c a n -> p c (a n)")
                    dve.tensor_tensor(o, o, ZT[:, e, :].rearrange("p (c n) -> p c n", c=NT), ALU.mult).then_inc(z_done, 1)
            for i, slabs in groups(dve, sb_qk):
                for t in range(2 * R):
                    n = i * (2 * R) + t
                    dve.wait_ge(h_rs, n + 2)
                    qk = QSK[:, ds(n, 1), :]
                    dve.scalar_tensor_tensor(qk, qk, dcol("sbq", i) if not isinstance(i, int) else col("sbq", i),
                                             NRS[:, :].unsqueeze(1), ALU.mult, ALU.mult).then_inc(h_done, 1)
            for t in range(KD):
                dve.wait_ge(sv_t, t + 1)
                dve.tensor_copy(SV[:, 0:NT, t * P:(t + 1) * P], ps[:, 6, :].rearrange("p (n c) -> p n c", n=NT))
                dve.tensor_copy(SV[0:META, NT, t * P:(t + 1) * P], ps[0:META, 7, 0:P]).then_inc(sv_done, 1)
            dve.memset(sbz[:, :, SBX:SBW], 0.0).then_inc(sv_done, 1)

            def sb_abs_of(n, par):
                dve.wait_ge(sb_zs, n + 3)
                z = sbz[:, par, :]
                for c in (0, 4, 7, 8):
                    d = z[:, c * P:(c + 1) * P]
                    dve.tensor_tensor(d, d, vis_neg, ALU.add)
                dve.drain()
                dve.scalar_tensor_tensor(sbe[:, :], z, -1.0, z, ALU.mult, ALU.max).then_inc(sb_abs, 1)

            def sb_turn(i, par, more):
                n = i * 2 + par
                z = sbz[:, par, :]
                dve.wait_ge(sb_ln, n + 1)
                dve.wait_ge(sb_c, n + 1)
                dve.scalar_tensor_tensor(sbn[:, :], z, 0.0, sbe[:, :], ALU.max, ALU.add).then_inc(sb_n, 1)
                if more:
                    sb_abs_of(n + 1, 1 - par)
                dve.wait_ge(sb_c, n + 2)
                two = lambda x: x.rearrange("p (a n) -> p a n", a=2)
                dve.tensor_tensor(two(z[:, 0:8 * P]), two(z[:, 0:8 * P]), ps[:, 4:6, :], ALU.subtract)
                dve.tensor_tensor(z[:, 8 * P:SBX], z[:, 8 * P:SBX], ps[:, 6, 0:2 * P], ALU.subtract).then_inc(sb_lw, 1)
                dve.tensor_tensor(z[0:META, SBX:SBW], z[0:META, SBX:SBW], ps[0:META, 7, :], ALU.subtract).then_inc(sb_lw, 1)

            sb_abs_of(0, 0)
            with dve.Fori(0, HEADS // 2 - 1) as i:
                sb_turn(i, 0, True)
                sb_turn(i, 1, True)
            sb_turn(HEADS // 2 - 1, 0, True)
            sb_turn(HEADS // 2 - 1, 1, False)

            def with_ada(gm, r):
                for c in ada_units(gm, r):
                    ada_dve(dve, 0, c)

            dve.wait_ge(sb_oc, 2 + HEADS)
            for c in range(NT):
                split_tile(dve, VO[:, c, :, :], VOH[:, c, :, :], VOL[:, c, :, :]).then_inc(split_x, 1)
            for i, slabs in groups(dve, branch_dn):
                for t in slabs:
                    b = acc_in(dve, branch_dn, i, t)
                    if isinstance(i, int):
                        taken(dve, gate_dn, 0, t)
                    else:
                        taken(dve, gate_dn, 0, KD - 2)
                        taken(dve, gate_dn, 0, KD - 1)
                    n = ds(i * R + t, 1)
                    dve.tensor_tensor(MG[:, n, :], ps[:, 2 * b:2 * b + 1, :], MG[:, n, :], ALU.mult).then_inc(acc_free[b], 1)
            dve.wait_ge(silu_c, 1)
            for r in range(R):
                with_ada(gate_sb, r)
            for k in range(KD):
                split_tile(dve, QSK[:, k, 0:SEQ], OSH[:, k, :], OSL[:, k, 0:SEQ]).then_inc(split_x, 1)
            for t in range(KD):
                if t % 2 == 0:
                    with_ada(branch_sb, t // 2)
                b = acc_in(dve, branch_sb, 0, t)
                taken(dve, gate_sb, 0, t)
                dve.tensor_tensor(GT[:, t, :], ps[:, 2 * b, :], GT[:, t, :], ALU.mult).then_inc(acc_free[b], 1)
                dve.drain()
                dve.tensor_tensor(MG[:, t, :], MG[:, t, :], GT[:, t, :], ALU.add)
                dve.drain()
                split_tile(dve, MG[:, t, :], MGH[:, t, :], MGL[:, t, :]).then_inc(merged, 1)

            def add_residual(gm, gate=None, before=None):
                for t in range(KD):
                    if before:
                        before(t)
                    b = acc_in(dve, gm, 0, t)
                    x = H[:, t, META:T]
                    if gate is None:
                        dve.tensor_tensor(x, x, ps[:, 2 * b, :], ALU.add).then_inc(acc_free[b], 1)
                    else:
                        dve.scalar_tensor_tensor(x, ps[:, 2 * b, :], gate(t), x, ALU.mult, ALU.add).then_inc(acc_free[b], 1)

            add_residual(mix_out, before=lambda t: t % 2 or with_ada(mix_out, t // 2))
            norm_dve(dve, 1, lambda k: H[:, k, META:T], lambda k: col("norm_ffn", k), SEQ)

            def split_act(j):
                n = ds(j, 1)
                dve.drain()
                split_tile(dve, ACTF[:, n, :], AFH[:, n, :], AFL[:, n, :]).then_inc(f_split, 1)

            for i, slabs in groups(dve, ffn_in):
                for r in slabs:
                    for c in ada_units(ffn_in, r):
                        ada_dve(dve, i, c)
                    taken(dve, ffn_in, i, 2 * r)
                    b = acc_in(dve, ffn_in, i, 2 * r + 1)
                    dve.tensor_tensor(ACTF[:, ds(i * R + r, 1), :], SG[:, r % 2, :].unsqueeze(1), ps[:, 2 * b:2 * b + 1, :], ALU.mult)\
                        .then_inc(acc_free[b], 1)
                    split_act(i * R + r)

            add_residual(ffn_out, before=lambda t: with_ada(ffn_out, t))

            dve.wait_ge(ada_red, 4 + ADA)
            dve.tensor_tensor(mod[:, :, :].rearrange("p l n -> p (l n)"), ps[:, 4, 0:ADA], cols("ada_b", 0, ADA), ALU.add)
            dve.drain()
            for l in range(2):
                for n, name in enumerate(("norm1", "norm2")):
                    c = (n * 3 + 1) * KD
                    ins = dve.scalar_tensor_tensor(gsc[:, l, n, :], mod[:, l, c:c + KD], 1.0, cols(name, l * KD, KD), ALU.add, ALU.mult)
            ins.then_inc(mod_done, 1)
            dve.drain()

            shift_dve(dve, 2, 0, 0)
            dve.wait_ge(a_in, 16)

            def rope(n):
                x = QG[:, GQ_TILES[n][2], :]
                dve.wait_ge(a_rot, n + 1)
                dve.tensor_tensor(rtmp[:, :], ps[:, 7, :], ropes[:, 1, :], ALU.mult)
                dve.tensor_tensor(x, x, ropes[:, 0, :], ALU.mult)
                dve.drain()
                dve.tensor_tensor(x, x, rtmp[:, :], ALU.add).then_inc(a_done, 1)

            for n, (_, _, place) in enumerate(GQ_TILES):
                dve.wait_ge(h_rs, 1 + 2 * HEADS + n + 1)
                dve.scalar_tensor_tensor(QG[:, place, :], QG[:, place, :], col("gq" if place < KD else "gk"), NRS[:, 0:SEQ],
                                         ALU.mult, ALU.mult).then_inc(h_done, 1)
                dve.drain().then_inc(a_nrm, 1)
                if n:
                    rope(n - 1)
            rope(9)
            for t in range(2):
                dve.wait_ge(sv_t, KD + t + 1)
                dve.tensor_copy(VG[:, :, t * P:(t + 1) * P], ps[:, 4 + t, :].rearrange("p (n c) -> p n c", n=NT)).then_inc(sv_done, 1)

            def maxima(g, j):
                n = g * 4 + j
                for q in range(NT):
                    dve.wait_ge(a_s, n * NT + q + 1)
                    dve.tensor_reduce(asm[:, j % 2, 0, q:q + 1], ps[:, q, :], AX.X, ALU.max)
                    dve.drain()
                    dve.tensor_scalar(asm[:, j % 2, 1, q:q + 1], asm[:, j % 2, 0, q:q + 1], -float(HD) ** -0.5, None, ALU.mult)\
                        .then_inc(a_mx, 1)

            def gq_turn(g, more):
                for j in range(4):
                    n = g * 4 + j
                    for q in range(NT):
                        dve.wait_ge(a_e, n * NT + q + NT + 1)
                        dve.reciprocal(asm[:, j % 2, 3, q:q + 1], asm[:, j % 2, 2, q:q + 1])
                        dve.drain()
                        dve.tensor_scalar(PB[:, j % 2, q, :], PB[:, j % 2, q, :], asm[:, j % 2, 3, q:q + 1], None, ALU.mult)\
                            .then_inc(a_p, 1)
                    if j < 3:
                        maxima(g, j + 1)
                    elif more:
                        maxima(g + 1, 0)

            maxima(0, 0)
            with dve.Fori(0, KVH - 1) as g:
                gq_turn(g, True)
            gq_turn(KVH - 1, False)
            for k in range(KD):
                dve.wait_ge(a_oc, k + 3)
                dve.tensor_tensor(OGL[:, k, :], OG[:, k, :], OGH[:, k, :], ALU.subtract).then_inc(split_x, 1)
            add_residual(gq_out, lambda t: mod[:, 0, 2 * KD + t:2 * KD + t + 1])

            def dve_conv_ffn(l, u):
                shift_dve(dve, u, l, 1)
                dve.memset(GP[:, :, 0:1], 0.0)
                dve.memset(GP[:, :, SEQ + 1:SEQ + 2], 0.0)
                dve.drain()
                for i, slabs in groups(dve, fc_in[l]):
                    for r in slabs:
                        j = i * R + r
                        taken(dve, fc_in[l], i, 2 * r)
                        x, y = GP[:, r % 2, :], SG[:, r % 2, :]
                        dve.tensor_scalar(y, x[:, 0:SEQ], dcol(f"fc_w{l}", j), dcol(f"fc_b{l}", j), ALU.mult, ALU.add)
                        dve.drain()
                        dve.scalar_tensor_tensor(y, x[:, 1:SEQ + 1], dcol(f"fc_w{l}", j + KF), y, ALU.mult, ALU.add)
                        dve.drain()
                        dve.scalar_tensor_tensor(y, x[:, 2:SEQ + 2], dcol(f"fc_w{l}", j + 2 * KF), y, ALU.mult, ALU.add)\
                            .then_inc(fc_conv, 1)
                        b = acc_in(dve, fc_in[l], i, 2 * r + 1)
                        dve.wait_ge(fc_silu, i * R + (l * KF + r + 1))
                        dve.tensor_tensor(ACTF[:, ds(j, 1), :], y.unsqueeze(1), ps[:, 2 * b:2 * b + 1, :], ALU.mult)\
                            .then_inc(acc_free[b], 1)
                        split_act(j)
                add_residual(fc_out[l], lambda t: mod[:, l, 5 * KD + t:5 * KD + t + 1])

            dve_conv_ffn(0, 3)
            dve.memset(UP[:, :, 0:1], 0.0)
            dve.memset(UP[:, :, SEQ + 1:SEQ + 2], 0.0)
            dve.memset(later_t[:, :], 1.0)
            dve.drain()
            dve.memset(later_t[0:1, :], 0.0)
            shift_dve(dve, 4, 1, 0)
            two_pi_hi = 6.28125
            two_pi_lo = 2.0 * np.pi - two_pi_hi
            rounder = 1.5 * 2.0 ** 23

            def sin_arg(n):
                x, k = A1[:, n, :], A1[:, 2, :]
                dve.wait_ge(y_mlp, n + 1)
                dve.tensor_scalar(x, ps[0:FW, 7 - n, :], col(("b1", "b2")[n])[0:FW], col("freq")[0:FW], ALU.add, ALU.mult)
                dve.drain()
                dve.tensor_scalar(k, x, 1.0 / (2.0 * np.pi), rounder, ALU.mult, ALU.add)
                dve.drain()
                dve.tensor_scalar(k, k, rounder, None, ALU.subtract)
                dve.drain()
                dve.scalar_tensor_tensor(x, k, -two_pi_hi, x, ALU.mult, ALU.add)
                dve.drain()
                dve.scalar_tensor_tensor(x, k, -two_pi_lo, x, ALU.mult, ALU.add)
                dve.drain()
                dve.tensor_scalar(x, x, 3.1415925, -3.1415925, ALU.min, ALU.max).then_inc(y_arg, 1)

            sin_arg(0)
            for i, slabs in groups(dve, hy_in):
                for t in range(2 * R):
                    n = i * (2 * R) + t
                    taken(dve, hy_in, i, t)
                    x, y = UP[:, t % 2, :], U[:, ds(n, 1), :].rearrange("p a n -> p (a n)")
                    dve.tensor_scalar(y, x[:, 0:SEQ], dcol("hy_w", n), dcol("hy_b", n), ALU.mult, ALU.add)
                    dve.drain()
                    dve.scalar_tensor_tensor(y, x[:, 1:SEQ + 1], dcol("hy_w", n + 3 * KD), y, ALU.mult, ALU.add)
                    dve.drain()
                    dve.scalar_tensor_tensor(y, x[:, 2:SEQ + 2], dcol("hy_w", n + 6 * KD), y, ALU.mult, ALU.add).then_inc(y_conv, 1)
            sin_arg(1)

            def filters(u, tiles):
                for t in tiles:
                    b = t % 2 * 2
                    dve.drain()
                    if t == 0:
                        dve.wait_ge(y_w, u * 32 + 32)
                    dve.wait_ge(y_f, u * (NT + 1) + (t + 1))
                    if t:
                        dve.wait_ge(y_ab, u * NT + t)
                    dve.tensor_tensor(FB[:, 0, :], ps[:, b, :], DEC[:, t, :], ALU.mult)
                    if t == 0:
                        dve.scalar_tensor_tensor(FB[:, 1, :], ps[:, b + 1, :], later_t[:, 0:1], DEC[:, t, :], ALU.mult, ALU.mult)\
                            .then_inc(y_fb, 1)
                    else:
                        dve.tensor_tensor(FB[:, 1, :], ps[:, b + 1, :], DEC[:, t, :], ALU.mult).then_inc(y_fb, 1)
                    dve.drain()
                    dve.tensor_tensor(PM[:, 0, t, :], FB[:, 0, :], FB[:, 1, :], ALU.add)
                    dve.tensor_tensor(PM[:, 1, t, :], FB[:, 0, :], FB[:, 1, :], ALU.subtract).then_inc(y_pm, 1)

            def filter_norm(u, dh):
                dve.wait_ge(y_f, u * (NT + 1) + (NT + 1))
                dve.reciprocal(rn[:, dh, :], ps[:, 0, 0:NT]).then_inc(y_rn, 1)

            def filters_start():
                filters(0, range(NT))
                filter_norm(0, 0)

            def hyena_pair(o, more):
                for dh in range(2):
                    u = o * 2 + dh
                    for f in range(2):
                        dve.drain()
                        dve.wait_ge(y_zc, u * 2 + f + 1)
                        dve.tensor_tensor(XZ[:, 0, :], ZS[:, 0, :], ps[:, 5, :], ALU.add)
                        dve.tensor_tensor(XZ[:, 1, :], ZS[:, 1, :], ps[:, 7, :], ALU.add)
                        dve.tensor_tensor(XZ[:, 2, :], ZS[:, 0, :], ps[:, 5, :], ALU.subtract)
                        dve.tensor_tensor(XZ[:, 3, :], ps[:, 7, :], ZS[:, 1, :], ALU.subtract).then_inc(y_x, 1)
                        dve.drain()
                        dve.wait_ge(y_kp, u * 2 + f + 2)
                        dve.wait_ge(y_y, u * 2 + f + 1)
                        zc, zs, zcm, zsm = (XZ[:, n, :] for n in range(4))
                        kc, ks, kcm, ksm = (KP[:, f, n, :] for n in range(4))
                        for part, (a, b, am, bm), op in ((0, (kc, ks, kcm, ksm), ALU.subtract), (1, (ks, kc, ksm, kcm), ALU.add)):
                            dve.tensor_tensor(YB[:, part, :], zc, a, ALU.mult)
                            dve.tensor_tensor(YT[:, 0, :], zs, b, ALU.mult)
                            dve.tensor_tensor(YB[:, 2 + part, :], zcm, am, ALU.mult)
                            dve.tensor_tensor(YT[:, 1, :], zsm, bm, ALU.mult)
                            dve.drain()
                            dve.tensor_tensor(YB[:, part, :], YB[:, part, :], YT[:, 0, :], op)
                            dve.tensor_tensor(YB[:, 2 + part, :], YB[:, 2 + part, :], YT[:, 1, :], op).then_inc(y_cb, 1)
                            dve.drain()
                    following = dh == 0 or more
                    if following:
                        filters(u + 1, range(2))
                    pairs = lambda x: x.rearrange("p (t e) -> p t e", e=2)
                    for c in range(NT):
                        if c == 2 and following:
                            filters(u + 1, range(2, NT))
                        n = dh * NT + c
                        z, y = U[:, n, :], ytmp[:, c % 2, :]
                        dve.tensor_scalar(y, z, dcol("skip", o * KD + n), None, ALU.mult)
                        dve.drain()
                        dve.wait_ge(y_inv, u * NT + c + 2)
                        dve.scalar_tensor_tensor(pairs(y), ps[:, 6 + c % 2, :].rearrange("p (e t) -> p t e", e=2), rn[:, dh, c:c + 1],
                                                 pairs(y), ALU.mult, ALU.add)
                        dve.drain()
                        dve.tensor_tensor(z.unsqueeze(1), ytmp[:, c % 2:c % 2 + 1, :], U[:, ds(o * KD + (KD + n), 1), :], ALU.mult)\
                            .then_inc(y_z, 1)
                        if not more:
                            dve.drain()
                            split_tile(dve, z, ZH[:, n, :], ZL[:, n, :]).then_inc(split_x, 1)
                    if following:
                        filter_norm(u + 1, 1 - dh)

            hyena_units(dve, filters_start, hyena_pair)
            add_residual(hy_out, lambda t: mod[:, 1, 2 * KD + t:2 * KD + t + 1])
            dve_conv_ffn(1, 5)
            dve.wait_ge(n_rs, 7)
            for k in range(KD):
                dve.scalar_tensor_tensor(HN[:, k, 0:SEQ], H[:, k, META:T], col("final", k), NRS[:, 0:SEQ], ALU.mult, ALU.mult)\
                    .then_inc(n_out, 1)
            for n in range(NT):
                for h in range(2):
                    dve.wait_ge(f_t, 2 * n + h + 1)
                    dve.tensor_copy(OUT[:, n, h * 4 * P:(h + 1) * 4 * P], ps[:, 4 + h, :]).then_inc(f_out, 1)


_TABLES = ("t_square", "t_delta", "t_rope", "t_fwd", "t_inv", "t_pos", "t_decay")
_SKIP = ("s5_",)


def kernel(**inputs):
    import concourse.bacc as bacc
    from concourse.bass_utils import run_bass_kernel_spmd

    nc = bacc.Bacc("TRN2", target_bir_lowering=False, num_devices=1)
    arrays, args = {}, {}
    given = {n: np.ascontiguousarray(a) for n, a in inputs.items() if not n.startswith(_SKIP)}
    for name, a in {**given, **tables()}.items():
        arrays[f"in_{name}"] = a
        args[name] = nc.dram_tensor(f"in_{name}", a.shape, F32, kind="ExternalInput").ap()
    out = nc.dram_tensor("out", (1, SEQ, D), F32, kind="ExternalOutput").ap()
    build(nc, args, out[0])
    r = run_bass_kernel_spmd(nc, [arrays], core_ids=[0])
    return r.results[0]["out"]
```
